# Optimizing a Trainium2 kernel written in Bass

```python
import math
import jax, jax.numpy as jnp
from jax import lax
import numpy as np

D_MODEL = 1024
BATCH = 1
SEQ = 512
DEPTH = 2

GRID_W = 64
CTX_LEN = 256
EPS = 1e-6
ROPE_THETA = 10000.0
F32 = jnp.float32

A_HEADS = 4
A_QK_DIM = 64
A_V_DIM = 2 * A_QK_DIM
A_WIDTH = A_HEADS * A_V_DIM
A_PROJ = 2 * (A_HEADS * 2 * A_QK_DIM) + A_WIDTH
Q_BLOCK = 128

B_HEADS = 8
B_HEAD = 64
B_WIDTH = B_HEADS * B_HEAD
B_DECAY_LORA = 64
B_AAA_LORA = 64
B_GATE_LORA = 128
B_GN_EPS = 64e-5
B_PROJ = 3 * B_WIDTH + B_DECAY_LORA + B_AAA_LORA + B_GATE_LORA

C_HEADS = 8
C_HEAD = 64
C_WIDTH = C_HEADS * C_HEAD
C_GROUPS = 2
C_REP = C_HEADS // C_GROUPS
C_STATE = 128
C_CONV = 5
C_CHUNK = 128
C_CONV_DIM = C_WIDTH + 2 * C_GROUPS * C_STATE
C_PROJ = C_WIDTH + C_CONV_DIM + 2 * C_HEADS

D_HEADS = 4
D_KEY = 64
D_VAL = 128
D_WIDTH = D_HEADS * D_VAL
D_GATE_LORA = 16
D_GATE_TAU = 16.0
D_CHUNK = 64
D_PROJ = 2 * D_HEADS * D_KEY + 2 * D_WIDTH + D_GATE_LORA

MLP_HIDDEN = 4 * D_MODEL
EVEN_IN = A_PROJ + B_PROJ
ODD_IN = C_PROJ + D_PROJ
MIX_WIDTH = A_WIDTH + B_WIDTH


def rmsnorm(x, g, eps=EPS):
    xf = x.astype(F32)
    y = xf * lax.rsqrt(jnp.mean(xf * xf, axis=-1, keepdims=True) + eps)
    return (y * g.astype(F32)).astype(x.dtype)

def _split(t, sizes):
    idx = [int(s) for s in np.cumsum(sizes)[:-1]]
    return jnp.split(t, idx, axis=-1)

def _flip_seq(*ts):
    return tuple(jnp.flip(t, axis=1) for t in ts)

def axial_rope_tables(n, dim):
    rows = n // GRID_W
    t = jnp.arange(rows * GRID_W)
    row = (t // GRID_W).astype(F32)
    col = (t % GRID_W).astype(F32)
    nf = dim // 4
    inv = ROPE_THETA ** (-jnp.arange(nf, dtype=F32) / nf)
    ar = row[:, None] * inv[None, :]
    ac = col[:, None] * inv[None, :]
    return jnp.cos(ar), jnp.sin(ar), jnp.cos(ac), jnp.sin(ac)

def _rot_half(x, cos, sin):
    x1, x2 = jnp.split(x, 2, axis=-1)
    return jnp.concatenate([x1 * cos - x2 * sin, x2 * cos + x1 * sin], axis=-1)

def apply_axial_rope(x, tabs):
    cr, sr, cc, sc = tabs
    xr, xc = jnp.split(x.astype(F32), 2, axis=-1)
    return jnp.concatenate([_rot_half(xr, cr, sr), _rot_half(xc, cc, sc)], axis=-1)

def _diff_softmax_mix(q, k, v, lam):
    s = jnp.einsum('bhmqd,bhmkd->bhmqk', q.astype(F32), k.astype(F32)) * (A_QK_DIM ** -0.5)
    p = jax.nn.softmax(s, axis=-1)
    w = p[:, :, 0] - lam * p[:, :, 1]
    return jnp.einsum('bhqk,bhkd->bhqd', w, v.astype(F32))

def diff_attention(t_lat, t_ctx, lam_q1, lam_k1, lam_q2, lam_k2, subln, layer_idx, need_ctx):
    bsz, n = t_lat.shape[0], t_lat.shape[1]
    lam_init = 0.8 - 0.6 * math.exp(-0.3 * layer_idx)
    lam = (jnp.exp(jnp.sum(lam_q1.astype(F32) * lam_k1.astype(F32)))
           - jnp.exp(jnp.sum(lam_q2.astype(F32) * lam_k2.astype(F32))) + lam_init)

    def heads(t):
        m = t.shape[1]
        q, k, v = _split(t, [A_HEADS * 2 * A_QK_DIM, A_HEADS * 2 * A_QK_DIM, A_WIDTH])
        q = q.reshape(bsz, m, A_HEADS, 2, A_QK_DIM).transpose(0, 2, 3, 1, 4)
        k = k.reshape(bsz, m, A_HEADS, 2, A_QK_DIM).transpose(0, 2, 3, 1, 4)
        v = v.reshape(bsz, m, A_HEADS, A_V_DIM).transpose(0, 2, 1, 3)
        return q, k, v

    q_l, k_l, v_l = heads(t_lat)
    q_c, k_c, v_c = heads(t_ctx)
    tabs = axial_rope_tables(n, A_QK_DIM)
    q_l = apply_axial_rope(q_l, tabs)
    k_l = apply_axial_rope(k_l, tabs)
    k_all = jnp.concatenate([k_c.astype(F32), k_l], axis=3)
    v_all = jnp.concatenate([v_c, v_l], axis=2)
    nb = n // Q_BLOCK
    qb = jnp.moveaxis(q_l.reshape(bsz, A_HEADS, 2, nb, Q_BLOCK, A_QK_DIM), 3, 0)
    ob = lax.map(lambda qq: _diff_softmax_mix(qq, k_all, v_all, lam), qb)
    o_l = jnp.moveaxis(ob, 0, 2).reshape(bsz, A_HEADS, n, A_V_DIM)

    def post(o):
        o = rmsnorm(o, subln, eps=1e-5) * (1.0 - lam_init)
        return o.transpose(0, 2, 1, 3).reshape(bsz, o.shape[2], A_WIDTH)

    out_l = post(o_l)
    out_c = post(_diff_softmax_mix(q_c, k_c, v_c, lam)) if need_ctx else None
    return out_l, out_c

def _token_shift_mix(f, mu):
    prev = jnp.pad(f[:, :-1], ((0, 0), (1, 0), (0, 0)))
    nxt = jnp.pad(f[:, 1:], ((0, 0), (0, 1), (0, 0)))
    return f + (0.5 * (prev + nxt) - f) * mu

def _rwkv7_scan(S0, r, w, k, v, kk, a):
    def step(S, inp):
        r_t, w_t, k_t, v_t, kk_t, a_t = inp
        sa = jnp.einsum('bhvk,bhk->bhv', S, kk_t)
        S = (S * w_t[:, :, None, :] - sa[..., None] * (kk_t * a_t)[:, :, None, :]
             + v_t[..., None] * k_t[:, :, None, :])
        return S, jnp.einsum('bhvk,bhk->bhv', S, r_t)
    xs = tuple(jnp.swapaxes(t, 0, 1) for t in (r, w, k, v, kk, a))
    S, ys = lax.scan(step, S0, xs)
    return jnp.swapaxes(ys, 0, 1), S

def rwkv7_mix(t_lat, t_ctx, mu, w0_f, w2_f, w0_b, w2_b, a0, a2, g2, k_k, k_a, r_k, lnx_w, lnx_b, need_ctx):
    def prep(t):
        bsz, n = t.shape[0], t.shape[1]
        f = _token_shift_mix(t, mu).astype(F32)
        r, k, v, wd, ad, gd = _split(f, [B_WIDTH, B_WIDTH, B_WIDTH, B_DECAY_LORA, B_AAA_LORA, B_GATE_LORA])
        hd = lambda u: u.reshape(bsz, n, B_HEADS, B_HEAD)
        a = jax.nn.sigmoid(a0 + ad @ a2)
        tw = jnp.tanh(wd)
        def decay(w0, w2):
            wl = -jax.nn.softplus(-(w0 + tw @ w2)) - 0.5
            return hd(jnp.exp(-jnp.exp(wl)))
        kk = hd(k * k_k)
        kk = kk / jnp.maximum(jnp.sqrt(jnp.sum(kk * kk, axis=-1, keepdims=True)), 1e-12)
        k = k * (1.0 + (a - 1.0) * k_a)
        g = jax.nn.sigmoid(gd) @ g2
        return (hd(r), hd(k), hd(v), kk, hd(a), decay(w0_f, w2_f), decay(w0_b, w2_b), g)

    r_c, k_c, v_c, kk_c, a_c, wf_c, wb_c, g_c = prep(t_ctx)
    r_l, k_l, v_l, kk_l, a_l, wf_l, wb_l, g_l = prep(t_lat)
    S0 = jnp.zeros((t_lat.shape[0], B_HEADS, B_HEAD, B_HEAD), F32)
    yf_c, Sf_c = _rwkv7_scan(S0, r_c, wf_c, k_c, v_c, kk_c, a_c)
    yb_c, Sb_c = _rwkv7_scan(S0, *_flip_seq(r_c, wb_c, k_c, v_c, kk_c, a_c))
    yf_l, _ = _rwkv7_scan(Sf_c, r_l, wf_l, k_l, v_l, kk_l, a_l)
    yb_l, _ = _rwkv7_scan(Sb_c, *_flip_seq(r_l, wb_l, k_l, v_l, kk_l, a_l))

    def post(r, k, v, g, yf, yb):
        bsz, n = r.shape[0], r.shape[1]
        y = yf + jnp.flip(yb, axis=1)
        mean = jnp.mean(y, axis=-1, keepdims=True)
        var = jnp.mean(jnp.square(y - mean), axis=-1, keepdims=True)
        y = ((y - mean) * lax.rsqrt(var + B_GN_EPS)).reshape(bsz, n, B_WIDTH) * lnx_w + lnx_b
        bonus = jnp.sum(r * k * r_k.reshape(B_HEADS, B_HEAD), axis=-1, keepdims=True) * v
        return (y + bonus.reshape(bsz, n, B_WIDTH)) * g

    out_l = post(r_l, k_l, v_l, g_l, yf_l, yb_l)
    out_c = post(r_c, k_c, v_c, g_c, yf_c, yb_c) if need_ctx else None
    return out_l, out_c

def _dwconv_centred(t, w, b):
    y = lax.conv_general_dilated(t, w[:, None, :].astype(t.dtype), window_strides=(1,),
                                 padding=[(C_CONV // 2, C_CONV // 2)],
                                 dimension_numbers=('NWC', 'WIO', 'NWC'),
                                 feature_group_count=t.shape[-1])
    return y + b

def _ssd_chunk_scan(h0, x, dt, la, bm, cm):
    bsz, n = x.shape[0], x.shape[1]
    nc = n // C_CHUNK
    chunks = lambda t: jnp.swapaxes(t.reshape((bsz, nc, C_CHUNK) + t.shape[2:]), 0, 1)
    idx = jnp.arange(C_CHUNK)
    lower = (idx[:, None] >= idx[None, :])[None, :, :, None, None]

    def step(h, inp):
        xc, dtc, lac, bc, cc = inp
        cum = jnp.cumsum(lac, axis=1)
        lmat = jnp.exp(jnp.where(lower, cum[:, :, None] - cum[:, None, :], -jnp.inf))
        cb = jnp.einsum('bign,bjgn->bijg', cc, bc)
        xdt = xc * dtc[..., None]
        y = jnp.einsum('bijgr,bjgrp->bigrp', cb[..., None] * lmat, xdt)
        y = y + jnp.einsum('bign,bgrpn->bigrp', cc, h) * jnp.exp(cum)[..., None]
        w_end = jnp.exp(cum[:, -1:] - cum)
        h = h * jnp.exp(cum[:, -1])[..., None, None] + jnp.einsum('bjgn,bjgrp->bgrpn', bc, xdt * w_end[..., None])
        return h, y

    h, ys = lax.scan(step, h0, tuple(chunks(t) for t in (x, dt, la, bm, cm)))
    return jnp.swapaxes(ys, 0, 1).reshape(x.shape), h

def ssd_mix(t_lat, t_ctx, conv_w, conv_b, dt_bias_f, a_log_f, dt_bias_b, a_log_b, d_skip, norm_g, need_ctx):
    def prep(t):
        bsz, n = t.shape[0], t.shape[1]
        z, xbc, dt_f, dt_b = _split(t, [C_WIDTH, C_CONV_DIM, C_HEADS, C_HEADS])
        xbc = jax.nn.silu(_dwconv_centred(xbc, conv_w, conv_b).astype(F32))
        xs, bm, cm = _split(xbc, [C_WIDTH, C_GROUPS * C_STATE, C_GROUPS * C_STATE])
        xs = xs.reshape(bsz, n, C_GROUPS, C_REP, C_HEAD)
        bm = bm.reshape(bsz, n, C_GROUPS, C_STATE)
        cm = cm.reshape(bsz, n, C_GROUPS, C_STATE)
        def direction(dt_raw, dt_bias, a_log):
            dt = jax.nn.softplus(dt_raw.astype(F32) + dt_bias).reshape(bsz, n, C_GROUPS, C_REP)
            return dt, dt * (-jnp.exp(a_log.astype(F32))).reshape(C_GROUPS, C_REP)
        return z, xs, bm, cm, direction(dt_f, dt_bias_f, a_log_f), direction(dt_b, dt_bias_b, a_log_b)

    z_c, x_c, b_c, c_c, (dtf_c, laf_c), (dtb_c, lab_c) = prep(t_ctx)
    z_l, x_l, b_l, c_l, (dtf_l, laf_l), (dtb_l, lab_l) = prep(t_lat)
    h0 = jnp.zeros((t_lat.shape[0], C_GROUPS, C_REP, C_HEAD, C_STATE), F32)
    yf_c, hf_c = _ssd_chunk_scan(h0, x_c, dtf_c, laf_c, b_c, c_c)
    yb_c, hb_c = _ssd_chunk_scan(h0, *_flip_seq(x_c, dtb_c, lab_c, b_c, c_c))
    yf_l, _ = _ssd_chunk_scan(hf_c, x_l, dtf_l, laf_l, b_l, c_l)
    yb_l, _ = _ssd_chunk_scan(hb_c, *_flip_seq(x_l, dtb_l, lab_l, b_l, c_l))

    def post(z, xs, yf, yb):
        bsz, n = xs.shape[0], xs.shape[1]
        y = yf + jnp.flip(yb, axis=1) + xs * d_skip.astype(F32).reshape(C_GROUPS, C_REP, 1)
        y = y.reshape(bsz, n, C_WIDTH) * jax.nn.silu(z.astype(F32))
        y = rmsnorm(y.reshape(bsz, n, C_GROUPS, C_WIDTH // C_GROUPS), norm_g.reshape(C_GROUPS, C_WIDTH // C_GROUPS))
        return y.reshape(bsz, n, C_WIDTH)

    out_l = post(z_l, x_l, yf_l, yb_l)
    out_c = post(z_c, x_c, yf_c, yb_c) if need_ctx else None
    return out_l, out_c

def _gla_chunk_scan(S0, q, k, v, lg):
    bsz, n = q.shape[0], q.shape[1]
    nc = n // D_CHUNK
    chunks = lambda t: jnp.swapaxes(t.reshape((bsz, nc, D_CHUNK) + t.shape[2:]), 0, 1)
    idx = jnp.arange(D_CHUNK)
    lower = (idx[:, None] >= idx[None, :])[None, :, :, None, None]

    def step(S, inp):
        qc, kc, vc, gc = inp
        cum = jnp.cumsum(gc, axis=1)
        dec = jnp.exp(jnp.where(lower, cum[:, :, None] - cum[:, None, :], -jnp.inf))
        att = jnp.einsum('bihk,bjhk,bijhk->bhij', qc, kc, dec)
        y = jnp.einsum('bhij,bjhv->bihv', att, vc) + jnp.einsum('bihk,bhkv->bihv', qc * jnp.exp(cum), S)
        S = S * jnp.exp(cum[:, -1])[..., None] + jnp.einsum('bjhk,bjhv->bhkv', kc * jnp.exp(cum[:, -1:] - cum), vc)
        return S, y

    S, ys = lax.scan(step, S0, tuple(chunks(t) for t in (q, k, v, lg)))
    return jnp.swapaxes(ys, 0, 1).reshape(v.shape), S

def gla_mix(t_lat, t_ctx, gk_up_f, gk_b_f, gk_up_b, gk_b_b, norm_g, need_ctx):
    def prep(t):
        bsz, n = t.shape[0], t.shape[1]
        q, k, v, g, gd = _split(t.astype(F32), [D_HEADS * D_KEY, D_HEADS * D_KEY, D_WIDTH, D_WIDTH, D_GATE_LORA])
        hk = lambda u: u.reshape(bsz, n, D_HEADS, D_KEY)
        def log_gate(up, b):
            return hk(jax.nn.log_sigmoid(gd @ up + b) / D_GATE_TAU)
        return (hk(q) * (D_KEY ** -0.5), hk(k), v.reshape(bsz, n, D_HEADS, D_VAL), g,
                log_gate(gk_up_f, gk_b_f), log_gate(gk_up_b, gk_b_b))

    q_c, k_c, v_c, g_c, gf_c, gb_c = prep(t_ctx)
    q_l, k_l, v_l, g_l, gf_l, gb_l = prep(t_lat)
    S0 = jnp.zeros((t_lat.shape[0], D_HEADS, D_KEY, D_VAL), F32)
    yf_c, Sf_c = _gla_chunk_scan(S0, q_c, k_c, v_c, gf_c)
    yb_c, Sb_c = _gla_chunk_scan(S0, *_flip_seq(q_c, k_c, v_c, gb_c))
    yf_l, _ = _gla_chunk_scan(Sf_c, q_l, k_l, v_l, gf_l)
    yb_l, _ = _gla_chunk_scan(Sb_c, *_flip_seq(q_l, k_l, v_l, gb_l))

    def post(g, yf, yb):
        bsz, n = g.shape[0], g.shape[1]
        y = rmsnorm(yf + jnp.flip(yb, axis=1), norm_g)
        return y.reshape(bsz, n, D_WIDTH) * jax.nn.silu(g)

    out_l = post(g_l, yf_l, yb_l)
    out_c = post(g_c, yf_c, yb_c) if need_ctx else None
    return out_l, out_c

def even_mixer(p_lat, p_ctx, lam_q1, lam_k1, lam_q2, lam_k2, subln, mu, w0_f, w2_f, w0_b, w2_b,
               a0, a2, g2, k_k, k_a, r_k, lnx_w, lnx_b, layer_idx, need_ctx):
    oa_l, oa_c = diff_attention(p_lat[..., :A_PROJ], p_ctx[..., :A_PROJ],
                                lam_q1, lam_k1, lam_q2, lam_k2, subln, layer_idx, need_ctx)
    ob_l, ob_c = rwkv7_mix(p_lat[..., A_PROJ:], p_ctx[..., A_PROJ:], mu, w0_f, w2_f, w0_b, w2_b,
                           a0, a2, g2, k_k, k_a, r_k, lnx_w, lnx_b, need_ctx)
    o_l = jnp.concatenate([oa_l, ob_l], axis=-1)
    o_c = jnp.concatenate([oa_c, ob_c], axis=-1) if need_ctx else None
    return o_l, o_c

def odd_mixer(p_lat, p_ctx, conv_w, conv_b, dt_bias_f, a_log_f, dt_bias_b, a_log_b, d_skip, ssm_norm,
              gk_up_f, gk_b_f, gk_up_b, gk_b_b, gla_norm, need_ctx):
    oc_l, oc_c = ssd_mix(p_lat[..., :C_PROJ], p_ctx[..., :C_PROJ], conv_w, conv_b, dt_bias_f, a_log_f,
                         dt_bias_b, a_log_b, d_skip, ssm_norm, need_ctx)
    od_l, od_c = gla_mix(p_lat[..., C_PROJ:], p_ctx[..., C_PROJ:], gk_up_f, gk_b_f, gk_up_b, gk_b_b,
                         gla_norm, need_ctx)
    o_l = jnp.concatenate([oc_l, od_l], axis=-1)
    o_c = jnp.concatenate([oc_c, od_c], axis=-1) if need_ctx else None
    return o_l, o_c

def _ada(x, g, shift, scale):
    return rmsnorm(x, g) * (1.0 + scale) + shift

def _sq_relu_mlp(h, w1, w2):
    return jnp.square(jax.nn.relu(h @ w1)) @ w2

def first_inputs(seed: int = 0) -> dict:
    key = jax.random.key(seed)
    keys = iter(jax.random.split(key, 64))
    D = D_MODEL
    def nrm(shape, scale):
        return jax.random.normal(next(keys), shape, F32) * scale
    def gain(n):
        return 1.0 + 0.05 * jax.random.normal(next(keys), (n,), F32)
    def unif(shape, lo, hi):
        return jax.random.uniform(next(keys), shape, F32, lo, hi)
    def dt_bias(n):
        dt = jnp.exp(unif((n,), math.log(1e-3), math.log(1e-1)))
        return dt + jnp.log(-jnp.expm1(-dt))
    inp = {}
    inp['x'] = nrm((BATCH, SEQ, D), 1.0)
    inp['c'] = nrm((BATCH, D), 1.0)
    inp['ctx'] = nrm((BATCH, CTX_LEN, D), 1.0)
    inp['c_ctx'] = nrm((D,), 1.0)
    inp['l0_mod_w'] = nrm((D, 6 * D), 0.5 * D ** -0.5)
    inp['l0_mod_b'] = nrm((6 * D,), 0.02)
    inp['l0_norm1'] = gain(D)
    inp['l0_norm2'] = gain(D)
    inp['l0_w_in'] = nrm((D, EVEN_IN), D ** -0.5)
    inp['l0_w_out'] = nrm((MIX_WIDTH, D), MIX_WIDTH ** -0.5)
    inp['l0_mlp_w1'] = nrm((D, MLP_HIDDEN), D ** -0.5)
    inp['l0_mlp_w2'] = nrm((MLP_HIDDEN, D), MLP_HIDDEN ** -0.5)
    inp['l0_lam_q1'] = nrm((A_QK_DIM,), 0.1)
    inp['l0_lam_k1'] = nrm((A_QK_DIM,), 0.1)
    inp['l0_lam_q2'] = nrm((A_QK_DIM,), 0.1)
    inp['l0_lam_k2'] = nrm((A_QK_DIM,), 0.1)
    inp['l0_subln'] = gain(A_V_DIM)
    inp['l0_mu'] = unif((B_PROJ,), 0.0, 1.0)
    inp['l0_w0_f'] = unif((B_WIDTH,), -6.0, -1.0)
    inp['l0_w2_f'] = nrm((B_DECAY_LORA, B_WIDTH), 0.1 * B_DECAY_LORA ** -0.5)
    inp['l0_w0_b'] = unif((B_WIDTH,), -6.0, -1.0)
    inp['l0_w2_b'] = nrm((B_DECAY_LORA, B_WIDTH), 0.1 * B_DECAY_LORA ** -0.5)
    inp['l0_a0'] = nrm((B_WIDTH,), 0.1)
    inp['l0_a2'] = nrm((B_AAA_LORA, B_WIDTH), B_AAA_LORA ** -0.5)
    inp['l0_g2'] = nrm((B_GATE_LORA, B_WIDTH), B_GATE_LORA ** -0.5)
    inp['l0_k_k'] = 0.85 + nrm((B_WIDTH,), 0.05)
    inp['l0_k_a'] = gain(B_WIDTH)
    inp['l0_r_k'] = nrm((B_WIDTH,), 0.1)
    inp['l0_lnx_w'] = gain(B_WIDTH)
    inp['l0_lnx_b'] = nrm((B_WIDTH,), 0.02)
    inp['l1_mod_w'] = nrm((D, 6 * D), 0.5 * D ** -0.5)
    inp['l1_mod_b'] = nrm((6 * D,), 0.02)
    inp['l1_norm1'] = gain(D)
    inp['l1_norm2'] = gain(D)
    inp['l1_w_in'] = nrm((D, ODD_IN), D ** -0.5)
    inp['l1_w_out'] = nrm((MIX_WIDTH, D), MIX_WIDTH ** -0.5)
    inp['l1_mlp_w1'] = nrm((D, MLP_HIDDEN), D ** -0.5)
    inp['l1_mlp_w2'] = nrm((MLP_HIDDEN, D), MLP_HIDDEN ** -0.5)
    inp['l1_conv_w'] = nrm((C_CONV, C_CONV_DIM), C_CONV ** -0.5)
    inp['l1_conv_b'] = nrm((C_CONV_DIM,), 0.02)
    inp['l1_dt_bias_f'] = dt_bias(C_HEADS)
    inp['l1_a_log_f'] = jnp.log(unif((C_HEADS,), 1.0, 16.0))
    inp['l1_dt_bias_b'] = dt_bias(C_HEADS)
    inp['l1_a_log_b'] = jnp.log(unif((C_HEADS,), 1.0, 16.0))
    inp['l1_d_skip'] = gain(C_HEADS)
    inp['l1_ssm_norm'] = gain(C_WIDTH)
    inp['l1_gk_up_f'] = nrm((D_GATE_LORA, D_HEADS * D_KEY), D_GATE_LORA ** -0.5)
    inp['l1_gk_b_f'] = nrm((D_HEADS * D_KEY,), 0.1)
    inp['l1_gk_up_b'] = nrm((D_GATE_LORA, D_HEADS * D_KEY), D_GATE_LORA ** -0.5)
    inp['l1_gk_b_b'] = nrm((D_HEADS * D_KEY,), 0.1)
    inp['l1_gla_norm'] = gain(D_VAL)
    inp['final_norm'] = gain(D)
    return inp

def first_block(x, c, ctx, c_ctx,
              l0_mod_w, l0_mod_b, l0_norm1, l0_norm2, l0_w_in, l0_w_out, l0_mlp_w1, l0_mlp_w2,
              l0_lam_q1, l0_lam_k1, l0_lam_q2, l0_lam_k2, l0_subln,
              l0_mu, l0_w0_f, l0_w2_f, l0_w0_b, l0_w2_b, l0_a0, l0_a2, l0_g2, l0_k_k, l0_k_a, l0_r_k,
              l0_lnx_w, l0_lnx_b,
              l1_mod_w, l1_mod_b, l1_norm1, l1_norm2, l1_w_in, l1_w_out, l1_mlp_w1, l1_mlp_w2,
              l1_conv_w, l1_conv_b, l1_dt_bias_f, l1_a_log_f, l1_dt_bias_b, l1_a_log_b, l1_d_skip, l1_ssm_norm,
              l1_gk_up_f, l1_gk_b_f, l1_gk_up_b, l1_gk_b_b, l1_gla_norm,
              final_norm):
    shared = [
        (l0_mod_w, l0_mod_b, l0_norm1, l0_norm2, l0_w_in, l0_w_out, l0_mlp_w1, l0_mlp_w2),
        (l1_mod_w, l1_mod_b, l1_norm1, l1_norm2, l1_w_in, l1_w_out, l1_mlp_w1, l1_mlp_w2),
    ]
    for i in range(DEPTH):
        mod_w, mod_b, norm1, norm2, w_in, w_out, mlp_w1, mlp_w2 = shared[i]
        need_ctx = i < DEPTH - 1
        m_l = (jax.nn.silu(c) @ mod_w + mod_b)[:, None, :]
        m_c = jax.nn.silu(c_ctx) @ mod_w + mod_b
        sh1_l, sc1_l, g1_l, sh2_l, sc2_l, g2_l = jnp.split(m_l, 6, axis=-1)
        sh1_c, sc1_c, g1_c, sh2_c, sc2_c, g2_c = jnp.split(m_c, 6, axis=-1)
        p_lat = _ada(x, norm1, sh1_l, sc1_l) @ w_in
        p_ctx = _ada(ctx, norm1, sh1_c, sc1_c) @ w_in
        if i % 2 == 0:
            o_l, o_c = even_mixer(p_lat, p_ctx, l0_lam_q1, l0_lam_k1, l0_lam_q2, l0_lam_k2, l0_subln,
                                  l0_mu, l0_w0_f, l0_w2_f, l0_w0_b, l0_w2_b, l0_a0, l0_a2, l0_g2,
                                  l0_k_k, l0_k_a, l0_r_k, l0_lnx_w, l0_lnx_b, i, need_ctx)
        else:
            o_l, o_c = odd_mixer(p_lat, p_ctx, l1_conv_w, l1_conv_b, l1_dt_bias_f, l1_a_log_f,
                                 l1_dt_bias_b, l1_a_log_b, l1_d_skip, l1_ssm_norm,
                                 l1_gk_up_f, l1_gk_b_f, l1_gk_up_b, l1_gk_b_b, l1_gla_norm, need_ctx)
        x = x + g1_l * (o_l.astype(x.dtype) @ w_out)
        x = x + g2_l * _sq_relu_mlp(_ada(x, norm2, sh2_l, sc2_l), mlp_w1, mlp_w2)
        if need_ctx:
            ctx = ctx + g1_c * (o_c.astype(ctx.dtype) @ w_out)
            ctx = ctx + g2_c * _sq_relu_mlp(_ada(ctx, norm2, sh2_c, sc2_c), mlp_w1, mlp_w2)
    return rmsnorm(x, final_norm)


HEAD_DIM = 64
DSW_GROUPS = ((128, 1), (512, 4), (2048, 16))
DSW_HEADS_PER_GROUP = 4
DSW_HEADS = DSW_HEADS_PER_GROUP * len(DSW_GROUPS)
SB_HEADS = D_MODEL // (4 * HEAD_DIM)
W_A = DSW_HEADS * HEAD_DIM
W_B = SB_HEADS * HEAD_DIM
OUT_A = DSW_HEADS_PER_GROUP * HEAD_DIM
OUT_B = W_B
N_IN = 3 * W_A + 3 * W_B + 2 * D_MODEL
BLOCK = 128
D_FF = 2816
CONV_WIDTH = 3
RMS_EPS = 1e-6


def rmsnorm_2(x, g):
    xf = x.astype(jnp.float32)
    y = xf * lax.rsqrt(jnp.mean(xf * xf, axis=-1, keepdims=True) + RMS_EPS)
    return (y * g.astype(jnp.float32)).astype(x.dtype)

def alibi_slopes(n):
    return jnp.asarray(2.0 ** (-8.0 * np.arange(1, n + 1) / n), dtype=jnp.float32)

def dilated_window_attention(q, k, v, slopes, window, dilation):
    B, S, H, hd = q.shape
    W = window // dilation
    L = S // dilation
    nb = -(-L // W)
    Lp = nb * W

    def to_sub(a):
        a = a.reshape(B, L, dilation, H, hd).transpose(0, 2, 3, 1, 4)
        return jnp.pad(a, ((0, 0), (0, 0), (0, 0), (0, Lp - L), (0, 0)))

    def windows(a):
        ap = jnp.pad(to_sub(a), ((0, 0), (0, 0), (0, 0), (W, 0), (0, 0))).reshape(B, dilation, H, nb + 1, W, hd)
        return jnp.concatenate([ap[:, :, :, :-1], ap[:, :, :, 1:]], axis=-2)

    qs = to_sub(q).reshape(B, dilation, H, nb, W, hd)
    kw = windows(k)
    vw = windows(v).astype(jnp.float32)
    scores = jnp.einsum('brhnqc,brhnkc->brhnqk', qs, kw).astype(jnp.float32) * (hd ** -0.5)
    qi = jnp.arange(W)[:, None]
    kj = jnp.arange(2 * W)[None, :]
    delta = qi + W - kj
    key_sub = (jnp.arange(nb) * W - W)[:, None, None] + kj[None]
    valid = (delta >= 0) & (delta <= W) & (key_sub >= 0)
    bias = -slopes[:, None, None, None] * (delta * dilation).astype(jnp.float32)
    scores = jnp.where(valid, scores + bias, -jnp.inf)
    mx = jnp.max(scores, axis=-1, keepdims=True)
    p = jnp.exp(scores - mx)
    den = jnp.sum(p, axis=-1, keepdims=True)
    o = jnp.einsum('brhnqk,brhnkc->brhnqc', p, vw) / den
    lse = (mx + jnp.log(den))[..., 0]
    o = o.reshape(B, dilation, H, Lp, hd)[:, :, :, :L].transpose(0, 3, 1, 2, 4).reshape(B, S, H, hd)
    lse = lse.reshape(B, dilation, H, Lp)[:, :, :, :L].transpose(0, 3, 1, 2).reshape(B, S, H)
    return o, lse

def dilated_mixture(q, k, v):
    B, S = q.shape[:2]
    slopes = alibi_slopes(DSW_HEADS)
    outs, lses = [], []
    for g, (window, dilation) in enumerate(DSW_GROUPS):
        hs = slice(g * DSW_HEADS_PER_GROUP, (g + 1) * DSW_HEADS_PER_GROUP)
        o, lse = dilated_window_attention(q[:, :, hs], k[:, :, hs], v[:, :, hs], slopes[hs], window, dilation)
        outs.append(o)
        lses.append(lse)
    alpha = jax.nn.softmax(jnp.stack(lses, axis=0), axis=0)
    o = jnp.sum(alpha[..., None] * jnp.stack(outs, axis=0), axis=0)
    return o.reshape(B, S, OUT_A).astype(q.dtype)

def stick_breaking_attention(q, k, v):
    B, S, H, hd = q.shape
    nq = S // BLOCK
    scale = hd ** -0.5
    qb = q.reshape(B, nq, BLOCK, H, hd).transpose(1, 0, 3, 2, 4)
    kt = k.transpose(0, 2, 1, 3)
    vt = v.transpose(0, 2, 1, 3).astype(jnp.float32)
    key_pos = jnp.arange(S)

    def block(args):
        q_blk, i = args
        z = jnp.einsum('bhqc,bhkc->bhqk', q_blk, kt).astype(jnp.float32) * scale
        qpos = i * BLOCK + jnp.arange(BLOCK)
        causal = key_pos[None, :] < qpos[:, None]
        log_stay = jnp.where(causal, jax.nn.log_sigmoid(-z), 0.0)
        later = lax.cumsum(log_stay, axis=3, reverse=True) - log_stay
        attn = jnp.where(causal, jnp.exp(jax.nn.log_sigmoid(z) + later), 0.0)
        return jnp.einsum('bhqk,bhkc->bhqc', attn, vt)

    o = lax.map(block, (qb, jnp.arange(nq)))
    return o.transpose(1, 0, 3, 2, 4).reshape(B, S, H * hd).astype(q.dtype)

def causal_depthwise_conv(a, w, b):
    S = a.shape[1]
    ap = jnp.pad(a, ((0, 0), (CONV_WIDTH - 1, 0), (0, 0)))
    y = b
    for i in range(CONV_WIDTH):
        y = y + ap[:, i:i + S] * w[i]
    return y

def second_inputs(seed: int = 0) -> dict:
    key = jax.random.key(seed)
    ks = jax.random.split(key, 12)
    f32 = jnp.float32
    x = jax.random.normal(ks[0], (BATCH, SEQ, D_MODEL), f32)
    norm1 = 1.0 + 0.05 * jax.random.normal(ks[1], (DEPTH, D_MODEL), f32)
    w_in = jax.random.normal(ks[2], (DEPTH, D_MODEL, N_IN), f32) * D_MODEL ** -0.5
    b_gate = 0.01 * jax.random.normal(ks[3], (DEPTH, 2 * D_MODEL), f32)
    w_br = jax.random.normal(ks[4], (DEPTH, OUT_A + OUT_B, D_MODEL), f32) * OUT_A ** -0.5
    w_o = jax.random.normal(ks[5], (DEPTH, D_MODEL, D_MODEL), f32) * D_MODEL ** -0.5
    norm2 = 1.0 + 0.05 * jax.random.normal(ks[6], (DEPTH, D_MODEL), f32)
    w_up = jax.random.normal(ks[7], (DEPTH, D_MODEL, 2 * D_FF), f32) * D_MODEL ** -0.5
    conv_w = jax.random.normal(ks[8], (DEPTH, CONV_WIDTH, D_FF), f32) * CONV_WIDTH ** -0.5
    conv_b = 0.01 * jax.random.normal(ks[9], (DEPTH, D_FF), f32)
    w_down = jax.random.normal(ks[10], (DEPTH, D_FF, D_MODEL), f32) * D_FF ** -0.5
    norm_f = 1.0 + 0.05 * jax.random.normal(ks[11], (D_MODEL,), f32)
    return {"x": x, "norm1": norm1, "w_in": w_in, "b_gate": b_gate, "w_br": w_br, "w_o": w_o,
            "norm2": norm2, "w_up": w_up, "conv_w": conv_w, "conv_b": conv_b, "w_down": w_down,
            "norm_f": norm_f}

def second_block(x, norm1, w_in, b_gate, w_br, w_o, norm2, w_up, conv_w, conv_b, w_down, norm_f):
    B, S, _ = x.shape
    splits = [W_A, 2 * W_A, 3 * W_A, 3 * W_A + W_B, 3 * W_A + 2 * W_B, 3 * W_A + 3 * W_B]
    for l in range(DEPTH):
        h = rmsnorm_2(x, norm1[l])
        proj = h @ w_in[l]
        qa, ka, va, qb, kb, vb, gate_pre = jnp.split(proj, splits, axis=-1)
        hd4 = lambda t, n: t.reshape(B, S, n, HEAD_DIM)
        o_a = dilated_mixture(hd4(qa, DSW_HEADS), hd4(ka, DSW_HEADS), hd4(va, DSW_HEADS))
        o_b = stick_breaking_attention(hd4(qb, SB_HEADS), hd4(kb, SB_HEADS), hd4(vb, SB_HEADS))
        gates = jax.nn.sigmoid(gate_pre + b_gate[l])
        g_a, g_b = gates[..., :D_MODEL], gates[..., D_MODEL:]
        merged = g_a * (o_a @ w_br[l, :OUT_A]) + g_b * (o_b @ w_br[l, OUT_A:])
        x = x + merged @ w_o[l]
        h2 = rmsnorm_2(x, norm2[l])
        up = h2 @ w_up[l]
        a, v = up[..., :D_FF], up[..., D_FF:]
        a = causal_depthwise_conv(a, conv_w[l], conv_b[l])
        x = x + (jax.nn.gelu(a, approximate=False) * v) @ w_down[l]
    return rmsnorm_2(x, norm_f)


def setup_inputs(seed=0):
    out = dict(first_inputs(seed))
    for name, value in second_inputs(seed + 1).items():
        if name != "x":
            out[name + "_2"] = value
    return out


def reference(
    x, c, ctx, c_ctx, l0_mod_w, l0_mod_b, l0_norm1, l0_norm2, l0_w_in, l0_w_out, l0_mlp_w1,
    l0_mlp_w2, l0_lam_q1, l0_lam_k1, l0_lam_q2, l0_lam_k2, l0_subln, l0_mu, l0_w0_f, l0_w2_f,
    l0_w0_b, l0_w2_b, l0_a0, l0_a2, l0_g2, l0_k_k, l0_k_a, l0_r_k, l0_lnx_w, l0_lnx_b, l1_mod_w,
    l1_mod_b, l1_norm1, l1_norm2, l1_w_in, l1_w_out, l1_mlp_w1, l1_mlp_w2, l1_conv_w, l1_conv_b,
    l1_dt_bias_f, l1_a_log_f, l1_dt_bias_b, l1_a_log_b, l1_d_skip, l1_ssm_norm, l1_gk_up_f,
    l1_gk_b_f, l1_gk_up_b, l1_gk_b_b, l1_gla_norm, final_norm, norm1_2, w_in_2, b_gate_2,
    w_br_2, w_o_2, norm2_2, w_up_2, conv_w_2, conv_b_2, w_down_2, norm_f_2,
):
    x = first_block(
        x, c, ctx, c_ctx, l0_mod_w, l0_mod_b, l0_norm1, l0_norm2, l0_w_in, l0_w_out, l0_mlp_w1,
        l0_mlp_w2, l0_lam_q1, l0_lam_k1, l0_lam_q2, l0_lam_k2, l0_subln, l0_mu, l0_w0_f,
        l0_w2_f, l0_w0_b, l0_w2_b, l0_a0, l0_a2, l0_g2, l0_k_k, l0_k_a, l0_r_k, l0_lnx_w,
        l0_lnx_b, l1_mod_w, l1_mod_b, l1_norm1, l1_norm2, l1_w_in, l1_w_out, l1_mlp_w1,
        l1_mlp_w2, l1_conv_w, l1_conv_b, l1_dt_bias_f, l1_a_log_f, l1_dt_bias_b, l1_a_log_b,
        l1_d_skip, l1_ssm_norm, l1_gk_up_f, l1_gk_b_f, l1_gk_up_b, l1_gk_b_b, l1_gla_norm,
        final_norm,
    )
    return second_block(
        x, norm1_2, w_in_2, b_gate_2, w_br_2, w_o_2, norm2_2, w_up_2, conv_w_2, conv_b_2,
        w_down_2, norm_f_2,
    )


_drawn_inputs = setup_inputs


def setup_inputs(seed=0):
    import zlib

    import numpy as np

    out = dict(_drawn_inputs(seed))
    spreads = {}
    factors = {'l0_norm1': 3.143,
     'l0_lam_q1': 5.303,
     'l0_lam_q2': 64.0,
     'l0_lam_k2': 4.719,
     'l0_subln': 4.041,
     'l0_w2_f': 8.0,
     'l0_w2_b': 8.0,
     'l0_a0': 8.0,
     'l0_k_k': 3.154,
     'l0_k_a': 3.374,
     'l0_lnx_w': 6.487,
     'l0_lnx_b': 24.279,
     'l1_conv_b': 7.195,
     'l1_d_skip': 200.0,
     'l1_ssm_norm': 16.884,
     'l1_gk_b_f': 8.0,
     'l1_gk_b_b': 8.0,
     'l1_gla_norm': 25.55,
     'b_gate_2': 24.375,
     'conv_b_2': 7.882,
     'l0_norm2': 2.887,
     'l1_norm2': 4.316,
     'l1_dt_bias_f': 21.744,
     'l1_a_log_b': 30.248,
     'l1_a_log_f': 8.0,
     'l1_dt_bias_b': 8.0}
    for name, (base, spread) in spreads.items():
        noise = np.random.default_rng([zlib.crc32(name.encode()), seed]).standard_normal(out[name].shape)
        drawn = base * np.exp(spread * noise) if base else spread * noise
        out[name] = __import__('jax').numpy.asarray(drawn.astype(out[name].dtype))
    for name, factor in factors.items():
        out[name] = (out[name] * factor).astype(out[name].dtype)
    return out
```

```python
import math
from contextlib import ExitStack

import concourse.bass as bass
from concourse import mybir
import numpy as np

F32 = mybir.dt.float32
ACT = mybir.ActivationFunctionType
ALU = mybir.AluOpType
AX = mybir.AxisListType

D = 1024
DT = D // 128
CTX, LAT = 256, 512
T = CTX + LAT
EVERY = ((0, CTX), (CTX, LAT))
LATENTS = ((CTX, LAT),)
RELU2, COPY, ADD, GATE, GLU, MERGE = range(6)


class Steps:

    def __init__(self, engine, sem, base=0):
        self.engine, self.sem, self.n, self.base = engine, sem, 0, base

    def did(self, instruction):
        instruction.then_inc(self.sem, 1)
        self.n += 1

    def wait(self):
        self.engine.wait_ge(self.sem, self.base + self.n)


class Side:

    def __init__(self, w_dram, act, out, bias, first, per):
        self.w, self.act, self.out, self.bias, self.first, self.per = w_dram, act, out, bias, first, per


def product(nc, name, w_dram, act, kt, tiles, parts, mode, out, unit=8, per=4, gate=None, bias=None,
            taps=None, side=None, tile0=0, k0=0):
    units = kt // unit
    np_ = len(parts)
    assert per % 2 == 0 and tiles >= per
    ring = per * units
    wide = unit * 128
    F32R = mybir.dt.float32r
    cols = max(t0 + tn for t0, tn in parts)
    SR = 4
    with ExitStack() as st:
        s = Stage(nc, st, name)
        raw = s.sb("raw", [128, ring, wide])
        w_hi, w_lo = (st.enter_context(nc.sbuf_tensor(f"{name}_w{x}", [128, 2, wide], F32R)) for x in ("hi", "lo"))
        a_hi, a_lo = (st.enter_context(nc.sbuf_tensor(f"{name}_a{x}", [128, kt, cols], F32R)) for x in ("hi", "lo"))
        scratch = s.sb("scratch", [128, 2, 512]) if mode in (GLU, MERGE) else None
        psum = [[s.ps(f"acc{b}{p}", [128, 512]) for p in range(np_)] for b in range(2)]
        loaded = [s.sem(f"loaded{r}") for r in range(ring)]
        w_hi_done, w_split, w_used = s.sem("w_hi_done"), s.sem("w_split"), s.sem("w_used")
        a_hi_done, a_split = s.sem("a_hi_done"), s.sem("a_split")
        summed, bank_free, squared = s.sem("summed"), s.sem("bank_free"), s.sem("squared")
        tap0, tap1, tap2, gelu, glu = (s.sem(n) for n in ("tap0", "tap1", "tap2", "gelu", "glu"))
        mine, theirs, merged = s.sem("mine"), s.sem("theirs"), s.sem("merged")
        if side:
            side_w = s.sb("side_w", [128, SR, DT * 128])
            side_ps = [s.ps(f"side{b}", [128, side.per, 2]) for b in range(2)]
            side_loaded = [s.sem(f"side_loaded{r}") for r in range(SR)]
            side_summed, side_read = s.sem("side_summed"), s.sem("side_read")
        block = st.enter_context(nc.Block())
        rounds = tiles // per

        def over_tiles(engine, body):
            if rounds > 1:
                with engine.Fori(0, rounds) as i:
                    for j in range(per):
                        body(i, j, i * per + j)
            else:
                for j in range(per):
                    body(0, j, j)
            for j in range(tiles - rounds * per):
                body(rounds, j, rounds * per + j)

        def split_ahead(engine, split, finish):
            def run(i, js):
                for j in js:
                    split(i, j, i * per + j)
                    if j:
                        finish(i, j - 1, i * per + j - 1)
                    elif not (isinstance(i, int) and i == 0):
                        finish(i - 1, per - 1, i * per - 1)
            run(0, range(per))
            if rounds > 1:
                with engine.Fori(1, rounds) as i:
                    run(i, range(per))
            run(rounds, range(tiles - rounds * per))
            last = tiles - 1
            finish(last // per, last % per, last)

        def unit_at(j, u):
            return j * units + u

        def pair(i, j):
            return i * (per // 2) + j // 2

        @block.sync
        def _(sp):
            def load(i, j, n):
                for u in range(units):
                    sp.wait_ge(w_split, n * units + u + 1)
                    sp.dma_start(raw[:, unit_at(j, u), :],
                                 w_dram[bass.ds(n + tile0, 1), :, (k0 + u * unit) * 128:(k0 + (u + 1) * unit) * 128])\
                      .then_inc(loaded[unit_at(j, u)], 16)
                if side:
                    for k in range(side.per):
                        q = j * side.per + k
                        sp.wait_ge(side_summed, n * side.per + k + 1)
                        sp.dma_start(side_w[:, q % SR, :], side.w[bass.ds(n * side.per + (k + side.first), 1), :, :])\
                          .then_inc(side_loaded[q % SR], 16)
            over_tiles(sp, load)

        @block.tensor
        def _(pe):
            mm = nc.tensor.matmul
            pe.sem_inc(w_used, 2)
            if side:
                pe.sem_inc(side_summed, SR)

            def tile(i, j, n):
                for u in range(units):
                    r = unit_at(j, u) % 2
                    pe.wait_ge(w_split, n * units + u + 1 + ring)
                    for p, (t0, tn) in enumerate(parts):
                        if u == 0:
                            pe.wait_ge(bank_free, n * np_ + p + 1)
                        own = range(p * kt // 2, (p + 1) * kt // 2) if mode == MERGE else range(unit)
                        for k in own:
                            if isinstance(i, int) and i == 0 and j == 0:
                                pe.wait_ge(a_split, u * unit + k + 1)
                            w = slice(k * 128, (k + 1) * 128)
                            x = u * unit + k
                            for q, (lhs, rhs) in enumerate(((w_hi, a_hi), (w_lo, a_hi), (w_hi, a_lo))):
                                ins = mm(psum[j % 2][p][:, 0:tn], lhs[:, r, w], rhs[:, x, t0:t0 + tn],
                                         start=(u == 0 and k == own[0] and q == 0),
                                         stop=(u == units - 1 and k == own[-1] and q == 2))
                        if u == units - 1:
                            ins.then_inc(summed, 1)
                    if u < units - 1:
                        ins.then_inc(w_used, 1)
                    else:
                        pe.wait_ge(summed, (n + 1) * np_)
                        pe.sem_inc(w_used, 1)
                if side:
                    pe.wait_ge(side_read, n + 1)
                    for k in range(side.per):
                        q = j * side.per + k
                        pe.wait_ge(side_loaded[q % SR], 16 * (i * (per * side.per // SR) + q // SR + 1))
                        for x in range(DT):
                            ins = mm(side_ps[j % 2][:, k, :], side_w[:, q % SR, x * 128:(x + 1) * 128],
                                     side.act[:, x, :], start=(x == 0), stop=(x == DT - 1))
                        ins.then_inc(side_summed, 1)

            for j in range(per):
                tile(0, j, j)
            if rounds > 1:
                with pe.Fori(1, rounds) as i:
                    for j in range(per):
                        tile(i, j, i * per + j)
            for j in range(tiles - rounds * per):
                tile(rounds, j, rounds * per + j)

        @block.scalar
        def _(act_e):
            A = nc.scalar.activation
            for k in range(kt):
                A(a_hi[:, k, :], act[:, k, 0:cols], ACT.Copy).then_inc(a_hi_done, 1)
            if mode in (COPY, RELU2, GATE):
                act_e.sem_inc(bank_free, 2 * np_)
            if side:
                act_e.sem_inc(side_read, 2)

            def split(i, j, n):
                for u in range(units):
                    g = unit_at(j, u)
                    act_e.wait_ge(loaded[g], 16 * (i + 1))
                    act_e.wait_ge(w_used, n * units + u + 1)
                    A(w_hi[:, g % 2, :], raw[:, g, :], ACT.Copy).then_inc(w_hi_done, 1)

            def finish(i, j, n):
                if mode in (COPY, RELU2, GATE):
                    for p, (t0, tn) in enumerate(parts):
                        act_e.wait_ge(summed, n * np_ + p + 1)
                        dst = out[:, bass.ds(n, 1), t0:t0 + tn]
                        src = psum[j % 2][p][:, 0:tn]
                        if mode == GATE:
                            ins = A(dst, src, ACT.Sigmoid, bias=bias[:, bass.ds(n, 1)])
                        else:
                            ins = A(dst, src, ACT.Relu if mode == RELU2 else ACT.Copy)
                        ins.then_inc(bank_free, 1)
                if mode == GLU and j % 2 == 0:
                    m = pair(i, j)
                    x = scratch[:, j // 2 % 2, :]
                    act_e.wait_ge(summed, n + 1)
                    act_e.wait_ge(glu, m + 1)
                    A(x, psum[0][0][:, :], ACT.Identity, scale=taps(2, m), bias=bias[:, bass.ds(m, 1)])\
                        .then_inc(tap0, 1)
                    act_e.wait_ge(tap2, m + 1)
                    A(x, x, ACT.Gelu).then_inc(gelu, 1)
                if side:
                    act_e.wait_ge(side_summed, (n + 1) * side.per + SR)
                    for k in range(side.per):
                        t = n * side.per + (k + side.first)
                        ins = A(side.out[:, bass.ds(t, 1), :], side_ps[j % 2][:, k:k + 1, :], ACT.Identity,
                                bias=side.bias[:, bass.ds(t, 1)])
                    ins.then_inc(side_read, 1)
            split_ahead(act_e, split, finish)

        @block.vector
        def _(dve):
            V = nc.vector
            dve.sem_inc(w_split, ring)
            if mode in (ADD, MERGE, GLU):
                dve.sem_inc(bank_free, 2 * np_)
            for q, mine_too in ((merged, MERGE), (glu, GLU)):
                if mode == mine_too:
                    dve.sem_inc(q, 1)
            for k in range(kt):
                dve.wait_ge(a_hi_done, k + 1)
                V.tensor_tensor(a_lo[:, k, :], act[:, k, 0:cols], a_hi[:, k, :].bitcast(F32), ALU.subtract)\
                    .then_inc(a_split, 1)

            def split(i, j, n):
                for u in range(units):
                    g = unit_at(j, u)
                    dve.wait_ge(w_hi_done, n * units + u + 1)
                    V.tensor_tensor(w_lo[:, g % 2, :], raw[:, g, :], w_hi[:, g % 2, :].bitcast(F32), ALU.subtract)\
                        .then_inc(w_split, 1)

            def finish(i, j, n):
                if mode == ADD:
                    for p, (t0, tn) in enumerate(parts):
                        dve.wait_ge(summed, n * np_ + p + 1)
                        dst = out[:, bass.ds(n, 1), t0:t0 + tn]
                        src = psum[j % 2][p][:, 0:tn]
                        if gate is None:
                            V.tensor_tensor(dst, src, dst, ALU.add).then_inc(bank_free, 1)
                        else:
                            g = gate[:, bass.ds(n, 1), p + 2 - np_]
                            V.scalar_tensor_tensor(dst, src, g, dst, ALU.mult, ALU.add).then_inc(bank_free, 1)
                if mode == MERGE:
                    x, dst = scratch[:, j % 2:j % 2 + 1, :], out[:, bass.ds(n, 1), :]
                    dve.wait_ge(summed, (n + 1) * 2)
                    dve.wait_ge(merged, n + 1)
                    V.tensor_tensor(x, gate[:, bass.ds(n, 1), :], psum[j % 2][0][:].unsqueeze(1), ALU.mult)\
                        .then_inc(mine, 1)
                    V.tensor_tensor(dst, gate[:, bass.ds(n + tiles, 1), :], psum[j % 2][1][:].unsqueeze(1), ALU.mult)\
                        .then_inc(theirs, 1)
                    dve.wait_ge(mine, n + 1)
                    dve.wait_ge(theirs, n + 1)
                    dve.sem_inc(bank_free, 2)
                    V.tensor_tensor(dst, dst, x, ALU.add).then_inc(merged, 1)
                if mode == GLU:
                    m = pair(i, j)
                    x = scratch[:, j // 2 % 2, :]
                    if j % 2 == 0:
                        a = psum[0][0]
                        dve.wait_ge(tap0, m + 1)
                        V.scalar_tensor_tensor(x[:, 1:LAT], a[:, 0:LAT - 1], taps(1, m), x[:, 1:LAT],
                                               ALU.mult, ALU.add).then_inc(tap1, 1)
                        dve.wait_ge(tap1, m + 1)
                        V.scalar_tensor_tensor(x[:, 2:LAT], a[:, 0:LAT - 2], taps(0, m), x[:, 2:LAT],
                                               ALU.mult, ALU.add).then_inc(tap2, 1)
                        dve.wait_ge(tap2, m + 1)
                        dve.sem_inc(bank_free, 1)
                    else:
                        dve.wait_ge(summed, n + 1)
                        dve.wait_ge(gelu, m + 1)
                        V.tensor_tensor(out[:, bass.ds(m, 1), :], x.unsqueeze(1), psum[1][0][:].unsqueeze(1),
                                        ALU.mult).then_inc(glu, 1)
                        dve.wait_ge(glu, m + 2)
                        dve.sem_inc(bank_free, 1)
            split_ahead(dve, split, finish)

        if mode == RELU2:
            @block.gpsimd
            def _(pool):
                def square(i, j, n):
                    pool.wait_ge(bank_free, 2 * np_)
                    pool.wait_ge(bank_free, (n + 1) * np_ + 2 * np_)
                    for t0, tn in parts:
                        dst = out[:, bass.ds(n, 1), t0:t0 + tn]
                        nc.gpsimd.tensor_tensor(dst, dst, dst, ALU.mult).then_inc(squared, 1)
                over_tiles(pool, square)


def small_product(nc, name, w_dram, act, tiles, out, bias, per=4):
    with ExitStack() as st:
        s = Stage(nc, st, name)
        w = s.sb("w", [128, 2 * per, DT * 128])
        bank = [s.ps(f"bank{b}", [128, 2]) for b in range(2)]
        loaded = [s.sem(f"loaded{r}") for r in range(2 * per)]
        summed, read = s.sem("summed"), s.sem("read")
        block = st.enter_context(nc.Block())

        @block.sync
        def _(sp):
            for n in range(tiles):
                if n >= 2 * per:
                    sp.wait_ge(summed, n - 2 * per + 1)
                sp.dma_start(w[:, n % (2 * per), :], w_dram[n]).then_inc(loaded[n % (2 * per)], 16)

        @block.tensor
        def _(pe):
            for n in range(tiles):
                pe.wait_ge(loaded[n % (2 * per)], 16 * (n // (2 * per) + 1))
                if n >= 2:
                    pe.wait_ge(read, n - 1)
                for k in range(DT):
                    ins = nc.tensor.matmul(bank[n % 2][:, :], w[:, n % (2 * per), k * 128:(k + 1) * 128], act[:, k, :],
                                           start=(k == 0), stop=(k == DT - 1))
                ins.then_inc(summed, 1)

        @block.scalar
        def _(act_e):
            for n in range(tiles):
                act_e.wait_ge(summed, n + 1)
                nc.scalar.activation(out[:, n, :], bank[n % 2][:, :], ACT.Identity, bias=bias[:, n:n + 1])\
                    .then_inc(read, 1)


HALF = 64
RC = 64
DECAY = 0.6065306597126334


class Stage:

    def __init__(self, nc, st, name):
        self.nc, self.st, self.name, self.sems = nc, st, name, {}
        st.callback(self.close)

    def seed(self):
        for sem in self.sems.values():
            self.nc.gpsimd.sem_inc(sem, 1)
        self.nc.all_engine_barrier()

    def close(self):
        if self.sems:
            for sem in self.sems.values():
                self.nc.gpsimd.sem_clear(sem)
                self.nc.release_semaphore(sem)

    def sb(self, name, shape):
        return self.st.enter_context(self.nc.sbuf_tensor(f"{self.name}_{name}", shape, F32))

    def ps(self, name, shape):
        return self.st.enter_context(self.nc.psum_tensor(f"{self.name}_{name}", shape, F32))

    def sem(self, name):
        if name not in self.sems:
            self.sems[name] = self.nc.alloc_semaphore(name=f"{self.name}_{name}")
        return self.sems[name]


def bcast(ap, axis, n):
    wide = ap.unsqueeze(axis)
    return wide.broadcast_to([n if k == axis else m for k, m in enumerate(wide.shape)])


def scan_views(d, seg, t0, m):
    base, n = seg
    start = t0[d]

    def view(x, lo, tiles=4):
        return x[:, lo:lo + tiles, base:base + n][:, :, bass.ds(start, m)]
    return view


def scan_steps(engine, body, m):
    for seg, u0 in ((EVERY[0], 0), (EVERY[1], CTX // m)):
        with engine.register(f"back_{engine.bass.next_id()}") as back:
            engine.reg_mov(back, seg[1] - m)
            with engine.Fori(0, seg[1] // m) as i:
                body(seg, (i * m, engine.snap(back, min_val=0, max_val=seg[1] - m)), i + u0)
                engine.reg_sub(back, back, m)


def turned(d, x):
    if d == 0:
        return x
    return x[(slice(None),) * (len(x.shape) - 1) + (slice(None, None, -1),)]


def rwkv_prepare(nc, p, sig, kk, a, col, w_lora, c):
    with ExitStack() as st:
        s = Stage(nc, st, "rp")
        tmp = s.sb("tmp", [128, 2, T])
        tw = s.sb("tw", [64, T])
        lora_a, lora_b = s.sb("lora_a", [128, 512]), s.sb("lora_b", [64, 512])
        sq = s.sb("sq", [128, 2, T])
        inv = s.sb("inv", [128, 2, T])
        acc = [s.ps(f"acc{b}", [128, 1024]) for b in range(2)]
        nrm = [s.ps(f"nrm{b}", [128, 1024]) for b in range(2)]
        sem = s.sem
        order = [12, 13] + list(range(0, 12))
        block = st.enter_context(nc.Block())
        for n in ("loaded", "shifted", "dstep", "tanh", "lora_sum", "sig_done", "kk_raw", "squared",
                  "norm_sum", "root", "kk_done", "acc_read"):
            sem(n)

        @block.sync
        def _(sp):
            sp.dma_start(lora_a[:, :], w_lora[0]).then_inc(sem("loaded"), 16)
            sp.dma_start(lora_b[:, :], w_lora[1][0:64, :]).then_inc(sem("loaded"), 16)

        @block.vector
        def _(dve):
            k = Steps(dve, sem("dstep"))
            for i, m in enumerate(order):
                x, y = p[:, 12 + m, :], tmp[:, i % 2, :]
                k.did(nc.vector.tensor_tensor(y[:, 1:T - 1], x[:, 0:T - 2], x[:, 2:T], ALU.add))
                k.wait()
                k.did(nc.vector.tensor_copy(y[:, 0:CTX + 1:CTX], x[:, 1:CTX + 2:CTX]))
                k.did(nc.vector.tensor_copy(y[:, CTX - 1:T:LAT], x[:, CTX - 2:T - 1:LAT]))
                k.wait()
                k.did(nc.vector.scalar_tensor_tensor(y, y, 0.5, x, ALU.mult, ALU.subtract))
                k.wait()
                nc.vector.scalar_tensor_tensor(x, y, col("mu", m), x, ALU.mult, ALU.add)\
                    .then_inc(sem("shifted"), 1)
                dve.wait_ge(sem("shifted"), i + 1)
            for t in range(4):
                nc.vector.tensor_scalar(kk[:, t, :], p[:, 16 + t, :], col("k_k", t), None, ALU.mult)\
                    .then_inc(sem("kk_raw"), 1)
            for t in range(4):
                dve.wait_ge(sem("root"), t + 1)
                r = inv[:, t % 2, :]
                k.did(nc.vector.tensor_scalar_max(r, r, 1e-12))
                k.wait()
                k.did(nc.vector.reciprocal(r, r))
                k.wait()
                dve.wait_ge(sem("kk_raw"), 4)
                dve.wait_ge(sem("squared"), t + 1)
                nc.vector.tensor_tensor(kk[:, t, :], kk[:, t, :], r, ALU.mult).then_inc(sem("kk_done"), 1)
            for t in range(4):
                dve.wait_ge(sem("sig_done"), 8 + t + 1)
                y = tmp[:, t % 2, :]
                k.wait()
                k.did(nc.vector.tensor_scalar(y, a[:, t, :], -1.0, col("k_a", t), ALU.add, ALU.mult))
                k.wait()
                k.did(nc.vector.scalar_tensor_tensor(p[:, 16 + t, :], y, 1.0, p[:, 16 + t, :], ALU.add, ALU.mult))
                dve.wait_ge(sem("kk_done"), t + 1)
                k.did(nc.vector.tensor_tensor(a[:, t, :], a[:, t, :], kk[:, t, :], ALU.mult))
            for t in range(8):
                dve.wait_ge(sem("sig_done"), t + 1)
                x = sig[:, t, :] if t < 4 else sig[:, t, ::-1]
                k.did(nc.vector.tensor_tensor_scan(x, c["chunk_mask"], x, 0.0, ALU.mult, ALU.add))

        @block.tensor
        def _(pe):
            pe.wait_ge(sem("loaded"), 32)
            pe.wait_ge(sem("tanh"), 1)
            pe.wait_ge(sem("shifted"), 2)
            for n in range(12):
                kind, m = n // 4, n % 4
                lhs = (lora_a[0:64], lora_b[0:64], lora_a[64:128])[kind][:, m * 128:(m + 1) * 128]
                rhs = (tw[:, :], tw[:, :], p[64:128, 24, :])[kind]
                if n >= 2:
                    pe.wait_ge(sem("sig_done"), n - 1)
                for t0, tn in ((0, 512), (512, 256)):
                    ins = nc.tensor.matmul(acc[n % 2][:, t0:t0 + tn], lhs, rhs[:, t0:t0 + tn],
                                           start=True, stop=True)
                ins.then_inc(sem("lora_sum"), 1)
            for t in range(4):
                pe.wait_ge(sem("squared"), t + 1)
                if t >= 2:
                    pe.wait_ge(sem("root"), t - 1)
                for t0, tn in ((0, 512), (512, 256)):
                    ins = nc.tensor.matmul(nrm[t % 2][:, t0:t0 + tn], c["head_ones"], sq[:, t % 2, t0:t0 + tn],
                                           start=True, stop=True)
                ins.then_inc(sem("norm_sum"), 1)

        @block.scalar
        def _(act):
            act.wait_ge(sem("shifted"), 1)
            nc.scalar.activation(tw[:, :], p[0:64, 24, :], ACT.Tanh).then_inc(sem("tanh"), 1)
            for n in range(12):
                kind, m = n // 4, n % 4
                act.wait_ge(sem("lora_sum"), n + 1)
                dst = (sig[:, m, :], sig[:, 4 + m, :], a[:, m, :])[kind]
                nc.scalar.activation(dst, acc[n % 2][:, 0:T], ACT.Sigmoid,
                                     bias=col(("w0_f", "w0_b", "a0")[kind], m)).then_inc(sem("sig_done"), 1)
            for t in range(4):
                act.wait_ge(sem("kk_raw"), t + 1)
                if t >= 2:
                    act.wait_ge(sem("norm_sum"), t - 1)
                nc.scalar.activation(sq[:, t % 2, :], kk[:, t, :], ACT.Square).then_inc(sem("squared"), 1)
                act.wait_ge(sem("norm_sum"), t + 1)
                if t >= 2:
                    act.wait_ge(sem("kk_done"), t - 1)
                nc.scalar.activation(inv[:, t % 2, :], nrm[t % 2][:, 0:T], ACT.Sqrt).then_inc(sem("root"), 1)


def rwkv_scan(nc, p, sig, kk, b, y, c):
    with ExitStack() as st:
        s = Stage(nc, st, "rs")
        sem = s.sem
        W = [128, 4, 128]
        dirs = range(2)
        mk = lambda n, shape=W: [s.sb(f"{n}{d}", shape) for d in dirs]
        E, IE = mk("E", [128, 4, 2, RC + 1]), mk("IE", [128, 4, 2, RC])
        A, B, K, R, V = mk("A"), mk("B"), mk("K"), mk("R"), mk("V")
        Vt, Kt, Bt, L, X, XT = mk("Vt"), mk("Kt"), mk("Bt"), mk("L"), mk("X"), mk("XT")
        Q, MT, RKT, RBT, S = mk("Q"), mk("MT"), mk("RKT"), mk("RBT"), mk("S")
        C = [[V[d], K[d]] for d in dirs]
        RHS, SAn = L, Q
        bank = [[s.ps(f"b{d}{j}", [128, 4, 128]) for j in range(4)] for d in dirs]
        sem("zeroed")
        names = {n: [sem(f"{n}{d}") for d in dirs] for n in
                 ("decay", "staged", "p1", "p2", "L", "x0", "x1", "m", "rb", "tr", "join", "q", "qs",
                  "pp", "xs", "rhs", "rhss", "sa", "sas", "ys", "yr", "ss", "sadd", "sadd2", "snew")}
        wend = mk("wend", [128, 4])
        ident, m_low, m_str_t, m_inc_t, levels, halves = (
            c["ident"], c["lower"], c["upper"], c["upper_inc"], c["levels"], c["halves"])
        pairs = lambda m: bcast(m, 1, 4)
        LEV = 6
        s.seed()
        block = st.enter_context(nc.Block())

        def steps(engine, body):
            scan_steps(engine, body, RC)

        @block.vector
        def _(dve):
            N = names
            for d in dirs:
                for t in (E[d], IE[d], S[d]):
                    nc.vector.memset(t[:], 0.0).then_inc(sem("zeroed"), 1)
            dve.wait_ge(sem("zeroed"), 1 + 6)
            for d in dirs:
                for h in range(2):
                    nc.vector.memset(E[d][64 * h:64 * h + 64, :, h, 0:1], 1.0).then_inc(sem("zeroed"), 1)
            nc.vector.memset(y[:, :, :], 0.0).then_inc(sem("zeroed"), 1)
            dve.wait_ge(sem("zeroed"), 1 + 11)

            def body(seg, t0, u):
                for d in dirs:
                    v = scan_views(d, seg, t0, RC)
                    out4 = lambda x: turned(d, x[d][:].rearrange("p a (h t) -> p a h t", h=2))
                    in4 = lambda x: bcast(x, 2, 2)
                    dve.wait_ge(N["decay"][d], 1 + 4 * u + 4)
                    dve.wait_ge(N["ss"][d], 1 + u)
                    dve.wait_ge(N["qs"][d], 1 + (LEV - 1) * u)
                    nc.vector.tensor_tensor(out4(A), in4(v(kk, 0)), turned(d, E[d][:, :, :, 0:RC]), ALU.mult)\
                        .then_inc(N["staged"][d], 1)
                    nc.vector.tensor_tensor(out4(B), in4(v(b, 0)), turned(d, IE[d][:]), ALU.mult).then_inc(N["staged"][d], 1)
                    nc.vector.tensor_tensor(out4(K), in4(v(p, 16)), turned(d, IE[d][:]), ALU.mult).then_inc(N["staged"][d], 1)
                    nc.vector.tensor_tensor(out4(R), in4(v(p, 12)), turned(d, E[d][:, :, :, 1:RC + 1]), ALU.mult)\
                        .then_inc(N["staged"][d], 1)
                    nc.vector.tensor_tensor(out4(V), in4(v(p, 20)), bcast(bcast(halves, 1, 4), 3, RC), ALU.mult)\
                        .then_inc(N["staged"][d], 1)
                for d in dirs:
                    dve.wait_ge(N["p1"][d], 1 + 2 * u + 1)
                    nc.vector.tensor_tensor(L[d][:], bank[d][0][:], pairs(m_low), ALU.mult).then_inc(N["L"][d], 1)
                    nc.vector.tensor_tensor(XT[d][:], bank[d][1][:], pairs(c["level1_t"]), ALU.mult)\
                        .then_inc(N["x0"][d], 1)
                    dve.wait_ge(N["L"][d], 1 + u + 1)
                    nc.vector.tensor_tensor(X[d][:], L[d][:], pairs(c["level1"]), ALU.mult).then_inc(N["x0"][d], 1)
                    dve.wait_ge(N["x0"][d], 1 + 2 * u + 2)
                    nc.vector.tensor_tensor(XT[d][:], pairs(ident), XT[d][:], ALU.subtract).then_inc(N["x1"][d], 1)
                    nc.vector.tensor_tensor(X[d][:], pairs(ident), X[d][:], ALU.subtract).then_inc(N["x1"][d], 1)
                for d in dirs:
                    dve.wait_ge(N["p1"][d], 1 + 2 * u + 2)
                    nc.vector.tensor_tensor(MT[d][:], bank[d][2][:], pairs(m_str_t), ALU.mult).then_inc(N["m"][d], 1)
                    nc.vector.tensor_tensor(RKT[d][:], bank[d][3][:], pairs(m_inc_t), ALU.mult).then_inc(N["m"][d], 1)
                for d in dirs:
                    dve.wait_ge(N["p2"][d], 1 + 2 * u + 1)
                    nc.vector.tensor_tensor(RBT[d][:], bank[d][0][:], pairs(m_inc_t), ALU.mult).then_inc(N["rb"][d], 1)
                for l in range(1, LEV):
                    for d in dirs:
                        dve.wait_ge(N["pp"][d], 1 + (LEV - 1) * u + l)
                        dve.wait_ge(N["x1"][d], 1 + 2 * u + 2)
                        if l > 1:
                            dve.wait_ge(N["xs"][d], 1 + 2 * ((LEV - 1) * u + l - 1))
                        nc.vector.tensor_tensor(X[d][:], X[d][:], bank[d][1][:], ALU.subtract).then_inc(N["xs"][d], 1)
                        nc.vector.tensor_tensor(XT[d][:], XT[d][:], bank[d][2][:], ALU.subtract).then_inc(N["xs"][d], 1)
                for d in dirs:
                    v = scan_views(d, seg, t0, RC)
                    dve.wait_ge(N["ys"][d], 1 + u + 1)
                    if d:
                        dve.wait_ge(N["yr"][0], 1 + u + 1)
                    dve.wait_ge(N["yr"][d], 1 + u)
                    if not d:
                        dve.wait_ge(N["yr"][1], 1 + u)
                    yv = v(y, 0)
                    nc.vector.tensor_tensor(yv, yv, turned(d, bank[d][3][:, :, 0:RC]), ALU.add).then_inc(N["yr"][d], 1)
                    dve.wait_ge(N["ss"][d], 1 + u + 1)
                    nc.vector.tensor_tensor(S[d][:], S[d][:], bank[d][0][:], ALU.add).then_inc(N["sadd"][d], 1)
                    dve.wait_ge(N["sadd"][d], 1 + u + 1)
                    nc.vector.tensor_tensor(wend[d][:], E[d][:, :, 0, RC], E[d][:, :, 1, RC], ALU.add)\
                        .then_inc(N["sadd2"][d], 1)
                    dve.wait_ge(N["sadd2"][d], 1 + u + 1)
                    nc.vector.tensor_tensor(S[d][:], S[d][:], bcast(wend[d][:], 2, 128), ALU.mult)\
                        .then_inc(N["snew"][d], 1)
            steps(dve, body)

        @block.scalar
        def _(act):
            N = names
            act.wait_ge(sem("zeroed"), 1 + 11)

            def body(seg, t0, u):
                for d in dirs:
                    v = scan_views(d, seg, t0, RC)
                    act.wait_ge(N["staged"][d], 1 + 5 * u)
                    act.wait_ge(N["snew"][d], 1 + u)
                    for h in range(2):
                        rows = slice(64 * h, 64 * h + 64)
                        src = v(sig, 4 * d)[rows]
                        nc.scalar.activation(turned(d, E[d][rows, :, h, 1:RC + 1]), src, ACT.Exp, scale=-DECAY)\
                            .then_inc(N["decay"][d], 1)
                        nc.scalar.activation(turned(d, IE[d][rows, :, h, :]), src, ACT.Exp, scale=DECAY)\
                            .then_inc(N["decay"][d], 1)
                for d in dirs:
                    act.wait_ge(N["p2"][d], 1 + 2 * u + 2)
                    for j, x in enumerate((Vt, Kt, Bt)):
                        nc.scalar.activation(x[d][:], bank[d][1 + j][:], ACT.Copy).then_inc(N["tr"][d], 1)
                for l in range(1, LEV):
                    for d in dirs:
                        act.wait_ge(N["q"][d], 1 + (LEV - 1) * u + l)
                        nc.scalar.activation(Q[d][:], bank[d][0][:], ACT.Copy).then_inc(N["qs"][d], 1)
                for d in dirs:
                    act.wait_ge(N["rhs"][d], 1 + u + 1)
                    act.wait_ge(N["join"][d], 1 + (LEV - 1) * (u + 1))
                    nc.scalar.activation(RHS[d][:], bank[d][3][:], ACT.Copy).then_inc(N["rhss"][d], 1)
                for d in dirs:
                    act.wait_ge(N["sa"][d], 1 + u + 1)
                    nc.scalar.activation(SAn[d][:], bank[d][0][:], ACT.Copy, scale=-1.0).then_inc(N["sas"][d], 1)
            steps(act, body)

        @block.gpsimd
        def _(pool):
            N = names

            def body(seg, t0, u):
                for l in range(1, LEV):
                    for d in dirs:
                        if l == 1:
                            pool.wait_ge(N["L"][d], 1 + u + 1)
                            pool.wait_ge(N["p2"][d], 1 + 2 * u + 2)
                            pool.wait_ge(N["p1"][d], 1 + 2 * u + 2)
                        if l > 2:
                            pool.wait_ge(N["q"][d], 1 + (LEV - 1) * u + l - 2)
                        nc.gpsimd.tensor_tensor(C[d][l % 2][:], L[d][:], pairs(levels[:, l, :]), ALU.mult)\
                            .then_inc(N["join"][d], 1)
            steps(pool, body)

        @block.tensor
        def _(pe):
            N = names

            def each(d, j, lhs, rhs, start=True, stop=True, out=None):
                for q in range(4):
                    ins = nc.tensor.matmul(bank[d][j][:, q, :], lhs[d][:, q, :], rhs[d][:, q, :],
                                           start=start, stop=stop)
                return ins

            def body(seg, t0, u):
                for d in dirs:
                    pe.wait_ge(N["staged"][d], 1 + 5 * u + 5)
                    pe.wait_ge(N["sas"][d], 1 + u)
                    pe.wait_ge(N["yr"][d], 1 + u)
                    pe.wait_ge(N["snew"][d], 1 + u)
                    pe.wait_ge(N["xs"][d], 1 + 2 * (LEV - 1) * u)
                    each(d, 0, A, B)
                    each(d, 1, B, A).then_inc(N["p1"][d], 1)
                    each(d, 2, K, A)
                    each(d, 3, K, R).then_inc(N["p1"][d], 1)
                for d in dirs:
                    pe.wait_ge(N["L"][d], 1 + u + 1)
                    each(d, 0, B, R).then_inc(N["p2"][d], 1)
                    pe.wait_ge(N["x0"][d], 1 + 2 * u + 1)
                    pe.wait_ge(N["m"][d], 1 + 2 * u + 2)
                    for j, x in enumerate((V, K, B)):
                        for q in range(4):
                            ins = nc.tensor.transpose(bank[d][1 + j][:, q, :], x[d][:, q, :], ident)
                    ins.then_inc(N["p2"][d], 1)
                for l in range(1, LEV):
                    for d in dirs:
                        pe.wait_ge(N["join"][d], 1 + (LEV - 1) * u + l)
                        if l == 1:
                            pe.wait_ge(N["x1"][d], 1 + 2 * u + 2)
                            pe.wait_ge(N["rb"][d], 1 + u + 1)
                            pe.wait_ge(N["tr"][d], 1 + 3 * u + 3)
                        else:
                            pe.wait_ge(N["xs"][d], 1 + 2 * ((LEV - 1) * u + l - 1))
                        each(d, 0, C_at(d, l), XT).then_inc(N["q"][d], 1)
                    for d in dirs:
                        pe.wait_ge(N["qs"][d], 1 + (LEV - 1) * u + l)
                        each(d, 1, Q, X)
                        each(d, 2, X, Q).then_inc(N["pp"][d], 1)
                for d in dirs:
                    for q in range(4):
                        nc.tensor.matmul(bank[d][3][:, q, :], A[d][:, q, :], S[d][:, q, :], start=True, stop=False)
                        ins = nc.tensor.matmul(bank[d][3][:, q, :], MT[d][:, q, :], Vt[d][:, q, :],
                                               start=False, stop=True)
                    ins.then_inc(N["rhs"][d], 1)
                for d in dirs:
                    pe.wait_ge(N["rhss"][d], 1 + u + 1)
                    pe.wait_ge(N["xs"][d], 1 + 2 * (LEV - 1) * (u + 1))
                    each(d, 0, XT, RHS).then_inc(N["sa"][d], 1)
                for d in dirs:
                    pe.wait_ge(N["sas"][d], 1 + u + 1)
                    for q in range(4):
                        n = 0
                        for lhs, rhs in ((S, R), (Vt, RKT), (SAn, RBT)):
                            for h in range(2):
                                ins = nc.tensor.matmul(bank[d][3][:, q, 0:RC], lhs[d][:, q, :],
                                                       rhs[d][:, q, h * RC:(h + 1) * RC],
                                                       start=(n == 0), stop=(n == 5))
                                n += 1
                    ins.then_inc(N["ys"][d], 1)
                    for q in range(4):
                        nc.tensor.matmul(bank[d][0][:, q, :], Kt[d][:, q, :], Vt[d][:, q, :], start=True, stop=False)
                        ins = nc.tensor.matmul(bank[d][0][:, q, :], Bt[d][:, q, :], SAn[d][:, q, :],
                                               start=False, stop=True)
                    ins.then_inc(N["ss"][d], 1)

            def C_at(d, l):
                return {d: C[d][l % 2]}
            steps(pe, body)


def square_masks():
    i, j = np.arange(128)[:, None], np.arange(128)[None, :]
    same = i // 64 == j // 64
    m = {"ident": i == j, "lower": same & (i > j), "upper": same & (i < j), "upper_inc": same & (i <= j),
         "head_ones": same, "ones": i + j >= 0}
    for l in range(6):
        b = 2 << l
        m[f"level{l}"] = (i // b == j // b) & (i % b >= b // 2) & (j % b < b // 2)
    m["level1_t"] = m["level0"].T
    return m


CHUNK = 128


def ssd_prepare(nc, p, dtla, col, c):
    PAD = CTX + LAT + 6
    OUT = PAD - 4
    with ExitStack() as st:
        s = Stage(nc, st, "sp")
        sem = s.sem
        xp, acc = s.sb("xp", [128, 2, PAD]), s.sb("acc", [128, 2, OUT])
        h = s.sb("h", [16, 6, T])
        na = s.sb("na", [16, 2])
        for n in ("zero", "padded", "tap0", "conv", "done", "dstep", "absd", "e", "l", "na"):
            sem(n)
        block = st.enter_context(nc.Block())

        def finish(act, i):
            y = acc[:, i % 2, :]
            act.wait_ge(sem("conv"), i + 1)
            nc.scalar.activation(p[:, 4 + i, 0:CTX], y[:, 0:CTX], ACT.Silu).then_inc(sem("done"), 1)
            nc.scalar.activation(p[:, 4 + i, CTX:T], y[:, CTX + 2:OUT], ACT.Silu).then_inc(sem("done"), 1)

        @block.scalar
        def _(act):
            nc.scalar.activation(na[:, 0:1], col("a_log", 0)[0:16], ACT.Exp).then_inc(sem("na"), 1)
            act.wait_ge(sem("dstep"), 1)
            nc.scalar.activation(h[:, 1, :], h[:, 0, :], ACT.Abs).then_inc(sem("absd"), 1)
            act.wait_ge(sem("absd"), 1)
            nc.scalar.activation(h[:, 2, :], h[:, 1, :], ACT.Exp, scale=-1.0).then_inc(sem("e"), 1)
            act.wait_ge(sem("dstep"), 2)
            nc.scalar.activation(h[:, 4, :], h[:, 3, :], ACT.Ln).then_inc(sem("l"), 1)
            act.wait_ge(sem("zero"), 2)
            for i in range(8):
                x, y = xp[:, i % 2, :], acc[:, i % 2, :]
                if i >= 2:
                    act.wait_ge(sem("conv"), i - 1)
                nc.scalar.activation(x[:, 2:2 + CTX], p[:, 4 + i, 0:CTX], ACT.Copy).then_inc(sem("padded"), 1)
                nc.scalar.activation(x[:, 4 + CTX:4 + T], p[:, 4 + i, CTX:T], ACT.Copy).then_inc(sem("padded"), 1)
                act.wait_ge(sem("padded"), 2 * i + 2)
                if i >= 2:
                    act.wait_ge(sem("done"), 2 * (i - 1))
                nc.scalar.activation(y, x[:, 0:OUT], ACT.Identity, scale=col("conv_w", i),
                                     bias=col("conv_b", i)).then_inc(sem("tap0"), 1)
                if i >= 1:
                    finish(act, i - 1)
            finish(act, 7)

        @block.vector
        def _(dve):
            k = Steps(dve, sem("dstep"))
            V = nc.vector
            for b in range(2):
                V.memset(xp[:, b, :], 0.0).then_inc(sem("zero"), 1)
            x, e, u, l, w = h[:, 0, :], h[:, 2, :], h[:, 3, :], h[:, 4, :], h[:, 5, :]
            k.did(V.tensor_scalar(x, p[0:16, 24, :], col("dt_bias", 0)[0:16], None, ALU.add))
            dve.wait_ge(sem("e"), 1)
            k.did(V.tensor_scalar(u, e, 1.0, None, ALU.add))
            k.wait()
            k.did(V.tensor_scalar(w, u, 1.0, None, ALU.is_equal))
            k.wait()
            dve.wait_ge(sem("l"), 1)
            k.did(V.tensor_tensor(l, l, w, ALU.add))
            k.did(V.scalar_tensor_tensor(w, u, -1.0, w, ALU.add, ALU.add))
            k.wait()
            k.did(V.reciprocal(w, w))
            k.wait()
            k.did(V.tensor_tensor(l, l, w, ALU.mult))
            k.wait()
            k.did(V.tensor_tensor(l, l, e, ALU.mult))
            k.wait()
            k.did(V.scalar_tensor_tensor(dtla[:, 0, :], x, 0.0, l, ALU.max, ALU.add))
            k.wait()
            dve.wait_ge(sem("na"), 1)
            k.did(V.tensor_scalar(dtla[:, 1, :], dtla[:, 0, :], na[:, 0:1], -1.0, ALU.mult, ALU.mult))
            for i in range(8):
                x, y = xp[:, i % 2, :], acc[:, i % 2, :]
                dve.wait_ge(sem("tap0"), i + 1)
                for tap in range(1, 5):
                    if tap > 1:
                        k.wait()
                    ins = V.scalar_tensor_tensor(y, x[:, tap:tap + OUT], col("conv_w", 8 * tap + i), y,
                                                 ALU.mult, ALU.add)
                    if tap < 4:
                        k.did(ins)
                    else:
                        ins.then_inc(sem("conv"), 1)


def ssd_scan(nc, p, dtla, y, c):
    with ExitStack() as st:
        s = Stage(nc, st, "ss")
        sem = s.sem
        Bs, Cs, Xs = s.sb("Bs", [128, 2, 128]), s.sb("Cs", [128, 2, 128]), s.sb("Xs", [128, 4, 128])
        Ds = s.sb("Ds", [16, 2, 128])
        Bt, dl = s.sb("Bt", [128, 2, 128]), s.sb("dl", [128, 2, 16])
        xdt, xw = s.sb("xdt", [128, 8, 64]), s.sb("xw", [128, 8, 64])
        laU, G, Ce = s.sb("laU", [128, 8, 128]), s.sb("G", [128, 8, 128]), s.sb("Ce", [128, 8, 128])
        CBm, wend = s.sb("CBm", [128, 2, 128]), s.sb("wend", [128, 16])
        H = [s.sb(f"H{d}", [128, 8, 64]) for d in range(2)]
        px, pb, pc = s.ps("px", [128, 4, 128]), s.ps("pb", [128, 512]), s.ps("pc", [128, 512])
        pD, pE = s.ps("pD", [128, 8, 128]), s.ps("pE", [128, 8, 128])
        py = s.ps("py", [128, 4, 128])
        for n in ("zero", "st", "tr", "ev", "xdt", "lau", "sums", "cb", "exps", "cbm", "G", "Ce", "xw",
                  "y", "yr", "state", "hm", "h"):
            sem(n)
        s.seed()
        block = st.enter_context(nc.Block())

        @block.vector
        def _(dve):
            V = nc.vector
            for d in range(2):
                V.memset(H[d][:], 0.0).then_inc(sem("zero"), 1)
            V.memset(y[:, :, :], 0.0).then_inc(sem("zero"), 1)
            dve.wait_ge(sem("zero"), 1 + 3)

            def body(seg, t0, u):
                for d in range(2):
                    v = u * 2 + d
                    view = scan_views(d, seg, t0, CHUNK)
                    heads = slice(8 * d, 8 * d + 8)
                    dve.wait_ge(sem("tr"), 1 + 2 * v + 2)
                    dve.wait_ge(sem("ev"), 1 + 2 * v + 2)
                    dve.wait_ge(sem("state"), 1 + v)
                    V.tensor_tensor(xdt[:], px[:].rearrange("p a (b c) -> p (a b) c", b=2),
                                    bcast(dl[:, 0, heads], 2, 64), ALU.mult).then_inc(sem("xdt"), 1)
                    V.tensor_tensor(laU[:], bcast(c["upper_inc128"], 1, 8), bcast(dl[:, 1, heads], 2, 128),
                                    ALU.mult).then_inc(sem("lau"), 1)
                    dve.wait_ge(sem("cb"), 1 + v + 1)
                    V.tensor_tensor(CBm[:], px[:, 0:2, :],
                                    bcast(c["upper_inc128"], 1, 2), ALU.mult).then_inc(sem("cbm"), 1)
                    dve.wait_ge(sem("exps"), 1 + 3 * v + 3)
                    dve.wait_ge(sem("cbm"), 1 + v + 1)
                    dve.wait_ge(sem("xdt"), 1 + v + 1)
                    g4 = lambda x: x[:].rearrange("p (g r) i -> p g r i", g=2)
                    V.tensor_tensor(g4(G), g4(G), bcast(CBm[:], 2, 4), ALU.mult).then_inc(sem("G"), 1)
                    V.tensor_tensor(g4(Ce), g4(Ce), bcast(Cs[:], 2, 4), ALU.mult).then_inc(sem("Ce"), 1)
                    V.tensor_tensor(xw[:], xdt[:], bcast(wend[:, 0:8], 2, 64), ALU.mult).then_inc(sem("xw"), 1)
                    dve.wait_ge(sem("y"), 1 + v + 1)
                    dve.wait_ge(sem("yr"), 1 + v)
                    yv = view(y, 0, 4)
                    V.tensor_tensor(yv, yv, turned(d, py[:]), ALU.add).then_inc(sem("yr"), 1)
                    V.tensor_tensor(H[d][:], H[d][:], bcast(wend[:, 8:16], 2, 64), ALU.mult).then_inc(sem("hm"), 1)
                    dve.wait_ge(sem("hm"), 1 + v + 1)
                    dve.wait_ge(sem("state"), 1 + v + 1)
                    V.tensor_tensor(H[d][:], H[d][:], pb[:].rearrange("p (h c) -> p h c", h=8), ALU.add)\
                        .then_inc(sem("h"), 1)
            scan_steps(dve, body, CHUNK)

        @block.gpsimd
        def _(pool):
            def body(seg, t0, u):
                for d in range(2):
                    v = u * 2 + d
                    view = scan_views(d, seg, t0, CHUNK)
                    pool.wait_ge(sem("cb"), 1 + v)
                    pool.wait_ge(sem("Ce"), 1 + v)
                    P = nc.gpsimd
                    P.tensor_copy(turned(d, Ds[:]), view(dtla, 0, 2)).then_inc(sem("st"), 1)
                    P.tensor_copy(turned(d, Xs[:]), view(p, 4, 4)).then_inc(sem("st"), 1)
                    P.tensor_copy(turned(d, Bs[:]), view(p, 8, 2)).then_inc(sem("st"), 1)
                    P.tensor_copy(turned(d, Cs[:]), view(p, 10, 2)).then_inc(sem("st"), 1)
            scan_steps(pool, body, CHUNK)

        @block.scalar
        def _(act):
            A = nc.scalar.activation

            def body(seg, t0, u):
                for d in range(2):
                    v = u * 2 + d
                    act.wait_ge(sem("tr"), 1 + 2 * v + 1)
                    act.wait_ge(sem("sums"), 1 + 2 * v)
                    act.wait_ge(sem("lau"), 1 + v)
                    act.wait_ge(sem("xdt"), 1 + v)
                    A(dl[:], pc[:, 256:288].rearrange("p (a b) -> p a b", a=2), ACT.Copy).then_inc(sem("ev"), 1)
                    act.wait_ge(sem("tr"), 1 + 2 * v + 2)
                    act.wait_ge(sem("state"), 1 + v)
                    A(Bt[:], pb[:, 0:256].rearrange("p (a b) -> p a b", a=2), ACT.Copy).then_inc(sem("ev"), 1)
                    act.wait_ge(sem("sums"), 1 + 2 * v + 2)
                    act.wait_ge(sem("hm"), 1 + v)
                    act.wait_ge(sem("xw"), 1 + v)
                    A(wend[:], pc[:, 288:304], ACT.Exp).then_inc(sem("exps"), 1)
                    act.wait_ge(sem("y"), 1 + v)
                    A(G[:], pD[:], ACT.Exp).then_inc(sem("exps"), 1)
                    A(Ce[:], pE[:], ACT.Exp).then_inc(sem("exps"), 1)
            scan_steps(act, body, CHUNK)

        @block.tensor
        def _(pe):
            mm = nc.tensor.matmul
            pe.wait_ge(sem("zero"), 1 + 3)

            def body(seg, t0, u):
                for d in range(2):
                    v = u * 2 + d
                    heads = slice(8 * d, 8 * d + 8)
                    pe.wait_ge(sem("st"), 1 + 4 * v + 4)
                    pe.wait_ge(sem("cbm"), 1 + v)
                    pe.wait_ge(sem("exps"), 1 + 3 * v)
                    pe.wait_ge(sem("xdt"), 1 + v)
                    pe.wait_ge(sem("h"), 1 + v)
                    for a in range(4):
                        nc.tensor.transpose(px[:, a, :], Xs[:, a, :], c["ident"])
                    for a in range(2):
                        ins = nc.tensor.transpose(pc[:, 256 + 16 * a:272 + 16 * a], Ds[:, a, :], c["ident"][0:16, 0:16])
                    ins.then_inc(sem("tr"), 1)
                    for g in range(2):
                        ins = nc.tensor.transpose(pb[:, g * 128:(g + 1) * 128], Bs[:, g, :], c["ident"])
                    ins.then_inc(sem("tr"), 1)
                    pe.wait_ge(sem("ev"), 1 + 2 * v + 1)
                    mm(pc[:, 288:296], c["lower128"], dl[:, 1, heads], start=True, stop=True)
                    mm(pc[:, 296:304], c["ones"], dl[:, 1, heads], start=True, stop=True).then_inc(sem("sums"), 1)
                    pe.wait_ge(sem("lau"), 1 + v + 1)
                    for g in range(2):
                        mm(pD[:, 4 * g:4 * g + 4, :], c["lower128"], laU[:, 4 * g:4 * g + 4, :], start=True, stop=True)
                        ins = mm(pE[:, 4 * g:4 * g + 4, :], c["ones"], laU[:, 4 * g:4 * g + 4, :], start=True, stop=True)
                    ins.then_inc(sem("sums"), 1)
                    pe.wait_ge(sem("xdt"), 1 + v + 1)
                    for g in range(2):
                        ins = mm(px[:, g, :], Bs[:, g, :], Cs[:, g, :], start=True, stop=True)
                    ins.then_inc(sem("cb"), 1)
                    pe.wait_ge(sem("G"), 1 + v + 1)
                    pe.wait_ge(sem("Ce"), 1 + v + 1)
                    pe.wait_ge(sem("yr"), 1 + v)
                    for h in range(8):
                        o = py[64 * (h % 2):64 * (h % 2) + 64, h // 2, :]
                        mm(o, xdt[:, h, :], G[:, h, :], start=True, stop=False)
                        ins = mm(o, H[d][:, h, :], Ce[:, h, :], start=False, stop=True)
                    ins.then_inc(sem("y"), 1)
                    pe.wait_ge(sem("xw"), 1 + v + 1)
                    pe.wait_ge(sem("ev"), 1 + 2 * v + 2)
                    for g in range(2):
                        ins = mm(pb[:, g * 256:(g + 1) * 256], Bt[:, g, :], xw[:, 4 * g:4 * g + 4, :],
                                 start=True, stop=True)
                    ins.then_inc(sem("state"), 1)
            scan_steps(pe, body, CHUNK)


def gla_prepare(nc, p, sp, col, w_up, c):
    with ExitStack() as st:
        s = Stage(nc, st, "gp")
        sem = s.sem
        up = s.sb("up", [128, 512])
        za, zb, zc = s.sb("za", [128, T]), s.sb("zb", [128, T]), s.sb("zc", [128, T])
        acc = s.ps("acc", [128, 1024])
        for n in ("up", "z", "x", "abs", "e", "l", "sp", "scan"):
            sem(n)
        block = st.enter_context(nc.Block())

        @block.sync
        def _(sync):
            sync.dma_start(up[32:48, :], w_up).then_inc(sem("up"), 16)

        @block.tensor
        def _(pe):
            pe.wait_ge(sem("up"), 16)
            for i in range(4):
                pe.wait_ge(sem("x"), i)
                for t0, tn in ((0, 512), (512, 256)):
                    ins = nc.tensor.matmul(acc[:, t0:t0 + tn], up[32:48, 128 * i:128 * i + 128],
                                           p[32:48, 24, t0:t0 + tn], start=True, stop=True)
                ins.then_inc(sem("z"), 1)

        @block.scalar
        def _(act):
            A = nc.scalar.activation
            for i in range(4):
                act.wait_ge(sem("x"), i + 1)
                act.wait_ge(sem("sp"), i)
                A(zb[:, :], za[:, :], ACT.Abs).then_inc(sem("abs"), 1)
                act.wait_ge(sem("abs"), i + 1)
                A(zb[:, :], zb[:, :], ACT.Exp, scale=-1.0).then_inc(sem("e"), 1)
                act.wait_ge(sem("e"), i + 1)
                A(zc[:, :], zb[:, :], ACT.Ln, bias=1.0).then_inc(sem("l"), 1)

        @block.vector
        def _(dve):
            V = nc.vector
            for i in range(4):
                dve.wait_ge(sem("z"), i + 1)
                dve.wait_ge(sem("sp"), i)
                V.tensor_scalar(za[:, :], acc[:, 0:T], col("gk_b", i), -1.0, ALU.add, ALU.mult)\
                    .then_inc(sem("x"), 1)
                dve.wait_ge(sem("l"), i + 1)
                V.scalar_tensor_tensor(sp[:, i, :], za[:, :], 0.0, zc[:, :], ALU.max, ALU.add)\
                    .then_inc(sem("sp"), 1)
                dve.wait_ge(sem("sp"), i + 1)
                x = sp[:, i, :] if i < 2 else sp[:, i, ::-1]
                V.tensor_tensor_scan(x, c["chunk_mask128"], x, 0.0, ALU.mult, ALU.add).then_inc(sem("scan"), 1)


def gla_scan(nc, p, sp, y, c):
    LEV = 7
    with ExitStack() as st:
        s = Stage(nc, st, "gs")
        sem = s.sem
        Ps = s.sb("Ps", [128, 2, 128])
        qk = [s.sb("qs", [128, 2, 128]), s.sb("ks", [128, 2, 128])]
        Vs, Vt = s.sb("Vs", [128, 4, 128]), s.sb("Vt", [128, 4, 128])
        Dl = s.sb("Dl", [128, LEV, 256])
        QL, KL = s.sb("QL", [128, LEV, 256]), s.sb("KL", [128, LEV, 256])
        ew = s.sb("ew", [128, 2, 256])
        qe, ke = s.sb("qe", [128, 2, 128]), s.sb("ke", [128, 2, 128])
        pend = s.sb("pend", [128, 2])
        kt = s.sb("kt", [128, 2, 128])
        tick = s.sb("tick", [128, 1])
        att = s.sb("att", [128, 2, 2, 128])
        S = [s.sb(f"S{d}", [128, 2, 128]) for d in range(2)]
        pv, pk_ = s.ps("pv", [128, 4, 128]), s.ps("pk", [128, 4, 128])
        pS = pk_[:, 2:4, :]
        py = s.ps("py", [128, 2, 4, 128])
        pl = [s.ps(f"pl{i}", [128, 2, 4, 128]) for i in range(2)]
        for n in ("zero", "ps", "qk", "vs", "dl", "abs", "el", "ql", "kl", "ds", "ew", "pend", "qe", "ke", "trv",
                  "trk", "vt", "kt", "lev", "att", "y", "yr", "state", "sm", "snew"):
            sem(n)
        s.seed()
        block = st.enter_context(nc.Block())
        LV = LEV + 1

        @block.gpsimd
        def _(pool):
            P = nc.gpsimd

            def body(seg, t0, u):
                for d in range(2):
                    v = u * 2 + d
                    view = scan_views(d, seg, t0, CHUNK)
                    pool.wait_ge(sem("trv"), 1 + v)
                    P.tensor_copy(turned(d, Vs[:]), view(p, 16, 4)).then_inc(sem("vs"), 1)
                    pool.wait_ge(sem("el"), 1 + v + 1)
                    pool.wait_ge(sem("qk"), 1 + 2 * v + 2)
                    pool.wait_ge(sem("lev"), 1 + LV * v)
                    P.tensor_tensor(KL[:], bcast(qk[1][:].rearrange("p a t -> p (a t)"), 1, LEV), Dl[:], ALU.mult)\
                        .then_inc(sem("kl"), 1)
            scan_steps(pool, body, CHUNK)

        @block.scalar
        def _(act):
            A = nc.scalar.activation

            def body(seg, t0, u):
                for d in range(2):
                    v = u * 2 + d
                    view = scan_views(d, seg, t0, CHUNK)
                    act.wait_ge(sem("ds"), 1 + v)
                    act.wait_ge(sem("pend"), 1 + v)
                    act.wait_ge(sem("ew"), 1 + v)
                    A(turned(d, Ps[:]), view(sp, 2 * d, 2), ACT.Copy).then_inc(sem("ps"), 1)
                    act.wait_ge(sem("lev"), 1 + LV * v)
                    act.wait_ge(sem("ql"), 1 + v)
                    act.wait_ge(sem("kl"), 1 + v)
                    act.wait_ge(sem("ke"), 1 + v)
                    A(turned(d, qk[0][:]), view(p, 12, 2), ACT.Copy, scale=0.125).then_inc(sem("qk"), 1)
                    A(turned(d, qk[1][:]), view(p, 14, 2), ACT.Copy).then_inc(sem("qk"), 1)
                    act.wait_ge(sem("dl"), 1 + LEV * (v + 1))
                    A(Dl[:], Dl[:], ACT.Abs).then_inc(sem("abs"), 1)
                    act.wait_ge(sem("ds"), 1 + v + 1)
                    act.wait_ge(sem("ps"), 1 + v + 1)
                    A(ew[:, 0, :], Ps[:].rearrange("p a t -> p (a t)"), ACT.Exp, scale=-1 / 16)
                    act.wait_ge(sem("sm"), 1 + v)
                    A(pend[:, :], Ps[:, :, 127], ACT.Exp, scale=-1 / 16).then_inc(sem("pend"), 1)
                    A(ew[:, 1, :], ew[:, 1, :], ACT.Exp, scale=-1 / 16).then_inc(sem("ew"), 1)
                    act.wait_ge(sem("abs"), 1 + v + 1)
                    A(Dl[:], Dl[:], ACT.Exp, scale=-1 / 16).then_inc(sem("el"), 1)
                    act.wait_ge(sem("trv"), 1 + v + 1)
                    act.wait_ge(sem("state"), 1 + v)
                    A(Vt[:], pv[:], ACT.Copy).then_inc(sem("vt"), 1)
                    act.wait_ge(sem("trk"), 1 + v + 1)
                    A(kt[:], pk_[:, 0:2, :], ACT.Copy).then_inc(sem("kt"), 1)
            scan_steps(act, body, CHUNK)

        @block.vector
        def _(dve):
            V = nc.vector
            for d in range(2):
                V.memset(S[d][:], 0.0).then_inc(sem("zero"), 1)
            V.memset(y[:, :, :], 0.0).then_inc(sem("zero"), 1)
            V.memset(att[:], 0.0).then_inc(sem("zero"), 1)
            dve.wait_ge(sem("zero"), 1 + 4)
            flat = lambda x: x[:].rearrange("p a t -> p (a t)")

            def body(seg, t0, u):
                for d in range(2):
                    v = u * 2 + d
                    view = scan_views(d, seg, t0, CHUNK)
                    dve.wait_ge(sem("ps"), 1 + v + 1)
                    dve.wait_ge(sem("kl"), 1 + v)
                    dve.wait_ge(sem("ql"), 1 + v)
                    for l in range(LEV):
                        b = 1 << l
                        blocks = flat(Ps).rearrange("p (n w) -> p n w", w=2 * b)
                        V.tensor_tensor(Dl[:, l, :].rearrange("p (n w) -> p n w", w=2 * b), blocks,
                                        bcast(blocks[:, :, b - 1], 2, 2 * b), ALU.subtract).then_inc(sem("dl"), 1)
                    dve.wait_ge(sem("ke"), 1 + v)
                    V.tensor_tensor(ew[:, 1, :].rearrange("p (a t) -> p a t", a=2), bcast(Ps[:, :, 127], 2, 128), Ps[:],
                                    ALU.subtract).then_inc(sem("ds"), 1)
                    dve.wait_ge(sem("el"), 1 + v + 1)
                    dve.wait_ge(sem("qk"), 1 + 2 * v + 2)
                    dve.wait_ge(sem("lev"), 1 + LV * v)
                    V.tensor_tensor(QL[:], bcast(flat(qk[0]), 1, LEV), Dl[:], ALU.mult).then_inc(sem("ql"), 1)
                    dve.wait_ge(sem("ew"), 1 + v + 1)
                    dve.wait_ge(sem("y"), 1 + v)
                    dve.wait_ge(sem("trk"), 1 + v)
                    V.tensor_tensor(flat(qe), flat(qk[0]), ew[:, 0, :], ALU.mult).then_inc(sem("qe"), 1)
                    V.tensor_tensor(flat(ke), flat(qk[1]), ew[:, 1, :], ALU.mult).then_inc(sem("ke"), 1)
                    for l in range(LV):
                        dve.wait_ge(sem("lev"), 1 + LV * v + l + 1)
                        dve.wait_ge(sem("att"), 1 + LV * v + l)
                        V.memset(tick[:, :], 0.0)
                        V.copy_predicated(att[:], bcast(bcast(c["pair_level"][:, l, :], 1, 2), 1, 2)
                                          .bitcast(mybir.dt.int32), pl[l % 2][:, :, 0:2, :]).then_inc(sem("att"), 1)
                    dve.wait_ge(sem("y"), 1 + v + 1)
                    dve.wait_ge(sem("yr"), 1 + v)
                    yv = view(y, 0, 4).rearrange("p (t b) i -> p b t i", b=2)
                    V.tensor_tensor(yv, yv, turned(d, py[:, :, 0:2, :]), ALU.add).then_inc(sem("yr"), 1)
                    dve.wait_ge(sem("pend"), 1 + v + 1)
                    V.tensor_tensor(S[d][:], S[d][:], bcast(pend[:, :], 2, 128), ALU.mult).then_inc(sem("sm"), 1)
                    dve.wait_ge(sem("sm"), 1 + v + 1)
                    dve.wait_ge(sem("state"), 1 + v + 1)
                    V.tensor_tensor(S[d][:], S[d][:], pS, ALU.add).then_inc(sem("snew"), 1)
            scan_steps(dve, body, CHUNK)

        @block.tensor
        def _(pe):
            mm = nc.tensor.matmul
            pe.wait_ge(sem("zero"), 1 + 4)

            def body(seg, t0, u):
                for d in range(2):
                    v = u * 2 + d
                    pe.wait_ge(sem("vs"), 1 + v + 1)
                    pe.wait_ge(sem("vt"), 1 + v)
                    for h in range(4):
                        ins = nc.tensor.transpose(pv[:, h, :], Vs[:, h, :], c["ident"])
                    ins.then_inc(sem("trv"), 1)
                    for l in range(LV):
                        if l == 0:
                            pe.wait_ge(sem("qk"), 1 + 2 * v + 2)
                            pe.wait_ge(sem("att"), 1 + LV * v)
                        elif l == 1:
                            pe.wait_ge(sem("ql"), 1 + v + 1)
                            pe.wait_ge(sem("kl"), 1 + v + 1)
                        if l >= 2:
                            pe.wait_ge(sem("att"), 1 + LV * v + l - 1)
                        for h in range(4):
                            rows, t = slice(64 * (h % 2), 64 * (h % 2) + 64), h // 2
                            if l == 0:
                                k, q = qk[1][rows, t, :], qk[0][rows, t, :]
                            else:
                                cols = slice(128 * t, 128 * t + 128)
                                k, q = KL[rows, l - 1, cols], QL[rows, l - 1, cols]
                            ins = mm(pl[l % 2][:, h % 2, t, :], k, q, start=True, stop=True)
                        ins.then_inc(sem("lev"), 1)
                    pe.wait_ge(sem("ke"), 1 + v + 1)
                    pe.wait_ge(sem("snew"), 1 + v)
                    for t in range(2):
                        ins = nc.tensor.transpose(pk_[:, t, :], ke[:, t, :], c["ident"])
                    ins.then_inc(sem("trk"), 1)
                    pe.wait_ge(sem("snew"), 1 + v)
                    pe.wait_ge(sem("qe"), 1 + v + 1)
                    pe.wait_ge(sem("vt"), 1 + v + 1)
                    pe.wait_ge(sem("att"), 1 + LV * (v + 1))
                    pe.wait_ge(sem("yr"), 1 + v)
                    for h in range(4):
                        rows, t = slice(64 * (h % 2), 64 * (h % 2) + 64), h // 2
                        mm(py[:, h % 2, t, :], Vt[:, h, :], att[:, h % 2, t, :], start=True, stop=False)
                        ins = mm(py[:, h % 2, t, :], S[d][rows, t, :], qe[rows, t, :], start=False, stop=True)
                    ins.then_inc(sem("y"), 1)
                    pe.wait_ge(sem("kt"), 1 + v + 1)
                    for h in range(4):
                        rows, t = slice(64 * (h % 2), 64 * (h % 2) + 64), h // 2
                        ins = mm(pS[rows, t, :], kt[:, t, rows], Vt[:, h, :], start=True, stop=True)
                    ins.then_inc(sem("state"), 1)
            scan_steps(pe, body, CHUNK)


def chunk_masks():
    j, i = np.arange(128)[:, None], np.arange(128)[None, :]
    m = {"upper_inc128": j <= i, "lower128": j > i, "pair0": j == i}
    for l in range(7):
        b = 2 << l
        m[f"pair{l + 1}"] = (i // b == j // b) & (j % b < b // 2) & (i % b >= b // 2)
    return m


KEYS = T // 128
LAM_INIT = 0.8 - 0.6 * math.exp(-0.3 * 0)


def rope(nc, p, w_rope, c):
    with ExitStack() as st:
        s = Stage(nc, st, "ro")
        sem = s.sem
        tab = s.sb("tab", [128, 2, LAT])
        tmp = s.sb("tmp", [128, 2, LAT])
        acc = [s.ps(f"acc{i}", [128, LAT]) for i in range(2)]
        for n in ("tab", "rot", "sin", "cos", "done"):
            sem(n)
        block = st.enter_context(nc.Block())

        @block.sync
        def _(sp):
            sp.dma_start(tab[:], w_rope).then_inc(sem("tab"), 16)

        @block.tensor
        def _(pe):
            for i in range(8):
                if i >= 2:
                    pe.wait_ge(sem("sin"), i - 1)
                nc.tensor.matmul(acc[i % 2][:, :], c["rot"], p[:, i, CTX:T], start=True, stop=True)\
                    .then_inc(sem("rot"), 1)

        @block.vector
        def _(dve):
            dve.wait_ge(sem("tab"), 16)
            for i in range(8):
                x, y = p[:, i, CTX:T], tmp[:, i % 2, :]
                dve.wait_ge(sem("rot"), i + 1)
                if i >= 2:
                    dve.wait_ge(sem("done"), i - 1)
                nc.vector.tensor_tensor(y, acc[i % 2][:, :], tab[:, 1, :], ALU.mult).then_inc(sem("sin"), 1)
                nc.vector.tensor_tensor(x, x, tab[:, 0, :], ALU.mult).then_inc(sem("cos"), 1)
                dve.wait_ge(sem("sin"), i + 1)
                dve.wait_ge(sem("cos"), i + 1)
                nc.vector.tensor_tensor(x, x, y, ALU.add).then_inc(sem("done"), 1)


def diff_attention(nc, p, out, w_lam, c):
    HEADS = 4
    with ExitStack() as st:
        s = Stage(nc, st, "da")
        sem = s.sem
        lam, prod, elam, neglam = s.sb("lam", [64, 4]), s.sb("prod", [64, 2]), s.sb("elam", [128, 2]), s.sb("neglam", [128, 1])
        vt = s.sb("vt", [128, KEYS, 4, 128])
        qm = s.sb("qm", [128, HEADS, 2, 128])
        mx, nb = s.sb("mx", [128, 2]), s.sb("nb", [128, 2])
        P, W = s.sb("P", [128, 2, 2, T]), s.sb("W", [128, 2, T])
        rs, rr = s.sb("rs", [128, 2, 2]), s.sb("rr", [128, 2])
        WT = s.sb("WT", [128, KEYS, 128])
        score = s.ps("score", [128, 2, 1024])
        pt = s.ps("pt", [128, 8, 128])
        po = s.ps("po", [128, HEADS, 128])
        for n in ("lam", "prod", "plam", "elam", "neglam", "vtr", "vt", "q", "s", "mx", "nb", "exp", "rr0",
                  "rr", "w0", "w", "tr", "wt", "o", "or"):
            sem(n)
        s.seed()
        block = st.enter_context(nc.Block())

        def runs(engine, body):
            for base, n, keys, u0 in ((0, CTX, CTX // 128, 0), (CTX, LAT, KEYS, CTX // 128)):
                with engine.Fori(0, n // 128) as i:
                    body(base, i * 128, keys, (i + u0) * HEADS, i + u0)

        @block.sync
        def _(sp):
            sp.dma_start(lam[:, :], w_lam).then_inc(sem("lam"), 16)

        @block.gpsimd
        def _(pool):
            def body(base, t0, keys, u, r):
                pool.wait_ge(sem("elam"), 1 + 1)
                pool.wait_ge(sem("s"), 1 + u)
                q = p[:, 0:HEADS, base:T][:, :, bass.ds(t0, 128)]
                for m in range(2):
                    nc.gpsimd.tensor_tensor(qm[:, :, m, :], q, bcast(bcast(c["halves"][:, m], 1, HEADS), 2, 128),
                                            ALU.mult).then_inc(sem("q"), 1)
            runs(pool, body)

        @block.tensor
        def _(pe):
            mm = nc.tensor.matmul
            pe.wait_ge(sem("prod"), 1 + 1)
            mm(po[:, 0, 0:2], c["ones"][0:64, :], prod[:, :], start=True, stop=True).then_inc(sem("plam"), 1)
            for k in range(KEYS):
                if k >= 2:
                    pe.wait_ge(sem("vt"), 1 + k - 1)
                for h in range(4):
                    ins = nc.tensor.transpose(pt[:, 4 * (k % 2) + h, :], p[:, 8 + h, 128 * k:128 * k + 128], c["ident"])
                ins.then_inc(sem("vtr"), 1)
            pe.wait_ge(sem("vt"), 1 + KEYS)
            pe.wait_ge(sem("elam"), 1 + 1)

            def scores(base, t0, keys, u, r, h):
                if h == 0:
                    pe.wait_ge(sem("q"), 1 + 2 * r + 2)
                pe.wait_ge(sem("exp"), 1 + 2 * (u + h))
                for m in range(2):
                    for k0 in range(0, keys * 128, 512):
                        kn = min(512, keys * 128 - k0)
                        ins = mm(score[:, m, k0:k0 + kn], qm[:, h, m, :], p[:, 4 + h, k0:k0 + kn], start=True, stop=True)
                ins.then_inc(sem("s"), 1)

            def apply(base, t0, keys, u, r, h):
                pe.wait_ge(sem("w"), 1 + u + h + 1)
                pe.wait_ge(sem("wt"), 1 + u + h)
                for k in range(keys):
                    ins = nc.tensor.transpose(pt[:, k, :], W[:, h % 2, 128 * k:128 * k + 128], c["ident"])
                ins.then_inc(sem("tr"), 1)
                pe.wait_ge(sem("wt"), 1 + u + h + 1)
                if h == 0:
                    pe.wait_ge(sem("or"), 1 + r)
                for k in range(keys):
                    ins = mm(po[:, h, :], vt[:, k, h, :], WT[:, k, :], start=(k == 0), stop=(k == keys - 1))
                ins.then_inc(sem("o"), 1)

            def body(*a):
                scores(*a, 0)
                for h in range(1, HEADS):
                    scores(*a, h)
                    apply(*a, h - 1)
                apply(*a, HEADS - 1)
            runs(pe, body)

        @block.vector
        def _(dve):
            V = nc.vector
            dve.wait_ge(sem("lam"), 1 + 16)
            V.tensor_tensor(prod[:, :], lam[:, 0:2], lam[:, 2:4], ALU.mult).then_inc(sem("prod"), 1)
            dve.wait_ge(sem("elam"), 1 + 1)
            V.scalar_tensor_tensor(neglam[:, :], elam[:, 1:2], -LAM_INIT, elam[:, 0:1], ALU.add, ALU.subtract)\
                .then_inc(sem("neglam"), 1)
            dve.wait_ge(sem("neglam"), 1 + 1)

            def body(base, t0, keys, u, r):
                for h in range(HEADS):
                    n = keys * 128
                    g = u + h
                    dve.wait_ge(sem("s"), 1 + g + 1)
                    dve.wait_ge(sem("nb"), 1 + g)
                    V.tensor_reduce(mx[:, :], score[:, :, 0:n], AX.X, ALU.max, negate=True).then_inc(sem("mx"), 1)
                    dve.wait_ge(sem("mx"), 1 + g + 1)
                    dve.wait_ge(sem("exp"), 1 + 2 * g)
                    V.tensor_scalar(nb[:, :], mx[:, :], 0.125, None, ALU.mult).then_inc(sem("nb"), 1)
                    dve.wait_ge(sem("exp"), 1 + 2 * g + 2)
                    dve.wait_ge(sem("w"), 1 + g)
                    V.reciprocal(rr[:, :], rs[:, h % 2, :]).then_inc(sem("rr0"), 1)
                    dve.wait_ge(sem("rr0"), 1 + g + 1)
                    V.tensor_tensor(rr[:, 1:2], rr[:, 1:2], neglam[:, :], ALU.mult).then_inc(sem("rr"), 1)
                    if h < 2:
                        dve.wait_ge(sem("tr"), 1 + u)
                    else:
                        dve.wait_ge(sem("tr"), 1 + u + h - 1)
                    V.tensor_scalar(W[:, h % 2, 0:n], P[:, h % 2, 0, 0:n], rr[:, 0:1], None, ALU.mult).then_inc(sem("w0"), 1)
                    dve.wait_ge(sem("rr"), 1 + g + 1)
                    dve.wait_ge(sem("w0"), 1 + g + 1)
                    V.scalar_tensor_tensor(W[:, h % 2, 0:n], P[:, h % 2, 1, 0:n], rr[:, 1:2], W[:, h % 2, 0:n],
                                           ALU.mult, ALU.add).then_inc(sem("w"), 1)
            runs(dve, body)

        @block.scalar
        def _(act):
            A = nc.scalar.activation
            act.wait_ge(sem("plam"), 1 + 1)
            A(elam[:, :], po[:, 0, 0:2], ACT.Exp).then_inc(sem("elam"), 1)
            for k in range(KEYS):
                act.wait_ge(sem("vtr"), 1 + k + 1)
                A(vt[:, k], pt[:, 4 * (k % 2):4 * (k % 2) + 4, :], ACT.Copy).then_inc(sem("vt"), 1)

            def exps(base, t0, keys, u, r, h):
                n = keys * 128
                act.wait_ge(sem("nb"), 1 + u + h + 1)
                if h < 2:
                    act.wait_ge(sem("w"), 1 + u)
                else:
                    act.wait_ge(sem("w"), 1 + u + h - 1)
                for m in range(2):
                    A(P[:, h % 2, m, 0:n], score[:, m, 0:n], ACT.Exp, scale=0.125, bias=nb[:, m:m + 1],
                      accum_out=rs[:, h % 2, m:m + 1]).then_inc(sem("exp"), 1)

            def turned(base, t0, keys, u, r, h):
                act.wait_ge(sem("tr"), 1 + u + h + 1)
                act.wait_ge(sem("o"), 1 + u + h)
                A(WT[:, 0:keys, :], pt[:, 0:keys, :], ACT.Copy).then_inc(sem("wt"), 1)

            def body(base, t0, keys, u, r):
                a = (base, t0, keys, u, r)
                exps(*a, 0)
                for h in range(1, HEADS):
                    exps(*a, h)
                    turned(*a, h - 1)
                turned(*a, HEADS - 1)
                act.wait_ge(sem("o"), 1 + u + HEADS)
                A(out[:, 0:HEADS, base:T][:, :, bass.ds(t0, 128)], po[:], ACT.Copy).then_inc(sem("or"), 1)
            runs(act, body)


def rms(nc, name, src, dst, groups, parts, ones, n, eps, gain, shift=None, gate=None, silu_src=None):
    tn_max = max(tn for _, tn in parts)
    with ExitStack() as st:
        s = Stage(nc, st, name)
        sem = s.sem
        sq = s.sb("sq", [128, 2, tn_max])
        r = s.sb("r", [128, 2, tn_max])
        act_g = s.sb("gt", [128, 2, tn_max]) if silu_src is not None else None
        acc = [s.ps(f"acc{i}", [128, 512]) for i in range(2)]
        for k in ("sq", "sum", "root", "inv", "out", "shifted", "silu", "gated"):
            sem(k)
        work = [(g, p) for g in range(len(groups)) for p in range(len(parts))]
        order, i = [], 0
        for w, (g, p) in enumerate(work):
            for k, tile in enumerate(groups[g]):
                order.append((i, w, k, tile, len(groups[g]), parts[p], p))
                i += 1
        block = st.enter_context(nc.Block())
        last = lambda w: max(o[0] for o in order if o[1] == w)

        @block.scalar
        def _(act):
            for i, w, k, tile, m, (t0, tn), p in order:
                if i >= 2:
                    act.wait_ge(sem("sum"), i - 1)
                nc.scalar.activation(sq[:, i % 2, 0:tn], src(tile, t0, tn), ACT.Square).then_inc(sem("sq"), 1)
                if k == m - 1:
                    act.wait_ge(sem("sum"), i + 1)
                    if w >= 2:
                        act.wait_ge(sem("out"), last(w - 2) + 1)
                    nc.scalar.activation(r[:, w % 2, 0:tn], acc[w % 2][:, 0:tn], ACT.Sqrt, scale=1.0 / n,
                                         bias=eps).then_inc(sem("root"), 1)
            if shift is not None:
                for i, w, k, tile, m, (t0, tn), p in order:
                    act.wait_ge(sem("out"), i + 1)
                    d = dst(tile, t0, tn)
                    nc.scalar.activation(d, d, ACT.Identity, bias=shift(tile, p)).then_inc(sem("shifted"), 1)
            if silu_src is not None:
                for i, w, k, tile, m, (t0, tn), p in order:
                    if i >= 2:
                        act.wait_ge(sem("gated"), i - 1)
                    nc.scalar.activation(act_g[:, i % 2, 0:tn], silu_src(tile, t0, tn), ACT.Silu).then_inc(sem("silu"), 1)

        @block.tensor
        def _(pe):
            for i, w, k, tile, m, (t0, tn), p in order:
                pe.wait_ge(sem("sq"), i + 1)
                if k == 0 and w >= 2:
                    pe.wait_ge(sem("root"), w - 1)
                nc.tensor.matmul(acc[w % 2][:, 0:tn], ones, sq[:, i % 2, 0:tn], start=(k == 0), stop=(k == m - 1))\
                    .then_inc(sem("sum"), 1)

        @block.vector
        def _(dve):
            for i, w, k, tile, m, (t0, tn), p in order:
                if k == 0:
                    dve.wait_ge(sem("root"), w + 1)
                    rr = r[:, w % 2, 0:tn]
                    nc.vector.reciprocal(rr, rr).then_inc(sem("inv"), 1)
                    dve.wait_ge(sem("inv"), w + 1)
                nc.vector.scalar_tensor_tensor(dst(tile, t0, tn), src(tile, t0, tn), gain(tile, p), r[:, w % 2, 0:tn],
                                               ALU.mult, ALU.mult).then_inc(sem("out"), 1)
            if silu_src is not None:
                for i, w, k, tile, m, (t0, tn), p in order:
                    dve.wait_ge(sem("silu"), i + 1)
                    dve.wait_ge(sem("out"), i + 1)
                    d = dst(tile, t0, tn)
                    nc.vector.tensor_tensor(d, d, act_g[:, i % 2, 0:tn], ALU.mult).then_inc(sem("gated"), 1)


def rwkv_finish(nc, p, y, col, w_gate, c, eps):
    H = ((0, 512), (512, 256))
    with ExitStack() as st:
        s = Stage(nc, st, "rf")
        sem = s.sem
        g2 = s.sb("g2", [128, 512])
        rk, sq, r, bo = (s.sb(n, [128, T]) for n in ("rk", "sq", "r", "bo"))
        pm, pq, pb, pg = (s.ps(n, [128, 1024]) for n in ("pm", "pq", "pb", "pg"))
        for n in ("g2", "sg", "mean", "cen", "sq", "var", "root", "inv", "ln", "rk", "bsum", "bo", "sum", "gate", "out"):
            sem(n)
        block = st.enter_context(nc.Block())

        @block.sync
        def _(sp):
            sp.dma_start(g2[:, :], w_gate).then_inc(sem("g2"), 16)

        @block.tensor
        def _(pe):
            def over(bank, lhs, rhs, name):
                for t0, tn in H:
                    ins = nc.tensor.matmul(bank[:, t0:t0 + tn], lhs, rhs[:, t0:t0 + tn], start=True, stop=True)
                ins.then_inc(sem(name), 1)
            pe.wait_ge(sem("g2"), 16)
            pe.wait_ge(sem("sg"), 1)
            for t in range(4):
                pe.wait_ge(sem("cen"), t)
                over(pm, c["head_ones"], y[:, t, :], "mean")
                pe.wait_ge(sem("rk"), t + 1)
                pe.wait_ge(sem("bo"), t)
                over(pb, c["head_ones"], rk, "bsum")
                pe.wait_ge(sem("out"), t)
                over(pg, g2[:, 128 * t:128 * t + 128], p[:, 25, :], "gate")
                pe.wait_ge(sem("sq"), t + 1)
                pe.wait_ge(sem("root"), t)
                over(pq, c["head_ones"], sq, "var")

        @block.scalar
        def _(act):
            A = nc.scalar.activation
            A(p[:, 25, :], p[:, 25, :], ACT.Sigmoid).then_inc(sem("sg"), 1)
            for t in range(4):
                act.wait_ge(sem("cen"), t + 1)
                A(sq[:, :], y[:, t, :], ACT.Square).then_inc(sem("sq"), 1)
                act.wait_ge(sem("var"), t + 1)
                act.wait_ge(sem("ln"), t)
                A(r[:, :], pq[:, 0:T], ACT.Sqrt, scale=1.0 / 64, bias=eps).then_inc(sem("root"), 1)

        @block.vector
        def _(dve):
            V = nc.vector
            for t in range(4):
                yt = y[:, t, :]
                dve.wait_ge(sem("bsum"), t)
                V.scalar_tensor_tensor(rk[:, :], p[:, 12 + t, :], col("r_k", t), p[:, 16 + t, :], ALU.mult, ALU.mult)\
                    .then_inc(sem("rk"), 1)
                dve.wait_ge(sem("mean"), t + 1)
                V.scalar_tensor_tensor(yt, pm[:, 0:T], -1.0 / 64, yt, ALU.mult, ALU.add).then_inc(sem("cen"), 1)
                dve.wait_ge(sem("bsum"), t + 1)
                dve.wait_ge(sem("sum"), t)
                V.tensor_tensor(bo[:, :], pb[:, 0:T], p[:, 20 + t, :], ALU.mult).then_inc(sem("bo"), 1)
                dve.wait_ge(sem("root"), t + 1)
                V.reciprocal(r[:, :], r[:, :]).then_inc(sem("inv"), 1)
                dve.wait_ge(sem("inv"), t + 1)
                dve.wait_ge(sem("cen"), t + 1)
                V.scalar_tensor_tensor(yt, yt, col("lnx_w", t), r[:, :], ALU.mult, ALU.mult).then_inc(sem("ln"), 1)
                dve.wait_ge(sem("ln"), t + 1)
                dve.wait_ge(sem("bo"), t + 1)
                V.scalar_tensor_tensor(yt, yt, col("lnx_b", t), bo[:, :], ALU.add, ALU.add).then_inc(sem("sum"), 1)
                dve.wait_ge(sem("sum"), t + 1)
                dve.wait_ge(sem("gate"), t + 1)
                V.tensor_tensor(yt, yt, pg[:, 0:T], ALU.mult).then_inc(sem("out"), 1)


def ssd_finish(nc, p, y, col):
    with ExitStack() as st:
        s = Stage(nc, st, "sf")
        sem = s.sem
        sz = s.sb("sz", [128, 4, LAT])
        sem("silu"), sem("skip")
        block = st.enter_context(nc.Block())

        @block.scalar
        def _(act):
            for t in range(4):
                nc.scalar.activation(sz[:, t, :], p[:, t, CTX:T], ACT.Silu).then_inc(sem("silu"), 1)

        @block.vector
        def _(dve):
            for t in range(4):
                yt = y[:, t, CTX:T]
                nc.vector.scalar_tensor_tensor(yt, p[:, 4 + t, CTX:T], col("d_skip", t), yt, ALU.mult, ALU.add)\
                    .then_inc(sem("skip"), 1)
                dve.wait_ge(sem("skip"), 2 * t + 1)
                dve.wait_ge(sem("silu"), t + 1)
                nc.vector.tensor_tensor(yt, yt, sz[:, t, :], ALU.mult).then_inc(sem("skip"), 1)


GROUPS = ((128, 1), (512, 4), (2048, 16))
SLOTS = 4


def dilated_attention(nc, name, p, out, w_slope, w_dist, c):
    NB = LAT // 128
    near = [2, NB, NB]
    with ExitStack() as st:
        s = Stage(nc, st, name)
        sem = s.sem
        slope, dist = s.sb("slope", [128, 12]), s.sb("dist", [128, sum(near), 128])
        vt = s.sb("vt", [128, NB, 768])
        qm = s.sb("qm", [128, 2, 3, 128])
        S = s.sb("S", [128, 2, sum(near) * 128])
        PT = s.sb("PT", [128, sum(near), 128])
        mx, rs, ri = s.sb("mx", [128, 1]), s.sb("rs", [128, 2]), s.sb("ri", [128, 1])
        o = s.sb("o", [128, 2, 2, 128])
        score = s.ps("score", [128, 3, 512])
        pt = s.ps("pt", [128, 12, 128])
        po, pf = s.ps("po", [128, 512]), s.ps("pf", [128, 4, 128])
        for n in ("c", "vtr", "vt", "q", "s", "bias", "mx", "exp", "tr", "pt", "o", "ri", "or", "fin", "out"):
            sem(n)
        s.seed()
        block = st.enter_context(nc.Block())
        widths = lambda i: [min(i + 1, m) for m in near]

        def units(engine, body, after=None):
            for i in range(NB):
                with engine.Fori(0, 2) as pair:
                    for par in range(2):
                        body(i, pair, par, pair * 2 + (4 * i + par), pair + 2 * i)
                if after:
                    after(i)

        @block.sync
        def _(sp):
            sp.dma_start(slope[:, :], w_slope).then_inc(sem("c"), 16)
            sp.dma_start(dist[:], w_dist).then_inc(sem("c"), 16)

        @block.tensor
        def _(pe):
            mm = nc.tensor.matmul
            for k in range(NB):
                for t in range(6):
                    g = 6 * k + t
                    if g % 2 == 0 and g >= 4:
                        pe.wait_ge(sem("vt"), 1 + g // 2 - 1)
                    ins = nc.tensor.transpose(pt[:, 4 * (g // 2 % 2) + g % 2, :], p[:, 12 + t, 128 * k:128 * k + 128],
                                              c["ident"])
                    if g % 2:
                        ins.then_inc(sem("vtr"), 1)
            pe.wait_ge(sem("vt"), 1 + 3 * NB)

            def body(i, pair, par, u, r):
                pe.wait_ge(sem("q"), 1 + 3 * (u + 1))
                pe.wait_ge(sem("bias"), 1 + 3 * u)
                for g, w in enumerate(widths(i)):
                    k0 = 128 * (i + 1 - w)
                    k = p[:, 6 + 2 * g:8 + 2 * g, k0:128 * (i + 1)][:, bass.ds(pair, 1), :]
                    ins = mm(score[:, g, 0:128 * w], qm[:, par, g, :], k, start=True, stop=True)
                ins.then_inc(sem("s"), 1)
                pe.wait_ge(sem("exp"), 1 + u + 1)
                pe.wait_ge(sem("pt"), 1 + u)
                n = sum(widths(i))
                for k in range(n):
                    ins = nc.tensor.transpose(pt[:, k, :], S[:, par, 128 * k:128 * k + 128], c["ident"])
                ins.then_inc(sem("tr"), 1)
                pe.wait_ge(sem("pt"), 1 + u + 1)
                pe.wait_ge(sem("or"), 1 + u)
                k = 0
                for g, w in enumerate(widths(i)):
                    for j in range(i + 1 - w, i + 1):
                        v = vt[:, j, 256 * g:256 * g + 256].rearrange("p (a b) -> p a b", a=2)[:, bass.ds(pair, 1), 64 * par:64 * par + 64]
                        ins = mm(po[:, 0:64], PT[:, k, :], v, start=(k == 0), stop=(k == n - 1))
                        k += 1
                ins.then_inc(sem("o"), 1)

            def after(i):
                pe.wait_ge(sem("or"), 1 + 4 * (i + 1))
                pe.wait_ge(sem("out"), 1 + i)
                for t in range(2):
                    ins = nc.tensor.transpose(pf[:, t, :], o[:, i % 2, t, :], c["ident"])
                ins.then_inc(sem("fin"), 1)
            units(pe, body, after)

        @block.vector
        def _(dve):
            V = nc.vector
            dve.wait_ge(sem("c"), 1 + 32)

            def body(i, pair, par, u, r):
                ws = widths(i)
                n = sum(ws)
                dve.wait_ge(sem("s"), 1 + u)
                for g in range(3):
                    q = p[:, 2 * g:2 * g + 2, 128 * i:128 * i + 128][:, bass.ds(pair, 1), :]
                    V.tensor_tensor(qm[:, par, g:g + 1, :], q,
                                    bcast(bcast(c["halves8"][:, par], 1, 1), 2, 128), ALU.mult).then_inc(sem("q"), 1)
                dve.wait_ge(sem("s"), 1 + u + 1)
                dve.wait_ge(sem("tr"), 1 + (u - 1 if (i or par) else pair * 2))
                at = 0
                for g, w in enumerate(ws):
                    end = sum(near[:g + 1])
                    h = slope[:, 4 * g:4 * g + 4].rearrange("p (a b) -> p a b", b=2)[:, bass.ds(pair, 1), par]
                    V.scalar_tensor_tensor(S[:, par, 128 * at:128 * (at + w)],
                                           dist[:, end - w:end, :].rearrange("p a b -> p (a b)"), h,
                                           score[:, g, 0:128 * w], ALU.mult, ALU.add).then_inc(sem("bias"), 1)
                    at += w
                dve.wait_ge(sem("bias"), 1 + 3 * (u + 1))
                dve.wait_ge(sem("exp"), 1 + u)
                V.tensor_reduce(mx[:, :], S[:, par, 0:128 * n], AX.X, ALU.max, negate=True).then_inc(sem("mx"), 1)
                dve.wait_ge(sem("exp"), 1 + u + 1)
                V.reciprocal(ri[:, :], rs[:, par:par + 1]).then_inc(sem("ri"), 1)
                dve.wait_ge(sem("ri"), 1 + u + 1)
                dve.wait_ge(sem("o"), 1 + u + 1)
                dve.wait_ge(sem("fin"), 1 + max(i - 1, 0))
                V.tensor_scalar(o[:, i % 2, bass.ds(pair, 1), 64 * par:64 * par + 64], po[:, 0:64], ri[:, 0:1],
                                None, ALU.mult).then_inc(sem("or"), 1)
            units(dve, body)

        @block.scalar
        def _(act):
            A = nc.scalar.activation
            for g in range(3 * NB):
                act.wait_ge(sem("vtr"), 1 + g + 1)
                k, t = divmod(2 * g, 6)
                A(vt[:, k, 128 * t:128 * t + 256], pt[:, 4 * (g % 2):4 * (g % 2) + 2, :].rearrange("p a b -> p (a b)"),
                  ACT.Copy).then_inc(sem("vt"), 1)

            def body(i, pair, par, u, r):
                n = sum(widths(i))
                x = S[:, par, 0:128 * n]
                act.wait_ge(sem("mx"), 1 + u + 1)
                act.wait_ge(sem("ri"), 1 + u)
                A(x, x, ACT.Exp, bias=mx[:, 0:1], accum_out=rs[:, par:par + 1]).then_inc(sem("exp"), 1)
                act.wait_ge(sem("tr"), 1 + u + 1)
                act.wait_ge(sem("o"), 1 + u)
                A(PT[:, 0:n, :], pt[:, 0:n, :], ACT.Copy).then_inc(sem("pt"), 1)

            def after(i):
                act.wait_ge(sem("fin"), 1 + i + 1)
                A(out[:, 0:2, 128 * i:128 * i + 128], pf[:, 0:2, :], ACT.Copy).then_inc(sem("out"), 1)
            units(act, body, after)


def stick_breaking(nc, name, p, out, c):
    NB = LAT // 128
    with ExitStack() as st:
        s = Stage(nc, st, name)
        sem = s.sem
        vt = s.sb("vt", [128, NB, 256])
        z, e, l = s.sb("z", [128, 2, LAT]), s.sb("e", [128, 2, LAT]), s.sb("l", [128, 2, LAT])
        sp, at = s.sb("sp", [128, NB, LAT]), s.sb("at", [128, NB, LAT])
        pz = [s.ps(f"pz{i}", [128, LAT]) for i in range(2)]
        pr = [s.ps(f"pr{i}", [128, LAT]) for i in range(2)]
        po = [s.ps(f"po{i}", [128, LAT]) for i in range(2)]
        pt = s.ps("pt", [128, 4, 128])
        for n in ("vtr", "vt", "z", "zs", "abs", "exp", "ln", "sp0", "sp", "sum", "log", "min", "ex", "at", "o", "or"):
            sem(n)
        block = st.enter_context(nc.Block())
        units = [(4 * h + n, h, NB - 1 - n) for h in range(4) for n in range(NB)]
        rows = lambda h: slice(64 * (h % 2), 64 * (h % 2) + 64)

        @block.tensor
        def _(pe):
            mm = nc.tensor.matmul
            for k in range(NB):
                if k >= 2:
                    pe.wait_ge(sem("vt"), k - 1)
                for t in range(2):
                    ins = nc.tensor.transpose(pt[:, 2 * (k % 2) + t, :], p[:, 22 + t, 128 * k:128 * k + 128], c["ident"])
                ins.then_inc(sem("vtr"), 1)
                pe.wait_ge(sem("vt"), k + 1)

            def scores(u, h, j):
                if u >= 2:
                    pe.wait_ge(sem("zs"), u - 1)
                t0 = 128 * j
                mm(pz[u % 2][:, t0:LAT], p[rows(h), 20 + h // 2, t0:t0 + 128], p[rows(h), 18 + h // 2, t0:LAT],
                   start=True, stop=True).then_inc(sem("z"), 1)

            def sums(u, h, j):
                pe.wait_ge(sem("sp"), u + 1)
                if u >= 2:
                    pe.wait_ge(sem("log"), u - 1)
                t0 = 128 * j
                ins = mm(pr[u % 2][:, t0:LAT], c["from128"], sp[:, j, t0:LAT], start=True, stop=(j == NB - 1))
                for j2 in range(j + 1, NB):
                    ins = mm(pr[u % 2][:, 128 * j2:LAT], c["ones"], sp[:, j2, 128 * j2:LAT], start=False,
                             stop=(j2 == NB - 1))
                ins.then_inc(sem("sum"), 1)

            def apply(h):
                pe.wait_ge(sem("at"), 4 * h + 4)
                if h >= 2:
                    pe.wait_ge(sem("or"), h - 1)
                for j in range(NB):
                    ins = mm(po[h % 2][rows(h), 128 * j:LAT], vt[:, j, 64 * h:64 * h + 64], at[:, j, 128 * j:LAT],
                             start=(j == 0), stop=(j == NB - 1))
                ins.then_inc(sem("o"), 1)
            scores(*units[0])
            for n, (u, h, j) in enumerate(units):
                if n + 1 < len(units):
                    scores(*units[n + 1])
                sums(u, h, j)
                if j == 0:
                    apply(h)

        @block.scalar
        def _(act):
            A = nc.scalar.activation
            for k in range(NB):
                act.wait_ge(sem("vtr"), k + 1)
                A(vt[:, k, :], pt[:, 2 * (k % 2):2 * (k % 2) + 2, :].rearrange("p a b -> p (a b)"), ACT.Copy)\
                    .then_inc(sem("vt"), 1)

            def first(u, h, j):
                b, t = u % 2, slice(128 * j, LAT)
                act.wait_ge(sem("z"), u + 1)
                if u >= 2:
                    act.wait_ge(sem("log"), u - 1)
                    act.wait_ge(sem("sp0"), u - 1)
                A(z[:, b, t], pz[b][:, t], ACT.Copy, scale=0.125).then_inc(sem("zs"), 1)
                act.wait_ge(sem("zs"), u + 1)
                A(e[:, b, t], z[:, b, t], ACT.Abs).then_inc(sem("abs"), 1)
                act.wait_ge(sem("abs"), u + 1)
                A(e[:, b, t], e[:, b, t], ACT.Exp, scale=-1.0).then_inc(sem("exp"), 1)
                act.wait_ge(sem("exp"), u + 1)
                A(l[:, b, t], e[:, b, t], ACT.Ln, bias=1.0).then_inc(sem("ln"), 1)

            def second(u, h, j):
                t = slice(128 * j, LAT)
                act.wait_ge(sem("min"), u + 1)
                A(at[:, j, t], at[:, j, t], ACT.Exp).then_inc(sem("ex"), 1)
                if j == 0:
                    act.wait_ge(sem("o"), h + 1)
                    A(out[rows(h), 2 + h // 2, :], po[h % 2][rows(h), :], ACT.Copy).then_inc(sem("or"), 1)
            first(*units[0])
            for n, x in enumerate(units):
                if n + 1 < len(units):
                    first(*units[n + 1])
                second(*x)

        @block.vector
        def _(dve):
            V = nc.vector

            def first(u, h, j):
                b, t = u % 2, slice(128 * j, LAT)
                dve.wait_ge(sem("ln"), u + 1)
                if u >= 1:
                    dve.wait_ge(sem("sum"), u if j < NB - 1 else 4 * h)
                V.scalar_tensor_tensor(sp[:, j, t], z[:, b, t], 0.0, l[:, b, t], ALU.max, ALU.add).then_inc(sem("sp0"), 1)
                dve.wait_ge(sem("sp0"), u + 1)
                own = sp[:, j, 128 * j:128 * j + 128]
                V.tensor_tensor(own, own, c["before128"], ALU.mult).then_inc(sem("sp"), 1)

            def second(u, h, j):
                b, t = u % 2, slice(128 * j, LAT)
                dve.wait_ge(sem("sum"), u + 1)
                if h >= 1:
                    dve.wait_ge(sem("o"), h)
                V.tensor_tensor(at[:, j, t], z[:, b, t], pr[b][:, t], ALU.subtract).then_inc(sem("log"), 1)
                dve.wait_ge(sem("log"), u + 1)
                V.tensor_scalar_min(at[:, j, t], at[:, j, t], 0.0).then_inc(sem("min"), 1)
                dve.wait_ge(sem("ex"), u + 1)
                own = at[:, j, 128 * j:128 * j + 128]
                V.tensor_tensor(own, own, c["before128"], ALU.mult).then_inc(sem("at"), 1)
            for x in units:
                first(*x)
                second(*x)


def copy_in(nc, name, pairs):
    with ExitStack() as st:
        s = Stage(nc, st, name)
        sem = s.sem
        sem("in")
        block = st.enter_context(nc.Block())

        @block.sync
        def _(sp):
            for dst, src in pairs:
                sp.dma_start(dst, src).then_inc(sem("in"), 16)
            sp.wait_ge(sem("in"), 16 * len(pairs))


def ada_gain(nc, name, gain, scale, gm):
    with ExitStack() as st:
        s = Stage(nc, st, name)
        done = s.sem("done")
        block = st.enter_context(nc.Block())

        @block.vector
        def _(dve):
            nc.vector.scalar_tensor_tensor(gm[:], scale, 1.0, bcast(gain, 2, 2), ALU.add, ALU.mult).then_inc(done, 1)
            dve.wait_ge(done, 1)


def program(nc, a, out, at):
    x_dram = nc.dram_tensor("x_between", [128, DT, T], F32, kind="Internal").ap()
    with ExitStack() as top:
        g = Stage(nc, top, "top")
        cols = g.sb("cols", list(a["cols"].shape))
        base = g.sb("base", [128, 2, 128])
        halves = g.sb("halves", [128, 2, 2])
        every_mod = g.sb("mods", [128, 12 * DT, 2])
        mods = every_mod[:, 0:6 * DT, :]
        sil = g.sb("sil", [128, DT, 2])
        gm = g.sb("gm", [128, DT, 2])
        h = g.sb("h", [128, DT, T])
        copy_in(nc, "in", [(cols[:], a["cols"]), (base[:], a["base"]), (halves[:], a["halves"])])
        consts = {"ident": base[:, 0, :], "ones": base[:, 1, :], "halves": halves[:, 0, :], "halves8": halves[:, 1, :]}
        col = lambda n, m=0: cols[:, at[n] + m:at[n] + m + 1]
        span = lambda n, m: cols[:, at[n]:at[n] + m]
        dyn = lambda n, lo, m: cols[:, at[n] + lo:at[n] + lo + DT * 3][:, bass.ds(m, 1)]

        def masks(st, name, names, extra=()):
            m = st.enter_context(nc.sbuf_tensor("m_" + name, [128, len(names), 128], F32))
            copy_in(nc, name + "_in", [(m[:], a[name])] + list(extra))
            return {n: m[:, i, :] for i, n in enumerate(names)}, m

        def ada(name, x, dst, norm, first, parts=EVERY):
            ada_gain(nc, name + "_g", span(norm, DT), mods[:, first + DT:first + 2 * DT, :], gm)
            which = 2 - len(parts)
            view = lambda y: (lambda t, t0, tn: y[:, t, t0:t0 + tn])
            rms(nc, name, view(x), view(dst), [list(range(DT))], parts, consts["ones"], D, col("eps6"),
                lambda t, p: gm[:, t, p + which:p + which + 1],
                shift=lambda t, p: mods[:, first + t, p + which:p + which + 1])

        def mlp(layer, x, h, parts, pieces):
            m = 4 * DT // pieces
            for q in range(pieces):
                with nc.sbuf_tensor(f"hidden{layer}_{q}", [128, m, sum(tn for _, tn in parts)], F32) as hid:
                    n = f"up{layer}_{q}"
                    product(nc, n, a[f"mlp_w1_{layer}"], h, DT, m, parts, RELU2, hid, tile0=m * q,
                            side=rider(n) if n in riders else None)
                    product(nc, f"down{layer}_{q}", a[f"mlp_w2_{layer}"], hid, m, DT, parts, ADD, x, k0=m * q,
                            per=4 if m == DT else 2, gate=mods[:, 5 * DT:6 * DT, :])

        with ExitStack() as st:
            s = Stage(nc, st, "silu")
            done = s.sem("done")
            with nc.Block() as block:
                @block.scalar
                def _(act):
                    nc.scalar.activation(sil[:], cols[:, at["c"]:at["c"] + 2 * DT].rearrange("p (b a) -> p a b", b=2),
                                         ACT.Silu).then_inc(done, 1)
                    act.wait_ge(done, 1)
        FIRST = 20
        riders = {"in0": 2, "out0": 2, "up0_0": 1}
        starts = dict(zip(riders, (FIRST, FIRST + 2 * 26, FIRST + 2 * 26 + 2 * DT)))
        assert starts["up0_0"] + DT == 12 * DT
        rider = lambda n: Side(a["mod_w"], sil, every_mod, span("mod_b", 12 * DT), starts[n], riders[n])
        small_product(nc, "mod", a["mod_w"], sil, FIRST, every_mod, span("mod_b", 12 * DT))
        with nc.sbuf_tensor("x_0a", [128, DT, T], F32) as x:
            copy_in(nc, "x0", [(x[:], a["x"])])
            ada("n10", x, h, "norm1_0", 0)
        with ExitStack() as st:
            p = st.enter_context(nc.sbuf_tensor("p0", [128, 26, T], F32))
            product(nc, "in0", a["w_in0"], h, DT, 26, EVERY, COPY, p, side=rider("in0"))
            m, raw = masks(st, "masks0", MASKS0)
            c = {**consts, **m, "levels": raw[:, MASKS0.index("level0"):MASKS0.index("level0") + 6, :]}
            c["level1"] = c["level0"]
            rope(nc, p, a["rope"], c)
            diff_attention(nc, p, h, a["lam"], c)
            tiles = lambda lo: (lambda t, t0, tn: h[:, lo + t, t0:t0 + tn])
            rms(nc, "sub", tiles(0), tiles(0), [[t] for t in range(4)], ((0, 512), (512, 256)), consts["ones"],
                128 * (1 - LAM_INIT) ** 2, col("eps5"), lambda t, p_: col("subln"))
            sig, kk = p[:, 0:8, :], p[:, 8:12, :]
            with ExitStack() as st2:
                b = st2.enter_context(nc.sbuf_tensor("b", [128, 4, T], F32))
                with nc.sbuf_tensor("cmask", [128, T], F32) as cm:
                    chunk_mask(nc, "cm0", cm, RC)
                    c["chunk_mask"] = cm[:, :]
                    rwkv_prepare(nc, p, sig, kk, b, col, a["lora"], c)
                rwkv_scan(nc, p, sig, kk, b, h[:, 4:8, :], c)
            rwkv_finish(nc, p, h[:, 4:8, :], col, a["g2"], c, col("epsg"))
        with nc.sbuf_tensor("x_0b", [128, DT, T], F32) as x:
            copy_in(nc, "x1", [(x[:], a["x"])])
            product(nc, "out0", a["w_out0"], h, DT, DT, EVERY, ADD, x, gate=mods[:, 2 * DT:3 * DT, :],
                    side=rider("out0"))
            ada("n20", x, h, "norm2_0", 3 * DT)
            mlp(0, x, h, EVERY, 4)
            mods = every_mod[:, 6 * DT:12 * DT, :]
            ada("n11", x, h, "norm1_1", 0)
            copy_in(nc, "x2", [(x_dram, x[:])])
        with ExitStack() as st:
            m, raw = masks(st, "masks1", MASKS1)
            k0 = MASKS1.index("pair0")
            c = {**consts, **m, "pair_level": raw[:, k0:k0 + 8, :]}
            p = st.enter_context(nc.sbuf_tensor("p1", [128, 25, T], F32))
            sp = st.enter_context(nc.sbuf_tensor("sp", [128, 4, T], F32))
            product(nc, "in1", a["w_in1"], h, DT, 25, EVERY, COPY, p, per=4)
            with nc.sbuf_tensor("dtla", [16, 2, T], F32) as dtla:
                ssd_prepare(nc, p, dtla, col, c)
                ssd_scan(nc, p, dtla, h[:, 0:4, :], c)
            ssd_finish(nc, p, h[:, 0:4, :], col)
            with nc.sbuf_tensor("cmask1", [128, T], F32) as cm:
                chunk_mask(nc, "cm1", cm, CHUNK)
                c["chunk_mask128"] = cm[:, :]
                gla_prepare(nc, p, sp, col, a["gk_up"], c)
            gla_scan(nc, p, sp, h[:, 4:8, :], c)
            ht = lambda t, t0, tn: h[:, t, t0:t0 + tn]
            rms(nc, "ssdn", ht, ht, [[0, 1], [2, 3]], LATENTS, consts["ones"], 256, col("eps6"),
                lambda t, p_: col("ssm_norm", t))
            rms(nc, "glan", ht, ht, [[4], [5], [6], [7]], LATENTS, consts["ones"], 128, col("eps6"),
                lambda t, p_: col("gla_norm"), silu_src=lambda t, t0, tn: p[:, 16 + t, t0:t0 + tn])
        with nc.sbuf_tensor("xl", [128, DT, LAT], F32) as x:
            copy_in(nc, "x3", [(x[:], x_dram[:, :, CTX:T])])
            ONE = ((0, LAT),)
            hl = h[:, :, CTX:T]
            product(nc, "out1", a["w_out1"], hl, DT, DT, ONE, ADD, x, per=4, gate=mods[:, 2 * DT:3 * DT, :])
            ada("n21", x, hl, "norm2_1", 3 * DT, ONE)
            mlp(1, x, hl, ONE, 2)
            view = lambda y: (lambda t, t0, tn: y[:, t, t0:t0 + tn])
            all_tiles = [list(range(DT))]
            rms(nc, "fin1", view(x), view(x), all_tiles, ONE, consts["ones"], D, col("eps6"),
                lambda t, p_: col("final_norm", t))

            for l in range(2):
                hs = h[:, :, 0:LAT]
                rms(nc, f"b1{l}", view(x), view(hs), all_tiles, ONE, consts["ones"], D, col("eps6"),
                    lambda t, p_: col(f"b_norm1_{l}", t))
                with ExitStack() as st:
                    m, _ = masks(st, "masks2", MASKS2) if l == 0 else masks_again(nc, st, a)
                    c = {**consts, **m}
                    gates = st.enter_context(nc.sbuf_tensor(f"gates{l}", [128, 2 * DT, LAT], F32))
                    o = st.enter_context(nc.sbuf_tensor(f"o{l}", [128, 4, LAT], F32))
                    product(nc, f"bg{l}", a[f"b_w_in{l}"][24:40], hs, DT, 16, ONE, GATE, gates, per=4,
                            bias=span(f"b_gate_{l}", 16))
                    with nc.sbuf_tensor(f"pb{l}", [128, 24, LAT], F32) as p:
                        product(nc, f"bi{l}", a[f"b_w_in{l}"][0:24], hs, DT, 24, ONE, COPY, p, per=4)
                        dilated_attention(nc, f"di{l}", p, o, a["slope"], a["dist"], c)
                        stick_breaking(nc, f"sb{l}", p, o, c)
                    product(nc, f"bm{l}", a[f"b_w_br{l}"], o, 4, DT, ((0, LAT), (0, LAT)), MERGE, hs, unit=4,
                            per=4, gate=gates)
                product(nc, f"bo{l}", a[f"b_w_o{l}"], hs, DT, DT, ONE, ADD, x, per=4)
                rms(nc, f"b2{l}", view(x), view(hs), all_tiles, ONE, consts["ones"], D, col("eps6"),
                    lambda t, p_: col(f"b_norm2_{l}", t))
                FT = 22
                with nc.sbuf_tensor(f"glu{l}", [128, FT, LAT], F32) as hid:
                    product(nc, f"bu{l}", a[f"b_w_up{l}"], hs, DT, 2 * FT, ONE, GLU, hid, per=4,
                            bias=span(f"b_conv_b{l}", FT),
                            taps=lambda k, m: cols[:, at[f"b_conv_w{l}"] + FT * k:at[f"b_conv_w{l}"] + FT * (k + 1)]
                            [:, bass.ds(m, 1)])
                    for k0 in (0, FT // 2):
                        product(nc, f"bd{l}_{k0}", a[f"b_w_down{l}"], hid[:, k0:k0 + FT // 2, :], FT // 2, DT, ONE,
                                ADD, x, unit=FT // 2, per=4, k0=k0)
            rms(nc, "fin2", view(x), view(x), all_tiles, ONE, consts["ones"], D, col("eps6"),
                lambda t, p_: col("b_norm_f", t))
            copy_in(nc, "store", [(out, x[:])])


def masks_again(nc, st, a):
    m = st.enter_context(nc.sbuf_tensor("masks2b", [128, len(MASKS2), 128], F32))
    copy_in(nc, "masks2b_in", [(m[:], a["masks2"])])
    return {n: m[:, i, :] for i, n in enumerate(MASKS2)}, m


def chunk_mask(nc, name, m, chunk):
    with ExitStack() as st:
        s = Stage(nc, st, name)
        done = s.sem("done")
        block = st.enter_context(nc.Block())

        @block.vector
        def _(dve):
            nc.vector.memset(m[:, :], 1.0).then_inc(done, 1)
            dve.wait_ge(done, 1)
            nc.vector.memset(m[:, 0:T:chunk], 0.0).then_inc(done, 1)
            dve.wait_ge(done, 2)


MASKS0 = ["head_ones", "lower", "upper", "upper_inc"] + [f"level{l}" for l in range(6)] + ["level1_t", "rot"]
MASKS1 = ["upper_inc128", "lower128"] + [f"pair{l}" for l in range(8)]
MASKS2 = ["from128", "before128"]



def constants():
    m = {**square_masks(), **chunk_masks()}
    j, i = np.arange(128)[:, None], np.arange(128)[None, :]
    m["from128"], m["before128"] = j >= i, j < i
    lo = i % 32 < 16
    m["rot"] = np.where(lo & (j == i + 16), -1.0, 0.0) + np.where(~lo & (j == i - 16), 1.0, 0.0)
    pack = lambda names: np.stack([np.asarray(m[n], np.float32) for n in names], axis=1)
    out = {"base": pack(["ident", "ones"]), "masks0": pack(MASKS0), "masks1": pack(MASKS1), "masks2": pack(MASKS2)}
    half = (np.arange(128)[:, None] // 64 == np.arange(2)).astype(np.float32)
    out["halves"] = np.stack([half, half * np.float32(0.125)], axis=1)
    ch, t = np.arange(128), np.arange(LAT)
    inv = (np.float32(10000.0) ** (-np.arange(16, dtype=np.float32) / np.float32(16))).astype(np.float32)
    pos = np.where((ch % 64 // 32 == 0)[:, None], (t // 64)[None, :], (t % 64)[None, :]).astype(np.float32)
    ang = pos * inv[ch % 16][:, None]
    out["rope"] = np.stack([np.cos(ang), np.sin(ang)], axis=1).astype(np.float32)
    dist = []
    for (window, dilation), near in zip(GROUPS, (2, 4, 4)):
        for o in range(near - 1, -1, -1):
            d = o * 128 + j - i
            ok = (d >= 0) & (d <= window) & (d % dilation == 0)
            dist.append(np.where(ok, d, 1e30))
    out["dist"] = np.stack(dist, axis=1).astype(np.float32)
    slopes = (2.0 ** (-8.0 * np.arange(1, 13) / 12)).astype(np.float32)
    out["slope"] = np.broadcast_to(-slopes, (128, 12)).copy()
    return out


def layouts(v):
    f = np.float32
    tile_w = lambda w: np.ascontiguousarray(
        w.reshape(w.shape[0] // 128, 128, w.shape[1] // 128, 128).transpose(2, 1, 0, 3)).reshape(
            w.shape[1] // 128, 128, w.shape[0])
    chan = lambda x: np.ascontiguousarray(x.T.reshape(DT, 128, -1).transpose(1, 0, 2))
    d = constants()
    d["x"] = chan(np.concatenate([v["ctx"][0], v["x"][0]], axis=0))
    for l in range(2):
        d[f"w_out{l}"] = tile_w(v[f"l{l}_w_out"])
        d[f"mlp_w1_{l}"] = tile_w(v[f"l{l}_mlp_w1"])
        d[f"mlp_w2_{l}"] = tile_w(v[f"l{l}_mlp_w2"])
        d[f"b_w_in{l}"] = tile_w(v["w_in_2"][l])
        d[f"b_w_br{l}"] = tile_w(v["w_br_2"][l])
        d[f"b_w_o{l}"] = tile_w(v["w_o_2"][l])
        up = v["w_up_2"][l]
        d[f"b_w_up{l}"] = tile_w(up.reshape(D, 2, -1, 128).transpose(0, 2, 1, 3).reshape(D, -1))
        d[f"b_w_down{l}"] = tile_w(v["w_down_2"][l])
    d["mod_w"] = np.concatenate([tile_w(v[f"l{l}_mod_w"]) for l in range(2)], axis=0)
    d["w_in0"] = tile_w(v["l0_w_in"])
    w = v["l1_w_in"]
    last = np.zeros((D, 128), f)
    last[:, 0:16] = w[:, 1536:1552]
    last[:, 32:48] = w[:, 3088:3104]
    d["w_in1"] = tile_w(np.concatenate([w[:, 0:1536], w[:, 1552:3088], last], axis=1))
    d["lam"] = np.stack([v["l0_lam_q1"], v["l0_lam_q2"], v["l0_lam_k1"], v["l0_lam_k2"]], axis=1)
    lora = np.zeros((2, 128, 512), f)
    lora[0, 0:64], lora[0, 64:128], lora[1, 0:64] = v["l0_w2_f"], v["l0_a2"], v["l0_w2_b"]
    d["lora"], d["g2"] = lora, v["l0_g2"]
    d["gk_up"] = np.concatenate([v["l1_gk_up_f"], v["l1_gk_up_b"]], axis=1)
    one = lambda *x: np.concatenate(x + (np.zeros(128 - sum(y.size for y in x), f),))
    cols = {"c": np.concatenate([v["c_ctx"], v["c"][0]]), "final_norm": v["final_norm"], "b_norm_f": v["norm_f_2"],
            "subln": v["l0_subln"], "ssm_norm": v["l1_ssm_norm"], "gla_norm": v["l1_gla_norm"],
            "conv_w": v["l1_conv_w"].reshape(-1), "conv_b": v["l1_conv_b"],
            "dt_bias": one(v["l1_dt_bias_f"], v["l1_dt_bias_b"]), "a_log": one(v["l1_a_log_f"], v["l1_a_log_b"]),
            "gk_b": np.concatenate([v["l1_gk_b_f"], v["l1_gk_b_b"]]), "d_skip": np.repeat(v["l1_d_skip"], 64),
            "eps6": np.full(128, 1e-6, f), "eps5": np.full(128, 1e-5 / (1 - LAM_INIT) ** 2, f), "epsg": np.full(128, 64e-5, f)}
    for n in ("mu", "k_k", "k_a", "r_k", "w0_f", "w0_b", "a0", "lnx_w", "lnx_b"):
        cols[n] = v["l0_" + n]
    for l in range(2):
        for n in (1, 2):
            cols[f"norm{n}_{l}"] = v[f"l{l}_norm{n}"]
            cols[f"b_norm{n}_{l}"] = v[f"norm{n}_2"][l]
        cols[f"b_gate_{l}"] = v["b_gate_2"][l]
        cols[f"b_conv_w{l}"] = v["conv_w_2"][l].reshape(-1)
        cols[f"b_conv_b{l}"] = v["conv_b_2"][l]
    cols["mod_b"] = np.concatenate([v["l0_mod_b"], v["l1_mod_b"]])
    at, n = {}, 0
    for name, x in cols.items():
        at[name] = n
        n += x.size // 128
    d["cols"] = np.concatenate([x.reshape(-1, 128).T for x in cols.values()], axis=1)
    return {n: np.ascontiguousarray(x) for n, x in d.items()}, at


def kernel(**inputs):
    import concourse.bacc as bacc
    from concourse.bass_utils import run_bass_kernel_spmd

    arrays, at = layouts({n: np.asarray(x) for n, x in inputs.items()})
    nc = bacc.Bacc("TRN2", target_bir_lowering=False, num_devices=1)
    a = {n: nc.dram_tensor("in_" + n, x.shape, mybir.dt.from_np(x.dtype), kind="ExternalInput").ap()
         for n, x in arrays.items()}
    out = nc.dram_tensor("out", (128, DT, LAT), F32, kind="ExternalOutput").ap()
    program(nc, a, out, at)
    r = run_bass_kernel_spmd(nc, [{"in_" + n: x for n, x in arrays.items()}], core_ids=[0])
    got = r.results[0]["out"]
    return np.ascontiguousarray(got.transpose(2, 1, 0).reshape(1, LAT, D))
```

```python
import math
from contextlib import ExitStack

import concourse.bass as bass
from concourse import mybir
import numpy as np

F32 = mybir.dt.float32
ACT = mybir.ActivationFunctionType
ALU = mybir.AluOpType
AX = mybir.AxisListType

D = 1024
DT = D // 128
CTX, LAT = 256, 512
T = CTX + LAT
EVERY = ((0, CTX), (CTX, LAT))
LATENTS = ((CTX, LAT),)
RELU2, COPY, ADD, GATE, GLU, MERGE = range(6)


class Steps:

    def __init__(self, engine, sem, base=0):
        self.engine, self.sem, self.n, self.base = engine, sem, 0, base

    def did(self, instruction):
        instruction.then_inc(self.sem, 1)
        self.n += 1

    def wait(self):
        self.engine.wait_ge(self.sem, self.base + self.n)


class Side:

    def __init__(self, w_dram, act, out, bias, first, per):
        self.w, self.act, self.out, self.bias, self.first, self.per = w_dram, act, out, bias, first, per


def product(nc, name, w_dram, act, kt, tiles, parts, mode, out, unit=8, per=8, gate=None, bias=None,
            taps=None, side=None, tile0=0, k0=0):
    units = kt // unit
    np_ = len(parts)
    assert per % 2 == 0 and tiles >= per
    ring = 4
    assert per * units % ring == 0
    wide = unit * 128
    F32R = mybir.dt.float32r
    cols = max(t0 + tn for t0, tn in parts)
    SR = 4
    EARLY = 2
    with ExitStack() as st:
        s = Stage(nc, st, name)
        raw = s.sb("raw", [128, ring, wide])
        w_hi, w_lo = (st.enter_context(nc.sbuf_tensor(f"{name}_w{x}", [128, 2, wide], F32R)) for x in ("hi", "lo"))
        a_hi, a_lo = (st.enter_context(nc.sbuf_tensor(f"{name}_a{x}", [128, kt, cols], F32R)) for x in ("hi", "lo"))
        scratch = s.sb("scratch", [128, 2, 512]) if mode in (GLU, MERGE) else None
        psum = [[s.ps(f"acc{b}{p}", [128, 512]) for p in range(np_)] for b in range(2)]
        loaded = [s.sem(f"loaded{r}") for r in range(ring)]
        w_hi_done, w_split, w_used = s.sem("w_hi_done"), s.sem("w_split"), s.sem("w_used")
        a_hi_done, a_split = s.sem("a_hi_done"), s.sem("a_split")
        summed, bank_free, squared = s.sem("summed"), s.sem("bank_free"), s.sem("squared")
        tap0, tap1, tap2, gelu, glu = (s.sem(n) for n in ("tap0", "tap1", "tap2", "gelu", "glu"))
        mine, theirs, merged = s.sem("mine"), s.sem("theirs"), s.sem("merged")
        if side:
            side_w = s.sb("side_w", [128, SR, DT * 128])
            side_ps = [s.ps(f"side{b}", [128, side.per, 2]) for b in range(2)]
            side_loaded = [s.sem(f"side_loaded{r}") for r in range(SR)]
            side_summed, side_read = s.sem("side_summed"), s.sem("side_read")
        block = st.enter_context(nc.Block())
        rounds = tiles // per

        def over_tiles(engine, body):
            if rounds > 1:
                with engine.Fori(0, rounds) as i:
                    for j in range(per):
                        body(i, j, i * per + j)
            else:
                for j in range(per):
                    body(0, j, j)
            for j in range(tiles - rounds * per):
                body(rounds, j, rounds * per + j)

        def split_ahead(engine, split, finish):
            def run(i, js):
                for j in js:
                    split(i, j, i * per + j)
                    if j:
                        finish(i, j - 1, i * per + j - 1)
                    elif not (isinstance(i, int) and i == 0):
                        finish(i - 1, per - 1, i * per - 1)
            run(0, range(per))
            if rounds > 1:
                with engine.Fori(1, rounds) as i:
                    run(i, range(per))
            run(rounds, range(tiles - rounds * per))
            last = tiles - 1
            finish(last // per, last % per, last)

        def unit_at(j, u):
            return j * units + u

        def pair(i, j):
            return i * (per // 2) + j // 2

        @block.sync
        def _(sp):
            def load(i, j, n):
                for u in range(units):
                    sp.wait_ge(w_split, n * units + u + 1)
                    sp.dma_start(raw[:, unit_at(j, u) % ring, :],
                                 w_dram[bass.ds(n + tile0, 1), :, (k0 + u * unit) * 128:(k0 + (u + 1) * unit) * 128])\
                      .then_inc(loaded[unit_at(j, u) % ring], 16)
                if side:
                    for k in range(side.per):
                        q = j * side.per + k
                        sp.wait_ge(side_summed, n * side.per + k + 1)
                        sp.dma_start(side_w[:, q % SR, :], side.w[bass.ds(n * side.per + (k + side.first), 1), :, :])\
                          .then_inc(side_loaded[q % SR], 16)
            over_tiles(sp, load)

        @block.tensor
        def _(pe):
            mm = nc.tensor.matmul
            pe.sem_inc(w_used, 2)
            if side:
                pe.sem_inc(side_summed, SR)

            def tile(i, j, n):
                for u in range(units):
                    r = unit_at(j, u) % 2
                    pe.wait_ge(w_split, n * units + u + 1 + ring)
                    for p, (t0, tn) in enumerate(parts):
                        if u == 0:
                            pe.wait_ge(bank_free, n * np_ + p + 1)
                        own = range(p * kt // 2, (p + 1) * kt // 2) if mode == MERGE else range(unit)
                        for k in own:
                            if isinstance(i, int) and i == 0 and j == 0:
                                pe.wait_ge(a_split, u * unit + k + 1)
                            w = slice(k * 128, (k + 1) * 128)
                            x = u * unit + k
                            for q, (lhs, rhs) in enumerate(((w_hi, a_hi), (w_lo, a_hi), (w_hi, a_lo))):
                                ins = mm(psum[j % 2][p][:, 0:tn], lhs[:, r, w], rhs[:, x, t0:t0 + tn],
                                         start=(u == 0 and k == own[0] and q == 0),
                                         stop=(u == units - 1 and k == own[-1] and q == 2))
                        if u == units - 1:
                            ins.then_inc(summed, 1)
                    if u < units - 1:
                        ins.then_inc(w_used, 1)
                    else:
                        pe.wait_ge(summed, (n + 1) * np_)
                        pe.sem_inc(w_used, 1)
                if side:
                    pe.wait_ge(side_read, n + 1)
                    for k in range(side.per):
                        q = j * side.per + k
                        pe.wait_ge(side_loaded[q % SR], 16 * (i * (per * side.per // SR) + q // SR + 1))
                        for x in range(DT):
                            ins = mm(side_ps[j % 2][:, k, :], side_w[:, q % SR, x * 128:(x + 1) * 128],
                                     side.act[:, x, :], start=(x == 0), stop=(x == DT - 1))
                        ins.then_inc(side_summed, 1)

            for j in range(per):
                tile(0, j, j)
            if rounds > 1:
                with pe.Fori(1, rounds) as i:
                    for j in range(per):
                        tile(i, j, i * per + j)
            for j in range(tiles - rounds * per):
                tile(rounds, j, rounds * per + j)

        @block.scalar
        def _(act_e):
            A = nc.scalar.activation

            def split_act(ks):
                for k in ks:
                    A(a_hi[:, k, :], act[:, k, 0:cols], ACT.Copy).then_inc(a_hi_done, 1)
            split_act(range(EARLY))
            if mode in (COPY, RELU2, GATE):
                act_e.sem_inc(bank_free, 2 * np_)
            if side:
                act_e.sem_inc(side_read, 2)

            def split(i, j, n):
                for u in range(units):
                    g = unit_at(j, u)
                    act_e.wait_ge(loaded[g % ring], 16 * (i * (per * units // ring) + g // ring + 1))
                    act_e.wait_ge(w_used, n * units + u + 1)
                    A(w_hi[:, g % 2, :], raw[:, g % ring, :], ACT.Copy).then_inc(w_hi_done, 1)
                    if isinstance(i, int) and (i, j, u) == (0, 0, 0):
                        split_act(range(EARLY, kt))

            def finish(i, j, n):
                if mode in (COPY, RELU2, GATE):
                    for p, (t0, tn) in enumerate(parts):
                        act_e.wait_ge(summed, n * np_ + p + 1)
                        dst = out[:, bass.ds(n, 1), t0:t0 + tn]
                        src = psum[j % 2][p][:, 0:tn]
                        if mode == GATE:
                            ins = A(dst, src, ACT.Sigmoid, bias=bias[:, bass.ds(n, 1)])
                        else:
                            ins = A(dst, src, ACT.Relu if mode == RELU2 else ACT.Copy)
                        ins.then_inc(bank_free, 1)
                if mode == GLU and j % 2 == 0:
                    m = pair(i, j)
                    x = scratch[:, j // 2 % 2, :]
                    act_e.wait_ge(summed, n + 1)
                    act_e.wait_ge(glu, m + 1)
                    A(x, psum[0][0][:, :], ACT.Identity, scale=taps(2, m), bias=bias[:, bass.ds(m, 1)])\
                        .then_inc(tap0, 1)
                    act_e.wait_ge(tap2, m + 1)
                    A(x, x, ACT.Gelu).then_inc(gelu, 1)
                if side:
                    act_e.wait_ge(side_summed, (n + 1) * side.per + SR)
                    for k in range(side.per):
                        t = n * side.per + (k + side.first)
                        ins = A(side.out[:, bass.ds(t, 1), :], side_ps[j % 2][:, k:k + 1, :], ACT.Identity,
                                bias=side.bias[:, bass.ds(t, 1)])
                    ins.then_inc(side_read, 1)
            split_ahead(act_e, split, finish)

        @block.vector
        def _(dve):
            V = nc.vector
            dve.sem_inc(w_split, ring)
            if mode in (ADD, MERGE, GLU):
                dve.sem_inc(bank_free, 2 * np_)
            for q, mine_too in ((merged, MERGE), (glu, GLU)):
                if mode == mine_too:
                    dve.sem_inc(q, 1)

            def split_act(ks):
                for k in ks:
                    dve.wait_ge(a_hi_done, k + 1)
                    V.tensor_tensor(a_lo[:, k, :], act[:, k, 0:cols], a_hi[:, k, :].bitcast(F32), ALU.subtract)\
                        .then_inc(a_split, 1)
            split_act(range(EARLY))

            def split(i, j, n):
                for u in range(units):
                    g = unit_at(j, u)
                    dve.wait_ge(w_hi_done, n * units + u + 1)
                    V.tensor_tensor(w_lo[:, g % 2, :], raw[:, g % ring, :], w_hi[:, g % 2, :].bitcast(F32), ALU.subtract)\
                        .then_inc(w_split, 1)
                    if isinstance(i, int) and (i, j, u) == (0, 0, 0):
                        split_act(range(EARLY, kt))

            def finish(i, j, n):
                if mode == ADD:
                    for p, (t0, tn) in enumerate(parts):
                        dve.wait_ge(summed, n * np_ + p + 1)
                        dst = out[:, bass.ds(n, 1), t0:t0 + tn]
                        src = psum[j % 2][p][:, 0:tn]
                        if gate is None:
                            V.tensor_tensor(dst, src, dst, ALU.add).then_inc(bank_free, 1)
                        else:
                            g = gate[:, bass.ds(n, 1), p + 2 - np_]
                            V.scalar_tensor_tensor(dst, src, g, dst, ALU.mult, ALU.add).then_inc(bank_free, 1)
                if mode == MERGE:
                    x, dst = scratch[:, j % 2:j % 2 + 1, :], out[:, bass.ds(n, 1), :]
                    dve.wait_ge(summed, (n + 1) * 2)
                    dve.wait_ge(merged, n + 1)
                    V.tensor_tensor(x, gate[:, bass.ds(n, 1), :], psum[j % 2][0][:].unsqueeze(1), ALU.mult)\
                        .then_inc(mine, 1)
                    V.tensor_tensor(dst, gate[:, bass.ds(n + tiles, 1), :], psum[j % 2][1][:].unsqueeze(1), ALU.mult)\
                        .then_inc(theirs, 1)
                    dve.wait_ge(mine, n + 1)
                    dve.wait_ge(theirs, n + 1)
                    dve.sem_inc(bank_free, 2)
                    V.tensor_tensor(dst, dst, x, ALU.add).then_inc(merged, 1)
                if mode == GLU:
                    m = pair(i, j)
                    x = scratch[:, j // 2 % 2, :]
                    if j % 2 == 0:
                        a = psum[0][0]
                        dve.wait_ge(tap0, m + 1)
                        V.scalar_tensor_tensor(x[:, 1:LAT], a[:, 0:LAT - 1], taps(1, m), x[:, 1:LAT],
                                               ALU.mult, ALU.add).then_inc(tap1, 1)
                        dve.wait_ge(tap1, m + 1)
                        V.scalar_tensor_tensor(x[:, 2:LAT], a[:, 0:LAT - 2], taps(0, m), x[:, 2:LAT],
                                               ALU.mult, ALU.add).then_inc(tap2, 1)
                        dve.wait_ge(tap2, m + 1)
                        dve.sem_inc(bank_free, 1)
                    else:
                        dve.wait_ge(summed, n + 1)
                        dve.wait_ge(gelu, m + 1)
                        V.tensor_tensor(out[:, bass.ds(m, 1), :], x.unsqueeze(1), psum[1][0][:].unsqueeze(1),
                                        ALU.mult).then_inc(glu, 1)
                        dve.wait_ge(glu, m + 2)
                        dve.sem_inc(bank_free, 1)
            split_ahead(dve, split, finish)

        if mode == RELU2:
            @block.gpsimd
            def _(pool):
                def square(i, j, n):
                    pool.wait_ge(bank_free, 2 * np_)
                    pool.wait_ge(bank_free, (n + 1) * np_ + 2 * np_)
                    for t0, tn in parts:
                        dst = out[:, bass.ds(n, 1), t0:t0 + tn]
                        nc.gpsimd.tensor_tensor(dst, dst, dst, ALU.mult).then_inc(squared, 1)
                over_tiles(pool, square)


def small_product(nc, name, w_dram, act, tiles, out, bias, per=4):
    with ExitStack() as st:
        s = Stage(nc, st, name)
        w = s.sb("w", [128, 2 * per, DT * 128])
        bank = [s.ps(f"bank{b}", [128, 2]) for b in range(2)]
        loaded = [s.sem(f"loaded{r}") for r in range(2 * per)]
        summed, read = s.sem("summed"), s.sem("read")
        block = st.enter_context(nc.Block())

        @block.sync
        def _(sp):
            for n in range(tiles):
                if n >= 2 * per:
                    sp.wait_ge(summed, n - 2 * per + 1)
                sp.dma_start(w[:, n % (2 * per), :], w_dram[n]).then_inc(loaded[n % (2 * per)], 16)

        @block.tensor
        def _(pe):
            for n in range(tiles):
                pe.wait_ge(loaded[n % (2 * per)], 16 * (n // (2 * per) + 1))
                if n >= 2:
                    pe.wait_ge(read, n - 1)
                for k in range(DT):
                    ins = nc.tensor.matmul(bank[n % 2][:, :], w[:, n % (2 * per), k * 128:(k + 1) * 128], act[:, k, :],
                                           start=(k == 0), stop=(k == DT - 1))
                ins.then_inc(summed, 1)

        @block.scalar
        def _(act_e):
            for n in range(tiles):
                act_e.wait_ge(summed, n + 1)
                nc.scalar.activation(out[:, n, :], bank[n % 2][:, :], ACT.Identity, bias=bias[:, n:n + 1])\
                    .then_inc(read, 1)


HALF = 64
RC = 64
DECAY = 0.6065306597126334


class Stage:

    def __init__(self, nc, st, name):
        self.nc, self.st, self.name, self.sems = nc, st, name, {}
        st.callback(self.close)

    def seed(self):
        for sem in self.sems.values():
            self.nc.gpsimd.sem_inc(sem, 1)
        self.nc.all_engine_barrier()

    def close(self):
        if self.sems:
            for sem in self.sems.values():
                self.nc.gpsimd.sem_clear(sem)
                self.nc.release_semaphore(sem)

    def sb(self, name, shape):
        return self.st.enter_context(self.nc.sbuf_tensor(f"{self.name}_{name}", shape, F32))

    def ps(self, name, shape):
        return self.st.enter_context(self.nc.psum_tensor(f"{self.name}_{name}", shape, F32))

    def sem(self, name):
        if name not in self.sems:
            self.sems[name] = self.nc.alloc_semaphore(name=f"{self.name}_{name}")
        return self.sems[name]


def bcast(ap, axis, n):
    wide = ap.unsqueeze(axis)
    return wide.broadcast_to([n if k == axis else m for k, m in enumerate(wide.shape)])


def scan_views(d, seg, t0, m):
    base, n = seg
    start = t0[d]

    def view(x, lo, tiles=4):
        return x[:, lo:lo + tiles, base:base + n][:, :, bass.ds(start, m)]
    return view


def scan_steps(engine, body, m):
    for seg, u0 in ((EVERY[0], 0), (EVERY[1], CTX // m)):
        with engine.register(f"back_{engine.bass.next_id()}") as back:
            engine.reg_mov(back, seg[1] - m)
            with engine.Fori(0, seg[1] // m) as i:
                body(seg, (i * m, engine.snap(back, min_val=0, max_val=seg[1] - m)), i + u0)
                engine.reg_sub(back, back, m)


def turned(d, x):
    if d == 0:
        return x
    return x[(slice(None),) * (len(x.shape) - 1) + (slice(None, None, -1),)]


def rwkv_prepare(nc, p, sig, kk, a, col, w_lora, c):
    with ExitStack() as st:
        s = Stage(nc, st, "rp")
        tmp = s.sb("tmp", [128, 2, T])
        tw = s.sb("tw", [64, T])
        lora_a, lora_b = s.sb("lora_a", [128, 512]), s.sb("lora_b", [64, 512])
        sq = s.sb("sq", [128, 2, T])
        inv = s.sb("inv", [128, 2, T])
        acc = [s.ps(f"acc{b}", [128, 1024]) for b in range(2)]
        nrm = [s.ps(f"nrm{b}", [128, 1024]) for b in range(2)]
        sem = s.sem
        order = [12, 13] + list(range(0, 12))
        block = st.enter_context(nc.Block())
        for n in ("loaded", "shifted", "dstep", "tanh", "lora_sum", "sig_done", "kk_raw", "squared",
                  "norm_sum", "root", "kk_done", "acc_read"):
            sem(n)

        @block.sync
        def _(sp):
            sp.dma_start(lora_a[:, :], w_lora[0]).then_inc(sem("loaded"), 16)
            sp.dma_start(lora_b[:, :], w_lora[1][0:64, :]).then_inc(sem("loaded"), 16)

        @block.vector
        def _(dve):
            k = Steps(dve, sem("dstep"))
            for i, m in enumerate(order):
                x, y = p[:, 12 + m, :], tmp[:, i % 2, :]
                k.did(nc.vector.tensor_tensor(y[:, 1:T - 1], x[:, 0:T - 2], x[:, 2:T], ALU.add))
                k.wait()
                k.did(nc.vector.tensor_copy(y[:, 0:CTX + 1:CTX], x[:, 1:CTX + 2:CTX]))
                k.did(nc.vector.tensor_copy(y[:, CTX - 1:T:LAT], x[:, CTX - 2:T - 1:LAT]))
                k.wait()
                k.did(nc.vector.scalar_tensor_tensor(y, y, 0.5, x, ALU.mult, ALU.subtract))
                k.wait()
                nc.vector.scalar_tensor_tensor(x, y, col("mu", m), x, ALU.mult, ALU.add)\
                    .then_inc(sem("shifted"), 1)
                dve.wait_ge(sem("shifted"), i + 1)
            for t in range(4):
                nc.vector.tensor_scalar(kk[:, t, :], p[:, 16 + t, :], col("k_k", t), None, ALU.mult)\
                    .then_inc(sem("kk_raw"), 1)
            for t in range(4):
                dve.wait_ge(sem("root"), t + 1)
                r = inv[:, t % 2, :]
                k.did(nc.vector.tensor_scalar_max(r, r, 1e-12))
                k.wait()
                k.did(nc.vector.reciprocal(r, r))
                k.wait()
                dve.wait_ge(sem("kk_raw"), 4)
                dve.wait_ge(sem("squared"), t + 1)
                nc.vector.tensor_tensor(kk[:, t, :], kk[:, t, :], r, ALU.mult).then_inc(sem("kk_done"), 1)
            for t in range(4):
                dve.wait_ge(sem("sig_done"), 8 + t + 1)
                y = tmp[:, t % 2, :]
                k.wait()
                k.did(nc.vector.tensor_scalar(y, a[:, t, :], -1.0, col("k_a", t), ALU.add, ALU.mult))
                k.wait()
                k.did(nc.vector.scalar_tensor_tensor(p[:, 16 + t, :], y, 1.0, p[:, 16 + t, :], ALU.add, ALU.mult))
                dve.wait_ge(sem("kk_done"), t + 1)
                k.did(nc.vector.tensor_tensor(a[:, t, :], a[:, t, :], kk[:, t, :], ALU.mult))
            for t in range(8):
                dve.wait_ge(sem("sig_done"), t + 1)
                x = sig[:, t, :] if t < 4 else sig[:, t, ::-1]
                k.did(nc.vector.tensor_tensor_scan(x, c["chunk_mask"], x, 0.0, ALU.mult, ALU.add))

        @block.tensor
        def _(pe):
            pe.wait_ge(sem("loaded"), 32)
            pe.wait_ge(sem("tanh"), 1)
            pe.wait_ge(sem("shifted"), 2)
            for n in range(12):
                kind, m = n // 4, n % 4
                lhs = (lora_a[0:64], lora_b[0:64], lora_a[64:128])[kind][:, m * 128:(m + 1) * 128]
                rhs = (tw[:, :], tw[:, :], p[64:128, 24, :])[kind]
                if n >= 2:
                    pe.wait_ge(sem("sig_done"), n - 1)
                for t0, tn in ((0, 512), (512, 256)):
                    ins = nc.tensor.matmul(acc[n % 2][:, t0:t0 + tn], lhs, rhs[:, t0:t0 + tn],
                                           start=True, stop=True)
                ins.then_inc(sem("lora_sum"), 1)
            for t in range(4):
                pe.wait_ge(sem("squared"), t + 1)
                if t >= 2:
                    pe.wait_ge(sem("root"), t - 1)
                for t0, tn in ((0, 512), (512, 256)):
                    ins = nc.tensor.matmul(nrm[t % 2][:, t0:t0 + tn], c["head_ones"], sq[:, t % 2, t0:t0 + tn],
                                           start=True, stop=True)
                ins.then_inc(sem("norm_sum"), 1)

        @block.scalar
        def _(act):
            act.wait_ge(sem("shifted"), 1)
            nc.scalar.activation(tw[:, :], p[0:64, 24, :], ACT.Tanh).then_inc(sem("tanh"), 1)
            for n in range(12):
                kind, m = n // 4, n % 4
                act.wait_ge(sem("lora_sum"), n + 1)
                dst = (sig[:, m, :], sig[:, 4 + m, :], a[:, m, :])[kind]
                nc.scalar.activation(dst, acc[n % 2][:, 0:T], ACT.Sigmoid,
                                     bias=col(("w0_f", "w0_b", "a0")[kind], m)).then_inc(sem("sig_done"), 1)
            for t in range(4):
                act.wait_ge(sem("kk_raw"), t + 1)
                if t >= 2:
                    act.wait_ge(sem("norm_sum"), t - 1)
                nc.scalar.activation(sq[:, t % 2, :], kk[:, t, :], ACT.Square).then_inc(sem("squared"), 1)
                act.wait_ge(sem("norm_sum"), t + 1)
                if t >= 2:
                    act.wait_ge(sem("kk_done"), t - 1)
                nc.scalar.activation(inv[:, t % 2, :], nrm[t % 2][:, 0:T], ACT.Sqrt).then_inc(sem("root"), 1)


def rwkv_scan(nc, p, sig, kk, b, y, c):
    with ExitStack() as st:
        s = Stage(nc, st, "rs")
        sem = s.sem
        dirs = range(2)
        mk = lambda n, shape: [s.sb(f"{n}{d}", shape) for d in dirs]
        wide_ = lambda n: mk(n, [128, 4, 128])
        folded = lambda n: mk(n + "f", [128, 4, RC])
        E, IE = mk("E", [128, 4, RC + 1]), folded("IE")
        A, B, K, V, Vt, Kt, Bt = (wide_(n) for n in ("A", "B", "K", "V", "Vt", "Kt", "Bt"))
        X, Q, MT, S = (wide_(n) for n in ("X", "Q", "MT", "S"))
        ARf = mk("ARf", [128, 4, 2 * RC])
        Af, Rf = ([x[:, :, h * RC:(h + 1) * RC] for x in ARf] for h in range(2))
        Bf, Kf, Vtf, Lf = (folded(n) for n in ("B", "K", "Vt", "L"))
        Xf, XTf, Qf, RKTf, RBTf, Sf = (folded(n) for n in ("X", "XT", "Q", "RKT", "RBT", "S"))
        C = [[V[d], K[d]] for d in dirs]
        XT = X
        RHSf, SAnf, SAn = Kf, Qf, Q
        bank = [[s.ps(f"b{d}{j}", [128, 4, 128]) for j in range(4)] for d in dirs]
        half = [slice(64 * h, 64 * h + 64) for h in range(2)]
        sem("cleared")
        sem("zeroed")
        N = {n: [sem(f"{n}{d}") for d in dirs] for n in
             ("decay", "folded", "staged", "ab", "ba", "kar", "vt", "kt", "bt", "L", "x0", "x1", "xw", "m", "rb", "tr", "join", "q", "qs",
              "qw", "pt", "px", "xt", "xs", "xtw", "rhs", "rhss", "sa", "sas", "ys", "yr", "ss", "sadd", "snew", "sw")}
        ident, m_str_t, levels, halves = c["ident"], c["upper"], c["levels"], c["halves"]
        fold = lambda n, h: c[n][:, h * RC:(h + 1) * RC]
        low_f, inc_t_f, level1_f, level1_t_f, ident_f = (
            fold("fold0", 0), fold("fold0", 1), fold("fold1", 0), fold("fold1", 1), fold("fold2", 0))
        pairs = lambda m: bcast(m, 1, 4)
        halves_of = lambda x: x.rearrange("p a (h t) -> p a h t", h=2)
        twice = lambda x: bcast(x, 2, 2)
        blocks = halves_of(pairs(c["head_ones"]))
        F = slice(0, RC)
        LEV = 6
        UP = LEV - 1
        s.seed()
        block = st.enter_context(nc.Block())

        def steps(engine, body):
            scan_steps(engine, body, RC)

        @block.vector
        def _(dve):
            tt = nc.vector.tensor_tensor
            for d in dirs:
                for t in (S[d], Sf[d]):
                    nc.vector.memset(t[:], 0.0).then_inc(sem("zeroed"), 1)
                nc.vector.memset(E[d][:, :, 0:1], 1.0).then_inc(sem("zeroed"), 1)
            nc.vector.memset(y[:, :, :], 0.0).then_inc(sem("zeroed"), 1)
            dve.wait_ge(sem("zeroed"), 1 + 7)

            def body(seg, t0, u):
                for d in dirs:
                    v = scan_views(d, seg, t0, RC)
                    dve.wait_ge(N["decay"][d], 1 + 2 * u + 2)
                    dve.wait_ge(N["ss"][d], 1 + u)
                    fold_of = lambda x, src, w: tt(turned(d, x[d][:, :, :]), src, turned(d, w), ALU.mult)\
                        .then_inc(N["folded"][d], 1)
                    widen = lambda x, xf: tt(halves_of(x[d][:]), twice(xf[d][:, :, :]), blocks, ALU.mult)\
                        .then_inc(N["staged"][d], 1)
                    fold_of(Af, v(kk, 0), E[d][:, :, 0:RC])
                    fold_of(Bf, v(b, 0), IE[d][:])
                    fold_of(Rf, v(p, 12), E[d][:, :, 1:RC + 1])
                    fold_of(Kf, v(p, 16), IE[d][:])
                    dve.wait_ge(N["folded"][d], 1 + 4 * u + 4)
                    for x, xf in ((A, Af), (B, Bf), (K, Kf)):
                        widen(x, xf)
                    tt(turned(d, halves_of(V[d][:])), twice(v(p, 20)), bcast(bcast(halves, 1, 4), 3, RC), ALU.mult)\
                        .then_inc(N["staged"][d], 1)
                for d in dirs:
                    dve.wait_ge(N["ab"][d], 1 + u + 1)
                    tt(Lf[d][:], bank[d][0][:, :, F], pairs(low_f), ALU.mult).then_inc(N["L"][d], 1)
                    dve.wait_ge(N["ba"][d], 1 + u + 1)
                    tt(XTf[d][:], bank[d][1][:, :, F], pairs(level1_t_f), ALU.mult).then_inc(N["x0"][d], 1)
                    tt(RBTf[d][:], bank[d][1][:, :, RC:], pairs(inc_t_f), ALU.mult).then_inc(N["rb"][d], 1)
                    dve.wait_ge(N["L"][d], 1 + u + 1)
                    tt(Xf[d][:], Lf[d][:], pairs(level1_f), ALU.mult).then_inc(N["x0"][d], 1)
                    dve.wait_ge(N["x0"][d], 1 + 2 * u + 2)
                    tt(XTf[d][:], pairs(ident_f), XTf[d][:], ALU.subtract).then_inc(N["x1"][d], 1)
                    tt(Xf[d][:], pairs(ident_f), Xf[d][:], ALU.subtract).then_inc(N["x1"][d], 1)
                for d in dirs:
                    dve.wait_ge(N["kar"][d], 1 + u + 1)
                    tt(halves_of(MT[d][:]), twice(bank[d][2][:, :, F]), halves_of(pairs(m_str_t)), ALU.mult)\
                        .then_inc(N["m"][d], 1)
                    tt(RKTf[d][:], bank[d][2][:, :, RC:], pairs(inc_t_f), ALU.mult).then_inc(N["m"][d], 1)
                for l in range(1, LEV):
                    for d in dirs:
                        dve.wait_ge(N["pt"][d], 1 + UP * u + l)
                        if l == 1:
                            dve.wait_ge(N["x1"][d], 1 + 2 * u + 2)
                        else:
                            dve.wait_ge(N["xt"][d], 1 + UP * u + l - 1)
                        tt(XTf[d][:], XTf[d][:], bank[d][2][:, :, F], ALU.subtract).then_inc(N["xt"][d], 1)
                        if l < UP:
                            dve.wait_ge(N["px"][d], 1 + (UP - 1) * u + l)
                            dve.wait_ge(N["xw"][d], 1 + UP * u + l)
                            tt(Xf[d][:], Xf[d][:], bank[d][1][:, :, F], ALU.subtract).then_inc(N["xs"][d], 1)
                        else:
                            dve.wait_ge(N["xt"][d], 1 + UP * u + l)
                            tt(halves_of(XT[d][:]), twice(XTf[d][:]), blocks, ALU.mult).then_inc(N["xtw"][d], 1)
                for d in dirs:
                    v = scan_views(d, seg, t0, RC)
                    dve.wait_ge(N["ys"][d], 1 + u + 1)
                    if d:
                        dve.wait_ge(N["yr"][0], 1 + u + 1)
                    dve.wait_ge(N["yr"][d], 1 + u)
                    if not d:
                        dve.wait_ge(N["yr"][1], 1 + u)
                    yv = v(y, 0)
                    tt(yv, yv, turned(d, bank[d][3][:, :, F]), ALU.add).then_inc(N["yr"][d], 1)
                    dve.wait_ge(N["ss"][d], 1 + u + 1)
                    dve.wait_ge(N["sw"][d], 1 + u)
                    tt(Sf[d][:], Sf[d][:], bank[d][0][:, :, F], ALU.add).then_inc(N["sadd"][d], 1)
                    dve.wait_ge(N["sadd"][d], 1 + u + 1)
                    tt(Sf[d][:], Sf[d][:], bcast(E[d][:, :, RC], 2, RC), ALU.mult).then_inc(N["snew"][d], 1)
            steps(dve, body)

        @block.scalar
        def _(act):
            ac = nc.scalar.activation
            act.wait_ge(sem("zeroed"), 1 + 7)
            act.wait_ge(sem("cleared"), 1 + 2)

            def body(seg, t0, u):
                for d in dirs:
                    v = scan_views(d, seg, t0, RC)
                    act.wait_ge(N["folded"][d], 1 + 4 * u)
                    act.wait_ge(N["snew"][d], 1 + u)
                    src = v(sig, 4 * d)
                    ac(turned(d, E[d][:, :, 1:RC + 1]), src, ACT.Exp, scale=-DECAY).then_inc(N["decay"][d], 1)
                    ac(turned(d, IE[d][:]), src, ACT.Exp, scale=DECAY).then_inc(N["decay"][d], 1)
                for d in dirs:
                    for n, x, j in (("kt", Kt, 0), ("bt", Bt, 1), ("vt", Vt, 3)):
                        act.wait_ge(N[n][d], 1 + u + 1)
                        ac(x[d][:], bank[d][j][:], ACT.Copy).then_inc(N["tr"][d], 1)
                    for rows in half:
                        ac(Vtf[d][rows], bank[d][3][rows, :, rows], ACT.Copy).then_inc(N["tr"][d], 1)
                for l in range(1, LEV):
                    for d in dirs:
                        act.wait_ge(N["q"][d], 1 + UP * u + l)
                        ac(Qf[d][:], bank[d][0][:, :, F], ACT.Copy).then_inc(N["qs"][d], 1)
                        if l < UP:
                            for rows in half:
                                ac(Q[d][rows, :, rows], bank[d][0][rows, :, F], ACT.Copy).then_inc(N["qw"][d], 1)
                    if l == 1:
                        for d in dirs:
                            act.wait_ge(N["rhs"][d], 1 + u + 1)
                            ac(RHSf[d][:], bank[d][3][:, :, F], ACT.Copy).then_inc(N["rhss"][d], 1)
                for d in dirs:
                    act.wait_ge(N["sa"][d], 1 + u + 1)
                    ac(SAnf[d][:], bank[d][0][:, :, F], ACT.Copy, scale=-1.0).then_inc(N["sas"][d], 1)
                    for rows in half:
                        ac(SAn[d][rows, :, rows], bank[d][0][rows, :, F], ACT.Copy, scale=-1.0)\
                            .then_inc(N["sas"][d], 1)
            steps(act, body)

        @block.gpsimd
        def _(pool):
            tt = nc.gpsimd.tensor_tensor
            for d in dirs:
                nc.gpsimd.memset(Q[d][:], 0.0).then_inc(sem("cleared"), 1)
            pool.wait_ge(sem("cleared"), 1 + 2)

            def body(seg, t0, u):
                for l in range(1, LEV):
                    for d in dirs:
                        if l == 1:
                            pool.wait_ge(N["L"][d], 1 + u + 1)
                            pool.wait_ge(N["vt"][d], 1 + u + 1)
                            pool.wait_ge(N["kt"][d], 1 + u + 1)
                        if l > 2:
                            pool.wait_ge(N["q"][d], 1 + UP * u + l - 2)
                        tt(halves_of(C[d][l % 2][:]), twice(Lf[d][:]), halves_of(pairs(levels[:, l, :])), ALU.mult)\
                            .then_inc(N["join"][d], 1)
                    for d in dirs:
                        if l == 1:
                            pool.wait_ge(N["x1"][d], 1 + 2 * u + 2)
                        else:
                            pool.wait_ge(N["xs"][d], 1 + (UP - 1) * u + l - 1)
                        tt(halves_of(X[d][:]), twice(Xf[d][:]), blocks, ALU.mult).then_inc(N["xw"][d], 1)
                for d in dirs:
                    pool.wait_ge(N["snew"][d], 1 + u + 1)
                    tt(halves_of(S[d][:]), twice(Sf[d][:]), blocks, ALU.mult).then_inc(N["sw"][d], 1)
            steps(pool, body)

        @block.tensor
        def _(pe):
            pe.wait_ge(sem("zeroed"), 1 + 7)
            pe.wait_ge(sem("cleared"), 1 + 2)

            def each(d, j, *products):
                for q in range(4):
                    for n, (lhs, rhs) in enumerate(products):
                        width = rhs[d][:, q, :].shape[-1]
                        ins = nc.tensor.matmul(bank[d][j][:, q, 0:width], lhs[d][:, q, :], rhs[d][:, q, :],
                                               start=(n == 0), stop=(n == len(products) - 1))
                return ins

            def turn(d, j, x):
                for q in range(4):
                    ins = nc.tensor.transpose(bank[d][j][:, q, :], x[d][:, q, :], ident)
                return ins

            def body(seg, t0, u):
                for d in dirs:
                    pe.wait_ge(N["staged"][d], 1 + 4 * u + 2)
                    pe.wait_ge(N["sas"][d], 1 + 3 * u)
                    pe.wait_ge(N["snew"][d], 1 + u)
                    pe.wait_ge(N["xt"][d], 1 + UP * u)
                    each(d, 0, (A, Bf)).then_inc(N["ab"][d], 1)
                    each(d, 1, (B, ARf)).then_inc(N["ba"][d], 1)
                    pe.wait_ge(N["staged"][d], 1 + 4 * u + 4)
                    each(d, 2, (K, ARf)).then_inc(N["kar"][d], 1)
                    pe.wait_ge(N["yr"][d], 1 + u)
                    turn(d, 3, V).then_inc(N["vt"][d], 1)
                for d in dirs:
                    pe.wait_ge(N["L"][d], 1 + u + 1)
                    turn(d, 0, K).then_inc(N["kt"][d], 1)
                    pe.wait_ge(N["x0"][d], 1 + 2 * u + 1)
                    pe.wait_ge(N["rb"][d], 1 + u + 1)
                    turn(d, 1, B).then_inc(N["bt"][d], 1)
                for l in range(1, LEV):
                    for d in dirs:
                        pe.wait_ge(N["join"][d], 1 + UP * u + l)
                        if l == 1:
                            pe.wait_ge(N["x1"][d], 1 + 2 * u + 2)
                            pe.wait_ge(N["tr"][d], 1 + 5 * u + 1)
                        else:
                            pe.wait_ge(N["xt"][d], 1 + UP * u + l - 1)
                        each(d, 0, ({d: C[d][l % 2]}, XTf)).then_inc(N["q"][d], 1)
                    if l == 1:
                        for d in dirs:
                            pe.wait_ge(N["tr"][d], 1 + 5 * u + 5)
                            pe.wait_ge(N["m"][d], 1 + 2 * u + 2)
                            pe.wait_ge(N["sw"][d], 1 + u)
                            each(d, 3, (A, Sf), (MT, Vtf)).then_inc(N["rhs"][d], 1)
                    for d in dirs:
                        pe.wait_ge(N["qs"][d], 1 + UP * u + l)
                        pe.wait_ge(N["xw"][d], 1 + UP * u + l)
                        each(d, 2, (X, Qf)).then_inc(N["pt"][d], 1)
                        if l < UP:
                            pe.wait_ge(N["qw"][d], 1 + 2 * (UP - 1) * u + 2 * l)
                            each(d, 1, (Q, Xf)).then_inc(N["px"][d], 1)
                for d in dirs:
                    pe.wait_ge(N["rhss"][d], 1 + u + 1)
                    pe.wait_ge(N["xtw"][d], 1 + u + 1)
                    each(d, 0, (XT, RHSf)).then_inc(N["sa"][d], 1)
                for d in dirs:
                    pe.wait_ge(N["sas"][d], 1 + 3 * u + 3)
                    each(d, 3, (S, Rf), (Vt, RKTf), (SAn, RBTf)).then_inc(N["ys"][d], 1)
                    each(d, 0, (Kt, Vtf), (Bt, SAnf)).then_inc(N["ss"][d], 1)
            steps(pe, body)


def square_masks():
    i, j = np.arange(128)[:, None], np.arange(128)[None, :]
    same = i // 64 == j // 64
    m = {"ident": i == j, "lower": same & (i > j), "upper": same & (i < j), "upper_inc": same & (i <= j),
         "head_ones": same, "ones": i + j >= 0}
    for l in range(6):
        b = 2 << l
        m[f"level{l}"] = (i // b == j // b) & (i % b >= b // 2) & (j % b < b // 2)
    fold = lambda x: x[:, 0:64] | x[:, 64:128]
    for n, (x, y) in enumerate((("lower", m["upper_inc"]), ("level0", m["level0"].T), ("ident", m["ident"]))):
        m[f"fold{n}"] = np.concatenate([fold(m[x]), fold(y)], axis=1)
    return m


CHUNK = 128


def ssd_prepare(nc, p, dtla, col, c):
    PAD = CTX + LAT + 6
    OUT = PAD - 4
    with ExitStack() as st:
        s = Stage(nc, st, "sp")
        sem = s.sem
        xp, acc = s.sb("xp", [128, 2, PAD]), s.sb("acc", [128, 2, OUT])
        h = s.sb("h", [16, 6, T])
        na = s.sb("na", [16, 2])
        for n in ("zero", "padded", "tap0", "conv", "done", "dstep", "absd", "e", "l", "na"):
            sem(n)
        block = st.enter_context(nc.Block())

        def finish(act, i):
            y = acc[:, i % 2, :]
            act.wait_ge(sem("conv"), i + 1)
            nc.scalar.activation(p[:, 4 + i, 0:CTX], y[:, 0:CTX], ACT.Silu).then_inc(sem("done"), 1)
            nc.scalar.activation(p[:, 4 + i, CTX:T], y[:, CTX + 2:OUT], ACT.Silu).then_inc(sem("done"), 1)

        @block.scalar
        def _(act):
            nc.scalar.activation(na[:, 0:1], col("a_log", 0)[0:16], ACT.Exp).then_inc(sem("na"), 1)
            act.wait_ge(sem("dstep"), 1)
            nc.scalar.activation(h[:, 1, :], h[:, 0, :], ACT.Abs).then_inc(sem("absd"), 1)
            act.wait_ge(sem("absd"), 1)
            nc.scalar.activation(h[:, 2, :], h[:, 1, :], ACT.Exp, scale=-1.0).then_inc(sem("e"), 1)
            act.wait_ge(sem("dstep"), 2)
            nc.scalar.activation(h[:, 4, :], h[:, 3, :], ACT.Ln).then_inc(sem("l"), 1)
            act.wait_ge(sem("zero"), 2)
            for i in range(8):
                x, y = xp[:, i % 2, :], acc[:, i % 2, :]
                if i >= 2:
                    act.wait_ge(sem("conv"), i - 1)
                nc.scalar.activation(x[:, 2:2 + CTX], p[:, 4 + i, 0:CTX], ACT.Copy).then_inc(sem("padded"), 1)
                nc.scalar.activation(x[:, 4 + CTX:4 + T], p[:, 4 + i, CTX:T], ACT.Copy).then_inc(sem("padded"), 1)
                act.wait_ge(sem("padded"), 2 * i + 2)
                if i >= 2:
                    act.wait_ge(sem("done"), 2 * (i - 1))
                nc.scalar.activation(y, x[:, 0:OUT], ACT.Identity, scale=col("conv_w", i),
                                     bias=col("conv_b", i)).then_inc(sem("tap0"), 1)
                if i >= 1:
                    finish(act, i - 1)
            finish(act, 7)

        @block.vector
        def _(dve):
            k = Steps(dve, sem("dstep"))
            V = nc.vector
            for b in range(2):
                V.memset(xp[:, b, :], 0.0).then_inc(sem("zero"), 1)
            x, e, u, l, w = h[:, 0, :], h[:, 2, :], h[:, 3, :], h[:, 4, :], h[:, 5, :]
            k.did(V.tensor_scalar(x, p[0:16, 24, :], col("dt_bias", 0)[0:16], None, ALU.add))
            dve.wait_ge(sem("e"), 1)
            k.did(V.tensor_scalar(u, e, 1.0, None, ALU.add))
            k.wait()
            k.did(V.tensor_scalar(w, u, 1.0, None, ALU.is_equal))
            k.wait()
            dve.wait_ge(sem("l"), 1)
            k.did(V.tensor_tensor(l, l, w, ALU.add))
            k.did(V.scalar_tensor_tensor(w, u, -1.0, w, ALU.add, ALU.add))
            k.wait()
            k.did(V.reciprocal(w, w))
            k.wait()
            k.did(V.tensor_tensor(l, l, w, ALU.mult))
            k.wait()
            k.did(V.tensor_tensor(l, l, e, ALU.mult))
            k.wait()
            k.did(V.scalar_tensor_tensor(dtla[:, 0, :], x, 0.0, l, ALU.max, ALU.add))
            k.wait()
            dve.wait_ge(sem("na"), 1)
            k.did(V.tensor_scalar(dtla[:, 1, :], dtla[:, 0, :], na[:, 0:1], -1.0, ALU.mult, ALU.mult))
            for i in range(8):
                x, y = xp[:, i % 2, :], acc[:, i % 2, :]
                dve.wait_ge(sem("tap0"), i + 1)
                for tap in range(1, 5):
                    if tap > 1:
                        k.wait()
                    ins = V.scalar_tensor_tensor(y, x[:, tap:tap + OUT], col("conv_w", 8 * tap + i), y,
                                                 ALU.mult, ALU.add)
                    if tap < 4:
                        k.did(ins)
                    else:
                        ins.then_inc(sem("conv"), 1)


def ssd_scan(nc, p, dtla, y, c):
    with ExitStack() as st:
        s = Stage(nc, st, "ss")
        sem = s.sem
        both = lambda n, shape: [s.sb(f"{n}{d}", shape) for d in range(2)]
        Bs, Cs, Xs = both("Bs", [128, 2, 128]), both("Cs", [128, 2, 128]), both("Xs", [128, 4, 128])
        Ds = both("Ds", [16, 2, 128])
        Bt, dl = both("Bt", [128, 2, 128]), s.sb("dl", [128, 2, 16])
        xdt, xw = both("xdt", [128, 8, 64]), both("xw", [128, 8, 64])
        laU, G, Ce = s.sb("laU", [128, 8, 128]), both("G", [128, 8, 128]), both("Ce", [128, 8, 128])
        CBm, wend = s.sb("CBm", [128, 2, 128]), both("wend", [128, 16])
        H = both("H", [128, 8, 64])
        px, pb, pc = s.ps("px", [128, 4, 128]), s.ps("pb", [128, 512]), s.ps("pc", [128, 512])
        pD, pE = s.ps("pD", [128, 8, 128]), s.ps("pE", [128, 8, 128])
        py = s.ps("py", [128, 4, 128])
        for n in ("zero", "st", "tr", "ev", "xdt", "lau", "sums", "cb", "exps", "cbm", "G", "Ce", "xw",
                  "y", "yr", "state", "hm", "h"):
            sem(n)
        s.seed()
        block = st.enter_context(nc.Block())

        @block.vector
        def _(dve):
            V = nc.vector
            for d in range(2):
                V.memset(H[d][:], 0.0).then_inc(sem("zero"), 1)
            V.memset(y[:, :, :], 0.0).then_inc(sem("zero"), 1)
            dve.wait_ge(sem("zero"), 1 + 3)

            def body(seg, t0, u):
                for d in range(2):
                    v = u * 2 + d
                    heads = slice(8 * d, 8 * d + 8)
                    dve.wait_ge(sem("tr"), 1 + 2 * v + 2)
                    dve.wait_ge(sem("ev"), 1 + 2 * v + 2)
                    dve.wait_ge(sem("state"), 1 + 2 * u)
                    dve.wait_ge(sem("sums"), 1 + 2 * v)
                    V.tensor_tensor(xdt[d][:], px[:].rearrange("p a (b c) -> p (a b) c", b=2),
                                    bcast(dl[:, 0, heads], 2, 64), ALU.mult).then_inc(sem("xdt"), 1)
                    V.tensor_tensor(laU[:], bcast(c["upper_inc128"], 1, 8), bcast(dl[:, 1, heads], 2, 128),
                                    ALU.mult).then_inc(sem("lau"), 1)
                    dve.wait_ge(sem("cb"), 1 + v + 1)
                    V.tensor_tensor(CBm[:], px[:, 0:2, :],
                                    bcast(c["upper_inc128"], 1, 2), ALU.mult).then_inc(sem("cbm"), 1)
                    dve.wait_ge(sem("exps"), 1 + 3 * v + 3)
                    dve.wait_ge(sem("cbm"), 1 + v + 1)
                    dve.wait_ge(sem("xdt"), 1 + v + 1)
                    g4 = lambda x: x[:].rearrange("p (g r) i -> p g r i", g=2)
                    V.tensor_tensor(g4(G[d]), g4(G[d]), bcast(CBm[:], 2, 4), ALU.mult).then_inc(sem("G"), 1)
                    V.tensor_tensor(g4(Ce[d]), g4(Ce[d]), bcast(Cs[d][:], 2, 4), ALU.mult).then_inc(sem("Ce"), 1)
                    V.tensor_tensor(xw[d][:], xdt[d][:], bcast(wend[d][:, 0:8], 2, 64), ALU.mult).then_inc(sem("xw"), 1)
                for d in range(2):
                    v = u * 2 + d
                    view = scan_views(d, seg, t0, CHUNK)
                    dve.wait_ge(sem("y"), 1 + v + 1)
                    dve.wait_ge(sem("yr"), 1 + v)
                    yv = view(y, 0, 4)
                    V.tensor_tensor(yv, yv, turned(d, py[:]), ALU.add).then_inc(sem("yr"), 1)
                    V.tensor_tensor(H[d][:], H[d][:], bcast(wend[d][:, 8:16], 2, 64), ALU.mult).then_inc(sem("hm"), 1)
                    dve.wait_ge(sem("hm"), 1 + v + 1)
                    dve.wait_ge(sem("state"), 1 + v + 1)
                    V.tensor_tensor(H[d][:], H[d][:], pb[:].rearrange("p (h c) -> p h c", h=8), ALU.add)\
                        .then_inc(sem("h"), 1)
            scan_steps(dve, body, CHUNK)

        @block.gpsimd
        def _(pool):
            def body(seg, t0, u):
                for d in range(2):
                    v = u * 2 + d
                    view = scan_views(d, seg, t0, CHUNK)
                    pool.wait_ge(sem("cb"), 1 + 2 * u)
                    pool.wait_ge(sem("Ce"), 1 + 2 * u)
                    P = nc.gpsimd
                    P.tensor_copy(turned(d, Ds[d][:]), view(dtla, 0, 2)).then_inc(sem("st"), 1)
                    P.tensor_copy(turned(d, Xs[d][:]), view(p, 4, 4)).then_inc(sem("st"), 1)
                    P.tensor_copy(turned(d, Bs[d][:]), view(p, 8, 2)).then_inc(sem("st"), 1)
                    P.tensor_copy(turned(d, Cs[d][:]), view(p, 10, 2)).then_inc(sem("st"), 1)
            scan_steps(pool, body, CHUNK)

        @block.scalar
        def _(act):
            A = nc.scalar.activation

            def body(seg, t0, u):
                for d in range(2):
                    v = u * 2 + d
                    act.wait_ge(sem("tr"), 1 + 2 * v + 1)
                    act.wait_ge(sem("sums"), 1 + 2 * v)
                    act.wait_ge(sem("lau"), 1 + v)
                    act.wait_ge(sem("xdt"), 1 + v)
                    A(dl[:], pc[:, 256:288].rearrange("p (a b) -> p a b", a=2), ACT.Copy).then_inc(sem("ev"), 1)
                    act.wait_ge(sem("tr"), 1 + 2 * v + 2)
                    act.wait_ge(sem("state"), 1 + 2 * u)
                    A(Bt[d][:], pb[:, 0:256].rearrange("p (a b) -> p a b", a=2), ACT.Copy).then_inc(sem("ev"), 1)
                    act.wait_ge(sem("sums"), 1 + 2 * v + 2)
                    act.wait_ge(sem("hm"), 1 + 2 * u)
                    act.wait_ge(sem("xw"), 1 + 2 * u)
                    A(wend[d][:], pc[:, 288:304], ACT.Exp).then_inc(sem("exps"), 1)
                    act.wait_ge(sem("y"), 1 + 2 * u)
                    A(G[d][:], pD[:], ACT.Exp).then_inc(sem("exps"), 1)
                    A(Ce[d][:], pE[:], ACT.Exp).then_inc(sem("exps"), 1)
            scan_steps(act, body, CHUNK)

        @block.tensor
        def _(pe):
            mm = nc.tensor.matmul
            pe.wait_ge(sem("zero"), 1 + 3)

            def body(seg, t0, u):
                for d in range(2):
                    v = u * 2 + d
                    heads = slice(8 * d, 8 * d + 8)
                    pe.wait_ge(sem("st"), 1 + 4 * v + 4)
                    pe.wait_ge(sem("cbm"), 1 + v)
                    pe.wait_ge(sem("exps"), 1 + 3 * v)
                    pe.wait_ge(sem("xdt"), 1 + v)
                    if d == 0:
                        pe.wait_ge(sem("h"), 1 + v)
                    else:
                        pe.wait_ge(sem("ev"), 1 + 2 * v)
                    for a in range(4):
                        nc.tensor.transpose(px[:, a, :], Xs[d][:, a, :], c["ident"])
                    for a in range(2):
                        ins = nc.tensor.transpose(pc[:, 256 + 16 * a:272 + 16 * a], Ds[d][:, a, :], c["ident"][0:16, 0:16])
                    ins.then_inc(sem("tr"), 1)
                    for g in range(2):
                        ins = nc.tensor.transpose(pb[:, g * 128:(g + 1) * 128], Bs[d][:, g, :], c["ident"])
                    ins.then_inc(sem("tr"), 1)
                    pe.wait_ge(sem("ev"), 1 + 2 * v + 1)
                    mm(pc[:, 288:296], c["lower128"], dl[:, 1, heads], start=True, stop=True)
                    mm(pc[:, 296:304], c["ones"], dl[:, 1, heads], start=True, stop=True).then_inc(sem("sums"), 1)
                    pe.wait_ge(sem("lau"), 1 + v + 1)
                    for g in range(2):
                        mm(pD[:, 4 * g:4 * g + 4, :], c["lower128"], laU[:, 4 * g:4 * g + 4, :], start=True, stop=True)
                        ins = mm(pE[:, 4 * g:4 * g + 4, :], c["ones"], laU[:, 4 * g:4 * g + 4, :], start=True, stop=True)
                    ins.then_inc(sem("sums"), 1)
                    pe.wait_ge(sem("xdt"), 1 + v + 1)
                    for g in range(2):
                        ins = mm(px[:, g, :], Bs[d][:, g, :], Cs[d][:, g, :], start=True, stop=True)
                    ins.then_inc(sem("cb"), 1)
                for d in range(2):
                    v = u * 2 + d
                    pe.wait_ge(sem("G"), 1 + v + 1)
                    pe.wait_ge(sem("Ce"), 1 + v + 1)
                    pe.wait_ge(sem("yr"), 1 + v)
                    for h in range(8):
                        o = py[64 * (h % 2):64 * (h % 2) + 64, h // 2, :]
                        mm(o, xdt[d][:, h, :], G[d][:, h, :], start=True, stop=False)
                        ins = mm(o, H[d][:, h, :], Ce[d][:, h, :], start=False, stop=True)
                    ins.then_inc(sem("y"), 1)
                    pe.wait_ge(sem("xw"), 1 + v + 1)
                    if d == 0:
                        pe.wait_ge(sem("ev"), 1 + 2 * v + 4)
                    else:
                        pe.wait_ge(sem("h"), 1 + v)
                    for g in range(2):
                        ins = mm(pb[:, g * 256:(g + 1) * 256], Bt[d][:, g, :], xw[d][:, 4 * g:4 * g + 4, :],
                                 start=True, stop=True)
                    ins.then_inc(sem("state"), 1)
            scan_steps(pe, body, CHUNK)


def gla_prepare(nc, p, sp, col, w_up, c):
    with ExitStack() as st:
        s = Stage(nc, st, "gp")
        sem = s.sem
        up = s.sb("up", [128, 512])
        za, zb, zc = s.sb("za", [128, T]), s.sb("zb", [128, T]), s.sb("zc", [128, T])
        acc = s.ps("acc", [128, 1024])
        for n in ("up", "z", "x", "abs", "e", "l", "sp", "scan"):
            sem(n)
        block = st.enter_context(nc.Block())

        @block.sync
        def _(sync):
            sync.dma_start(up[32:48, :], w_up).then_inc(sem("up"), 16)

        @block.tensor
        def _(pe):
            pe.wait_ge(sem("up"), 16)
            for i in range(4):
                pe.wait_ge(sem("x"), i)
                for t0, tn in ((0, 512), (512, 256)):
                    ins = nc.tensor.matmul(acc[:, t0:t0 + tn], up[32:48, 128 * i:128 * i + 128],
                                           p[32:48, 24, t0:t0 + tn], start=True, stop=True)
                ins.then_inc(sem("z"), 1)

        @block.scalar
        def _(act):
            A = nc.scalar.activation
            for i in range(4):
                act.wait_ge(sem("x"), i + 1)
                act.wait_ge(sem("sp"), i)
                A(zb[:, :], za[:, :], ACT.Abs).then_inc(sem("abs"), 1)
                act.wait_ge(sem("abs"), i + 1)
                A(zb[:, :], zb[:, :], ACT.Exp, scale=-1.0).then_inc(sem("e"), 1)
                act.wait_ge(sem("e"), i + 1)
                A(zc[:, :], zb[:, :], ACT.Ln, bias=1.0).then_inc(sem("l"), 1)

        @block.vector
        def _(dve):
            V = nc.vector
            for i in range(4):
                dve.wait_ge(sem("z"), i + 1)
                dve.wait_ge(sem("sp"), i)
                V.tensor_scalar(za[:, :], acc[:, 0:T], col("gk_b", i), -1.0, ALU.add, ALU.mult)\
                    .then_inc(sem("x"), 1)
                dve.wait_ge(sem("l"), i + 1)
                V.scalar_tensor_tensor(sp[:, i, :], za[:, :], 0.0, zc[:, :], ALU.max, ALU.add)\
                    .then_inc(sem("sp"), 1)
                dve.wait_ge(sem("sp"), i + 1)
                x = sp[:, i, :] if i < 2 else sp[:, i, ::-1]
                V.tensor_tensor_scan(x, c["chunk_mask128"], x, 0.0, ALU.mult, ALU.add).then_inc(sem("scan"), 1)


def gla_scan(nc, p, sp, y, c):
    LEV = 7
    with ExitStack() as st:
        s = Stage(nc, st, "gs")
        sem = s.sem
        both = lambda n, shape: [s.sb(f"{n}{d}", shape) for d in range(2)]
        Ps = both("Ps", [128, 2, 128])
        qk = list(zip(both("qs", [128, 2, 128]), both("ks", [128, 2, 128])))
        Vs, Vt = s.sb("Vs", [128, 4, 128]), s.sb("Vt", [128, 4, 128])
        Dl, QL, KL = (both(n, [128, LEV, 256]) for n in ("Dl", "QL", "KL"))
        ew = both("ew", [128, 2, 256])
        qe, ke = both("qe", [128, 2, 128]), both("ke", [128, 2, 128])
        pend = both("pend", [128, 2])
        kt = s.sb("kt", [128, 2, 128])
        tick = s.sb("tick", [128, 1])
        att = s.sb("att", [128, 2, 2, 128])
        S = both("S", [128, 2, 128])
        pv, pk_ = s.ps("pv", [128, 4, 128]), s.ps("pk", [128, 4, 128])
        pS = pk_[:, 2:4, :]
        py = s.ps("py", [128, 2, 4, 128])
        pl = [s.ps(f"pl{i}", [128, 2, 4, 128]) for i in range(2)]
        for n in ("zero", "ps", "qk", "vs", "dl", "abs", "el", "ql", "kl", "ds", "ew", "pend", "qe", "ke", "trv",
                  "trk", "vt", "kt", "lev", "att", "y", "yr", "state", "sm", "snew"):
            sem(n)
        s.seed()
        block = st.enter_context(nc.Block())
        LV = LEV + 1

        @block.gpsimd
        def _(pool):
            P = nc.gpsimd

            def body(seg, t0, u):
                for d in range(2):
                    v = u * 2 + d
                    view = scan_views(d, seg, t0, CHUNK)
                    pool.wait_ge(sem("trv"), 1 + v)
                    P.tensor_copy(turned(d, Vs[:]), view(p, 16, 4)).then_inc(sem("vs"), 1)
                    pool.wait_ge(sem("el"), 1 + v + 1)
                    pool.wait_ge(sem("qk"), 1 + 2 * v + 2)
                    pool.wait_ge(sem("lev"), 1 + LV * 2 * u)
                    P.tensor_tensor(KL[d][:], bcast(qk[d][1][:].rearrange("p a t -> p (a t)"), 1, LEV), Dl[d][:], ALU.mult)\
                        .then_inc(sem("kl"), 1)
            scan_steps(pool, body, CHUNK)

        @block.scalar
        def _(act):
            A = nc.scalar.activation

            def body(seg, t0, u):
                for d in range(2):
                    v = u * 2 + d
                    view = scan_views(d, seg, t0, CHUNK)
                    act.wait_ge(sem("ds"), 1 + 2 * u)
                    act.wait_ge(sem("pend"), 1 + 2 * u)
                    act.wait_ge(sem("ew"), 1 + 2 * u)
                    A(turned(d, Ps[d][:]), view(sp, 2 * d, 2), ACT.Copy).then_inc(sem("ps"), 1)
                    act.wait_ge(sem("lev"), 1 + LV * 2 * u)
                    act.wait_ge(sem("ql"), 1 + 2 * u)
                    act.wait_ge(sem("kl"), 1 + 2 * u)
                    act.wait_ge(sem("ke"), 1 + 2 * u)
                    A(turned(d, qk[d][0][:]), view(p, 12, 2), ACT.Copy, scale=0.125).then_inc(sem("qk"), 1)
                    A(turned(d, qk[d][1][:]), view(p, 14, 2), ACT.Copy).then_inc(sem("qk"), 1)
                    act.wait_ge(sem("dl"), 1 + LEV * (v + 1))
                    A(Dl[d][:], Dl[d][:], ACT.Abs).then_inc(sem("abs"), 1)
                    act.wait_ge(sem("ds"), 1 + v + 1)
                    act.wait_ge(sem("ps"), 1 + v + 1)
                    A(ew[d][:, 0, :], Ps[d][:].rearrange("p a t -> p (a t)"), ACT.Exp, scale=-1 / 16)
                    act.wait_ge(sem("sm"), 1 + 2 * u)
                    A(pend[d][:, :], Ps[d][:, :, 127], ACT.Exp, scale=-1 / 16).then_inc(sem("pend"), 1)
                    A(ew[d][:, 1, :], ew[d][:, 1, :], ACT.Exp, scale=-1 / 16).then_inc(sem("ew"), 1)
                    act.wait_ge(sem("abs"), 1 + v + 1)
                    A(Dl[d][:], Dl[d][:], ACT.Exp, scale=-1 / 16).then_inc(sem("el"), 1)
                for d in range(2):
                    v = u * 2 + d
                    act.wait_ge(sem("trv"), 1 + v + 1)
                    act.wait_ge(sem("state"), 1 + v)
                    A(Vt[:], pv[:], ACT.Copy).then_inc(sem("vt"), 1)
                    act.wait_ge(sem("trk"), 1 + v + 1)
                    A(kt[:], pk_[:, 0:2, :], ACT.Copy).then_inc(sem("kt"), 1)
            scan_steps(act, body, CHUNK)

        @block.vector
        def _(dve):
            V = nc.vector
            for d in range(2):
                V.memset(S[d][:], 0.0).then_inc(sem("zero"), 1)
            V.memset(y[:, :, :], 0.0).then_inc(sem("zero"), 1)
            V.memset(att[:], 0.0).then_inc(sem("zero"), 1)
            dve.wait_ge(sem("zero"), 1 + 4)
            flat = lambda x: x[:].rearrange("p a t -> p (a t)")

            def body(seg, t0, u):
                for d in range(2):
                    v = u * 2 + d
                    dve.wait_ge(sem("ps"), 1 + v + 1)
                    dve.wait_ge(sem("kl"), 1 + 2 * u)
                    dve.wait_ge(sem("ql"), 1 + 2 * u)
                    for l in range(LEV):
                        b = 1 << l
                        blocks = flat(Ps[d]).rearrange("p (n w) -> p n w", w=2 * b)
                        V.tensor_tensor(Dl[d][:, l, :].rearrange("p (n w) -> p n w", w=2 * b), blocks,
                                        bcast(blocks[:, :, b - 1], 2, 2 * b), ALU.subtract).then_inc(sem("dl"), 1)
                    dve.wait_ge(sem("ke"), 1 + 2 * u)
                    V.tensor_tensor(ew[d][:, 1, :].rearrange("p (a t) -> p a t", a=2), bcast(Ps[d][:, :, 127], 2, 128), Ps[d][:],
                                    ALU.subtract).then_inc(sem("ds"), 1)
                    dve.wait_ge(sem("el"), 1 + v + 1)
                    dve.wait_ge(sem("qk"), 1 + 2 * v + 2)
                    dve.wait_ge(sem("lev"), 1 + LV * 2 * u)
                    V.tensor_tensor(QL[d][:], bcast(flat(qk[d][0]), 1, LEV), Dl[d][:], ALU.mult).then_inc(sem("ql"), 1)
                    dve.wait_ge(sem("ew"), 1 + v + 1)
                    dve.wait_ge(sem("y"), 1 + 2 * u)
                    dve.wait_ge(sem("trk"), 1 + 2 * u)
                    V.tensor_tensor(flat(qe[d]), flat(qk[d][0]), ew[d][:, 0, :], ALU.mult).then_inc(sem("qe"), 1)
                    V.tensor_tensor(flat(ke[d]), flat(qk[d][1]), ew[d][:, 1, :], ALU.mult).then_inc(sem("ke"), 1)
                for d in range(2):
                    v = u * 2 + d
                    view = scan_views(d, seg, t0, CHUNK)
                    for l in range(LV):
                        dve.wait_ge(sem("lev"), 1 + LV * v + l + 1)
                        dve.wait_ge(sem("att"), 1 + LV * v + l)
                        V.memset(tick[:, :], 0.0)
                        V.copy_predicated(att[:], bcast(bcast(c["pair_level"][:, l, :], 1, 2), 1, 2)
                                          .bitcast(mybir.dt.int32), pl[l % 2][:, :, 0:2, :]).then_inc(sem("att"), 1)
                    dve.wait_ge(sem("y"), 1 + v + 1)
                    dve.wait_ge(sem("yr"), 1 + v)
                    yv = view(y, 0, 4).rearrange("p (t b) i -> p b t i", b=2)
                    V.tensor_tensor(yv, yv, turned(d, py[:, :, 0:2, :]), ALU.add).then_inc(sem("yr"), 1)
                    dve.wait_ge(sem("pend"), 1 + v + 1)
                    V.tensor_tensor(S[d][:], S[d][:], bcast(pend[d][:, :], 2, 128), ALU.mult).then_inc(sem("sm"), 1)
                    dve.wait_ge(sem("sm"), 1 + v + 1)
                    dve.wait_ge(sem("state"), 1 + v + 1)
                    V.tensor_tensor(S[d][:], S[d][:], pS, ALU.add).then_inc(sem("snew"), 1)
            scan_steps(dve, body, CHUNK)

        @block.tensor
        def _(pe):
            mm = nc.tensor.matmul
            pe.wait_ge(sem("zero"), 1 + 4)

            def body(seg, t0, u):
                for d in range(2):
                    v = u * 2 + d
                    pe.wait_ge(sem("vs"), 1 + v + 1)
                    pe.wait_ge(sem("vt"), 1 + v)
                    for h in range(4):
                        ins = nc.tensor.transpose(pv[:, h, :], Vs[:, h, :], c["ident"])
                    ins.then_inc(sem("trv"), 1)
                    for l in range(LV):
                        if l == 0:
                            pe.wait_ge(sem("qk"), 1 + 2 * v + 2)
                            pe.wait_ge(sem("att"), 1 + LV * v)
                        elif l == 1:
                            pe.wait_ge(sem("ql"), 1 + v + 1)
                            pe.wait_ge(sem("kl"), 1 + v + 1)
                        if l >= 2:
                            pe.wait_ge(sem("att"), 1 + LV * v + l - 1)
                        for h in range(4):
                            rows, t = slice(64 * (h % 2), 64 * (h % 2) + 64), h // 2
                            if l == 0:
                                k, q = qk[d][1][rows, t, :], qk[d][0][rows, t, :]
                            else:
                                cols = slice(128 * t, 128 * t + 128)
                                k, q = KL[d][rows, l - 1, cols], QL[d][rows, l - 1, cols]
                            ins = mm(pl[l % 2][:, h % 2, t, :], k, q, start=True, stop=True)
                        ins.then_inc(sem("lev"), 1)
                    pe.wait_ge(sem("ke"), 1 + v + 1)
                    pe.wait_ge(sem("snew"), 1 + v)
                    for t in range(2):
                        ins = nc.tensor.transpose(pk_[:, t, :], ke[d][:, t, :], c["ident"])
                    ins.then_inc(sem("trk"), 1)
                    pe.wait_ge(sem("snew"), 1 + v)
                    pe.wait_ge(sem("qe"), 1 + v + 1)
                    pe.wait_ge(sem("vt"), 1 + v + 1)
                    pe.wait_ge(sem("att"), 1 + LV * (v + 1))
                    pe.wait_ge(sem("yr"), 1 + v)
                    for h in range(4):
                        rows, t = slice(64 * (h % 2), 64 * (h % 2) + 64), h // 2
                        mm(py[:, h % 2, t, :], Vt[:, h, :], att[:, h % 2, t, :], start=True, stop=False)
                        ins = mm(py[:, h % 2, t, :], S[d][rows, t, :], qe[d][rows, t, :], start=False, stop=True)
                    ins.then_inc(sem("y"), 1)
                    pe.wait_ge(sem("kt"), 1 + v + 1)
                    for h in range(4):
                        rows, t = slice(64 * (h % 2), 64 * (h % 2) + 64), h // 2
                        ins = mm(pS[rows, t, :], kt[:, t, rows], Vt[:, h, :], start=True, stop=True)
                    ins.then_inc(sem("state"), 1)
            scan_steps(pe, body, CHUNK)


def chunk_masks():
    j, i = np.arange(128)[:, None], np.arange(128)[None, :]
    m = {"upper_inc128": j <= i, "lower128": j > i, "pair0": j == i}
    for l in range(7):
        b = 2 << l
        m[f"pair{l + 1}"] = (i // b == j // b) & (j % b < b // 2) & (i % b >= b // 2)
    return m


KEYS = T // 128
LAM_INIT = 0.8 - 0.6 * math.exp(-0.3 * 0)


def rope(nc, p, w_rope, c):
    with ExitStack() as st:
        s = Stage(nc, st, "ro")
        sem = s.sem
        tab = s.sb("tab", [128, 2, LAT])
        tmp = s.sb("tmp", [128, 2, LAT])
        acc = [s.ps(f"acc{i}", [128, LAT]) for i in range(2)]
        for n in ("tab", "rot", "sin", "cos", "done"):
            sem(n)
        block = st.enter_context(nc.Block())

        @block.sync
        def _(sp):
            sp.dma_start(tab[:], w_rope).then_inc(sem("tab"), 16)

        @block.tensor
        def _(pe):
            for i in range(8):
                if i >= 2:
                    pe.wait_ge(sem("sin"), i - 1)
                nc.tensor.matmul(acc[i % 2][:, :], c["rot"], p[:, i, CTX:T], start=True, stop=True)\
                    .then_inc(sem("rot"), 1)

        @block.vector
        def _(dve):
            dve.wait_ge(sem("tab"), 16)
            for i in range(8):
                x, y = p[:, i, CTX:T], tmp[:, i % 2, :]
                dve.wait_ge(sem("rot"), i + 1)
                if i >= 2:
                    dve.wait_ge(sem("done"), i - 1)
                nc.vector.tensor_tensor(y, acc[i % 2][:, :], tab[:, 1, :], ALU.mult).then_inc(sem("sin"), 1)
                nc.vector.tensor_tensor(x, x, tab[:, 0, :], ALU.mult).then_inc(sem("cos"), 1)
                dve.wait_ge(sem("sin"), i + 1)
                dve.wait_ge(sem("cos"), i + 1)
                nc.vector.tensor_tensor(x, x, y, ALU.add).then_inc(sem("done"), 1)


def diff_attention(nc, p, out, w_lam, c):
    HEADS = 4
    with ExitStack() as st:
        s = Stage(nc, st, "da")
        sem = s.sem
        lam, prod, elam, neglam = s.sb("lam", [64, 4]), s.sb("prod", [64, 2]), s.sb("elam", [128, 2]), s.sb("neglam", [128, 1])
        vt = s.sb("vt", [128, KEYS, 4, 128])
        qm = s.sb("qm", [128, HEADS, 2, 128])
        mx, nb = s.sb("mx", [128, 2]), s.sb("nb", [128, 2])
        P, W = s.sb("P", [128, 2, 2, T]), s.sb("W", [128, 2, T])
        rs, rr = s.sb("rs", [128, 2, 2]), s.sb("rr", [128, 2])
        WT = s.sb("WT", [128, KEYS, 128])
        score = s.ps("score", [128, 2, 1024])
        pt = s.ps("pt", [128, 8, 128])
        po = s.ps("po", [128, HEADS, 128])
        for n in ("lam", "prod", "plam", "elam", "neglam", "vtr", "vt", "q", "s", "mx", "nb", "exp", "rr0",
                  "rr", "w0", "w", "tr", "wt", "o", "or"):
            sem(n)
        s.seed()
        block = st.enter_context(nc.Block())

        def runs(engine, body):
            for base, n, keys, u0 in ((0, CTX, CTX // 128, 0), (CTX, LAT, KEYS, CTX // 128)):
                with engine.Fori(0, n // 128) as i:
                    body(base, i * 128, keys, (i + u0) * HEADS, i + u0)

        @block.sync
        def _(sp):
            sp.dma_start(lam[:, :], w_lam).then_inc(sem("lam"), 16)

        @block.gpsimd
        def _(pool):
            def body(base, t0, keys, u, r):
                pool.wait_ge(sem("elam"), 1 + 1)
                pool.wait_ge(sem("s"), 1 + 2 * u)
                q = p[:, 0:HEADS, base:T][:, :, bass.ds(t0, 128)]
                for m in range(2):
                    nc.gpsimd.tensor_tensor(qm[:, :, m, :], q, bcast(bcast(c["halves"][:, m], 1, HEADS), 2, 128),
                                            ALU.mult).then_inc(sem("q"), 1)
            runs(pool, body)

        @block.tensor
        def _(pe):
            mm = nc.tensor.matmul
            pe.wait_ge(sem("prod"), 1 + 1)
            mm(po[:, 0, 0:2], c["ones"][0:64, :], prod[:, :], start=True, stop=True).then_inc(sem("plam"), 1)
            for k in range(KEYS):
                if k >= 2:
                    pe.wait_ge(sem("vt"), 1 + k - 1)
                for h in range(4):
                    ins = nc.tensor.transpose(pt[:, 4 * (k % 2) + h, :], p[:, 8 + h, 128 * k:128 * k + 128], c["ident"])
                ins.then_inc(sem("vtr"), 1)
            pe.wait_ge(sem("vt"), 1 + KEYS)
            pe.wait_ge(sem("elam"), 1 + 1)

            def scores(base, t0, keys, u, r, h):
                if h == 0:
                    pe.wait_ge(sem("q"), 1 + 2 * r + 2)
                for m in range(2):
                    pe.wait_ge(sem("exp"), 1 + 2 * (u + h) + (m - 1 if h else 0))
                    for k0 in range(0, keys * 128, 512):
                        kn = min(512, keys * 128 - k0)
                        ins = mm(score[:, m, k0:k0 + kn], qm[:, h, m, :], p[:, 4 + h, k0:k0 + kn], start=True, stop=True)
                    ins.then_inc(sem("s"), 1)

            def apply(base, t0, keys, u, r, h):
                pe.wait_ge(sem("w"), 1 + u + h + 1)
                pe.wait_ge(sem("wt"), 1 + u + h)
                for k in range(keys):
                    ins = nc.tensor.transpose(pt[:, k, :], W[:, h % 2, 128 * k:128 * k + 128], c["ident"])
                ins.then_inc(sem("tr"), 1)
                pe.wait_ge(sem("wt"), 1 + u + h + 1)
                if h == 0:
                    pe.wait_ge(sem("or"), 1 + r)
                for k in range(keys):
                    ins = mm(po[:, h, :], vt[:, k, h, :], WT[:, k, :], start=(k == 0), stop=(k == keys - 1))
                ins.then_inc(sem("o"), 1)

            def body(*a):
                scores(*a, 0)
                for h in range(1, HEADS):
                    scores(*a, h)
                    apply(*a, h - 1)
                apply(*a, HEADS - 1)
            runs(pe, body)

        @block.vector
        def _(dve):
            V = nc.vector
            dve.wait_ge(sem("lam"), 1 + 16)
            V.tensor_tensor(prod[:, :], lam[:, 0:2], lam[:, 2:4], ALU.mult).then_inc(sem("prod"), 1)
            dve.wait_ge(sem("elam"), 1 + 1)
            V.scalar_tensor_tensor(neglam[:, :], elam[:, 1:2], -LAM_INIT, elam[:, 0:1], ALU.add, ALU.subtract)\
                .then_inc(sem("neglam"), 1)
            dve.wait_ge(sem("neglam"), 1 + 1)

            def body(base, t0, keys, u, r):
                for h in range(HEADS):
                    n = keys * 128
                    g = u + h
                    for m in range(2):
                        one = slice(m, m + 1)
                        dve.wait_ge(sem("s"), 1 + 2 * g + m + 1)
                        dve.wait_ge(sem("nb"), 1 + 2 * g)
                        V.tensor_reduce(mx[:, one], score[:, m, 0:n], AX.X, ALU.max, negate=True).then_inc(sem("mx"), 1)
                        dve.wait_ge(sem("mx"), 1 + 2 * g + m + 1)
                        dve.wait_ge(sem("exp"), 1 + 2 * g)
                        V.tensor_scalar(nb[:, one], mx[:, one], 0.125, None, ALU.mult).then_inc(sem("nb"), 1)
                    dve.wait_ge(sem("exp"), 1 + 2 * g + 2)
                    dve.wait_ge(sem("w"), 1 + g)
                    V.reciprocal(rr[:, :], rs[:, h % 2, :]).then_inc(sem("rr0"), 1)
                    dve.wait_ge(sem("rr0"), 1 + g + 1)
                    V.tensor_tensor(rr[:, 1:2], rr[:, 1:2], neglam[:, :], ALU.mult).then_inc(sem("rr"), 1)
                    if h < 2:
                        dve.wait_ge(sem("tr"), 1 + u)
                    else:
                        dve.wait_ge(sem("tr"), 1 + u + h - 1)
                    V.tensor_scalar(W[:, h % 2, 0:n], P[:, h % 2, 0, 0:n], rr[:, 0:1], None, ALU.mult).then_inc(sem("w0"), 1)
                    dve.wait_ge(sem("rr"), 1 + g + 1)
                    dve.wait_ge(sem("w0"), 1 + g + 1)
                    V.scalar_tensor_tensor(W[:, h % 2, 0:n], P[:, h % 2, 1, 0:n], rr[:, 1:2], W[:, h % 2, 0:n],
                                           ALU.mult, ALU.add).then_inc(sem("w"), 1)
            runs(dve, body)

        @block.scalar
        def _(act):
            A = nc.scalar.activation
            act.wait_ge(sem("plam"), 1 + 1)
            A(elam[:, :], po[:, 0, 0:2], ACT.Exp).then_inc(sem("elam"), 1)
            for k in range(KEYS):
                act.wait_ge(sem("vtr"), 1 + k + 1)
                A(vt[:, k], pt[:, 4 * (k % 2):4 * (k % 2) + 4, :], ACT.Copy).then_inc(sem("vt"), 1)

            def exps(base, t0, keys, u, r, h):
                n = keys * 128
                if h < 2:
                    act.wait_ge(sem("w"), 1 + u)
                else:
                    act.wait_ge(sem("w"), 1 + u + h - 1)
                for m in range(2):
                    act.wait_ge(sem("nb"), 1 + 2 * (u + h) + m + 1)
                    A(P[:, h % 2, m, 0:n], score[:, m, 0:n], ACT.Exp, scale=0.125, bias=nb[:, m:m + 1],
                      accum_out=rs[:, h % 2, m:m + 1]).then_inc(sem("exp"), 1)

            def turned(base, t0, keys, u, r, h):
                act.wait_ge(sem("tr"), 1 + u + h + 1)
                act.wait_ge(sem("o"), 1 + u + h)
                A(WT[:, 0:keys, :], pt[:, 0:keys, :], ACT.Copy).then_inc(sem("wt"), 1)

            def body(base, t0, keys, u, r):
                a = (base, t0, keys, u, r)
                exps(*a, 0)
                for h in range(1, HEADS):
                    exps(*a, h)
                    turned(*a, h - 1)
                turned(*a, HEADS - 1)
                act.wait_ge(sem("o"), 1 + u + HEADS)
                A(out[:, 0:HEADS, base:T][:, :, bass.ds(t0, 128)], po[:], ACT.Copy).then_inc(sem("or"), 1)
            runs(act, body)


def rms(nc, name, src, dst, groups, parts, ones, n, eps, gain, shift=None, gate=None, silu_src=None):
    tn_max = max(tn for _, tn in parts)
    with ExitStack() as st:
        s = Stage(nc, st, name)
        sem = s.sem
        sq = s.sb("sq", [128, 2, tn_max])
        r = s.sb("r", [128, 2, tn_max])
        act_g = s.sb("gt", [128, 2, tn_max]) if silu_src is not None else None
        acc = [s.ps(f"acc{i}", [128, 512]) for i in range(2)]
        for k in ("sq", "sum", "root", "inv", "out", "shifted", "silu", "gated"):
            sem(k)
        work = [(g, p) for g in range(len(groups)) for p in range(len(parts))]
        order, i = [], 0
        for w, (g, p) in enumerate(work):
            for k, tile in enumerate(groups[g]):
                order.append((i, w, k, tile, len(groups[g]), parts[p], p))
                i += 1
        block = st.enter_context(nc.Block())
        last = lambda w: max(o[0] for o in order if o[1] == w)

        @block.scalar
        def _(act):
            for i, w, k, tile, m, (t0, tn), p in order:
                if i >= 2:
                    act.wait_ge(sem("sum"), i - 1)
                nc.scalar.activation(sq[:, i % 2, 0:tn], src(tile, t0, tn), ACT.Square).then_inc(sem("sq"), 1)
                if k == m - 1:
                    act.wait_ge(sem("sum"), i + 1)
                    if w >= 2:
                        act.wait_ge(sem("out"), last(w - 2) + 1)
                    nc.scalar.activation(r[:, w % 2, 0:tn], acc[w % 2][:, 0:tn], ACT.Sqrt, scale=1.0 / n,
                                         bias=eps).then_inc(sem("root"), 1)
            if shift is not None:
                for i, w, k, tile, m, (t0, tn), p in order:
                    act.wait_ge(sem("out"), i + 1)
                    d = dst(tile, t0, tn)
                    nc.scalar.activation(d, d, ACT.Identity, bias=shift(tile, p)).then_inc(sem("shifted"), 1)
            if silu_src is not None:
                for i, w, k, tile, m, (t0, tn), p in order:
                    if i >= 2:
                        act.wait_ge(sem("gated"), i - 1)
                    nc.scalar.activation(act_g[:, i % 2, 0:tn], silu_src(tile, t0, tn), ACT.Silu).then_inc(sem("silu"), 1)

        @block.tensor
        def _(pe):
            for i, w, k, tile, m, (t0, tn), p in order:
                pe.wait_ge(sem("sq"), i + 1)
                if k == 0 and w >= 2:
                    pe.wait_ge(sem("root"), w - 1)
                nc.tensor.matmul(acc[w % 2][:, 0:tn], ones, sq[:, i % 2, 0:tn], start=(k == 0), stop=(k == m - 1))\
                    .then_inc(sem("sum"), 1)

        @block.vector
        def _(dve):
            for i, w, k, tile, m, (t0, tn), p in order:
                if k == 0:
                    dve.wait_ge(sem("root"), w + 1)
                    rr = r[:, w % 2, 0:tn]
                    nc.vector.reciprocal(rr, rr).then_inc(sem("inv"), 1)
                    dve.wait_ge(sem("inv"), w + 1)
                nc.vector.scalar_tensor_tensor(dst(tile, t0, tn), src(tile, t0, tn), gain(tile, p), r[:, w % 2, 0:tn],
                                               ALU.mult, ALU.mult).then_inc(sem("out"), 1)
            if silu_src is not None:
                for i, w, k, tile, m, (t0, tn), p in order:
                    dve.wait_ge(sem("silu"), i + 1)
                    dve.wait_ge(sem("out"), i + 1)
                    d = dst(tile, t0, tn)
                    nc.vector.tensor_tensor(d, d, act_g[:, i % 2, 0:tn], ALU.mult).then_inc(sem("gated"), 1)


def rwkv_finish(nc, p, y, col, w_gate, c, eps):
    H = ((0, 512), (512, 256))
    with ExitStack() as st:
        s = Stage(nc, st, "rf")
        sem = s.sem
        g2 = s.sb("g2", [128, 512])
        rk, sq, r, bo = (s.sb(n, [128, T]) for n in ("rk", "sq", "r", "bo"))
        pm, pq, pb, pg = (s.ps(n, [128, 1024]) for n in ("pm", "pq", "pb", "pg"))
        for n in ("g2", "sg", "mean", "cen", "sq", "var", "root", "inv", "ln", "rk", "bsum", "bo", "sum", "gate", "out"):
            sem(n)
        block = st.enter_context(nc.Block())

        @block.sync
        def _(sp):
            sp.dma_start(g2[:, :], w_gate).then_inc(sem("g2"), 16)

        @block.tensor
        def _(pe):
            def over(bank, lhs, rhs, name):
                for t0, tn in H:
                    ins = nc.tensor.matmul(bank[:, t0:t0 + tn], lhs, rhs[:, t0:t0 + tn], start=True, stop=True)
                ins.then_inc(sem(name), 1)
            pe.wait_ge(sem("g2"), 16)
            pe.wait_ge(sem("sg"), 1)
            for t in range(4):
                pe.wait_ge(sem("cen"), t)
                over(pm, c["head_ones"], y[:, t, :], "mean")
                pe.wait_ge(sem("rk"), t + 1)
                pe.wait_ge(sem("bo"), t)
                over(pb, c["head_ones"], rk, "bsum")
                pe.wait_ge(sem("out"), t)
                over(pg, g2[:, 128 * t:128 * t + 128], p[:, 25, :], "gate")
                pe.wait_ge(sem("sq"), t + 1)
                pe.wait_ge(sem("root"), t)
                over(pq, c["head_ones"], sq, "var")

        @block.scalar
        def _(act):
            A = nc.scalar.activation
            A(p[:, 25, :], p[:, 25, :], ACT.Sigmoid).then_inc(sem("sg"), 1)
            for t in range(4):
                act.wait_ge(sem("cen"), t + 1)
                A(sq[:, :], y[:, t, :], ACT.Square).then_inc(sem("sq"), 1)
                act.wait_ge(sem("var"), t + 1)
                act.wait_ge(sem("ln"), t)
                A(r[:, :], pq[:, 0:T], ACT.Sqrt, scale=1.0 / 64, bias=eps).then_inc(sem("root"), 1)

        @block.vector
        def _(dve):
            V = nc.vector
            for t in range(4):
                yt = y[:, t, :]
                dve.wait_ge(sem("bsum"), t)
                V.scalar_tensor_tensor(rk[:, :], p[:, 12 + t, :], col("r_k", t), p[:, 16 + t, :], ALU.mult, ALU.mult)\
                    .then_inc(sem("rk"), 1)
                dve.wait_ge(sem("mean"), t + 1)
                V.scalar_tensor_tensor(yt, pm[:, 0:T], -1.0 / 64, yt, ALU.mult, ALU.add).then_inc(sem("cen"), 1)
                dve.wait_ge(sem("bsum"), t + 1)
                dve.wait_ge(sem("sum"), t)
                V.tensor_tensor(bo[:, :], pb[:, 0:T], p[:, 20 + t, :], ALU.mult).then_inc(sem("bo"), 1)
                dve.wait_ge(sem("root"), t + 1)
                V.reciprocal(r[:, :], r[:, :]).then_inc(sem("inv"), 1)
                dve.wait_ge(sem("inv"), t + 1)
                dve.wait_ge(sem("cen"), t + 1)
                V.scalar_tensor_tensor(yt, yt, col("lnx_w", t), r[:, :], ALU.mult, ALU.mult).then_inc(sem("ln"), 1)
                dve.wait_ge(sem("ln"), t + 1)
                dve.wait_ge(sem("bo"), t + 1)
                V.scalar_tensor_tensor(yt, yt, col("lnx_b", t), bo[:, :], ALU.add, ALU.add).then_inc(sem("sum"), 1)
                dve.wait_ge(sem("sum"), t + 1)
                dve.wait_ge(sem("gate"), t + 1)
                V.tensor_tensor(yt, yt, pg[:, 0:T], ALU.mult).then_inc(sem("out"), 1)


def ssd_finish(nc, p, y, col):
    with ExitStack() as st:
        s = Stage(nc, st, "sf")
        sem = s.sem
        sz = s.sb("sz", [128, 4, LAT])
        sem("silu"), sem("skip")
        block = st.enter_context(nc.Block())

        @block.scalar
        def _(act):
            for t in range(4):
                nc.scalar.activation(sz[:, t, :], p[:, t, CTX:T], ACT.Silu).then_inc(sem("silu"), 1)

        @block.vector
        def _(dve):
            for t in range(4):
                yt = y[:, t, CTX:T]
                nc.vector.scalar_tensor_tensor(yt, p[:, 4 + t, CTX:T], col("d_skip", t), yt, ALU.mult, ALU.add)\
                    .then_inc(sem("skip"), 1)
                dve.wait_ge(sem("skip"), 2 * t + 1)
                dve.wait_ge(sem("silu"), t + 1)
                nc.vector.tensor_tensor(yt, yt, sz[:, t, :], ALU.mult).then_inc(sem("skip"), 1)


GROUPS = ((128, 1), (512, 4), (2048, 16))
SLOTS = 4


def dilated_attention(nc, name, p, out, w_slope, w_dist, c):
    NB = LAT // 128
    near = [2, NB, NB]
    with ExitStack() as st:
        s = Stage(nc, st, name)
        sem = s.sem
        slope, dist = s.sb("slope", [128, 12]), s.sb("dist", [128, sum(near), 128])
        vt = s.sb("vt", [128, NB, 768])
        qm = s.sb("qm", [128, 2, 3, 128])
        S = s.sb("S", [128, 2, sum(near) * 128])
        PT = s.sb("PT", [128, sum(near), 128])
        mx, rs, ri = (s.sb(n, [128, 2]) for n in ("mx", "rs", "ri"))
        o = s.sb("o", [128, 2, 2, 128])
        score = s.ps("score", [128, 3, 512])
        pt = s.ps("pt", [128, 12, 128])
        po, pf = s.ps("po", [128, 512]), s.ps("pf", [128, 4, 128])
        for n in ("c", "vtr", "vt", "q", "s", "bias", "mx", "exp", "tr", "pt", "o", "ri", "or", "fin", "out"):
            sem(n)
        s.seed()
        block = st.enter_context(nc.Block())
        widths = lambda i: [min(i + 1, m) for m in near]

        def units(engine, phases, after=None):
            for i in range(NB):
                with engine.Fori(0, 2) as pair:
                    for phase in phases:
                        for par in range(2):
                            phase(i, pair, par, pair * 2 + (4 * i + par))
                if after:
                    after(i)

        @block.sync
        def _(sp):
            sp.dma_start(slope[:, :], w_slope).then_inc(sem("c"), 16)
            sp.dma_start(dist[:], w_dist).then_inc(sem("c"), 16)

        @block.tensor
        def _(pe):
            mm = nc.tensor.matmul
            for k in range(NB):
                for t in range(6):
                    g = 6 * k + t
                    if g % 2 == 0 and g >= 4:
                        pe.wait_ge(sem("vt"), 1 + g // 2 - 1)
                    ins = nc.tensor.transpose(pt[:, 4 * (g // 2 % 2) + g % 2, :], p[:, 12 + t, 128 * k:128 * k + 128],
                                              c["ident"])
                    if g % 2:
                        ins.then_inc(sem("vtr"), 1)
            pe.wait_ge(sem("vt"), 1 + 3 * NB)

            def scores(i, pair, par, u):
                pe.wait_ge(sem("q"), 1 + 3 * (u + 1))
                pe.wait_ge(sem("bias"), 1 + 3 * u)
                for g, w in enumerate(widths(i)):
                    k0 = 128 * (i + 1 - w)
                    k = p[:, 6 + 2 * g:8 + 2 * g, k0:128 * (i + 1)][:, bass.ds(pair, 1), :]
                    ins = mm(score[:, g, 0:128 * w], qm[:, par, g, :], k, start=True, stop=True)
                ins.then_inc(sem("s"), 1)

            def turn(i, pair, par, u):
                pe.wait_ge(sem("exp"), 1 + u + 1)
                pe.wait_ge(sem("pt"), 1 + u)
                for k in range(sum(widths(i))):
                    ins = nc.tensor.transpose(pt[:, k, :], S[:, par, 128 * k:128 * k + 128], c["ident"])
                ins.then_inc(sem("tr"), 1)

            def apply(i, pair, par, u):
                n = sum(widths(i))
                pe.wait_ge(sem("pt"), 1 + u + 1)
                pe.wait_ge(sem("or"), 1 + u)
                k = 0
                for g, w in enumerate(widths(i)):
                    for j in range(i + 1 - w, i + 1):
                        v = vt[:, j, 256 * g:256 * g + 256].rearrange("p (a b) -> p a b", a=2)[:, bass.ds(pair, 1), 64 * par:64 * par + 64]
                        ins = mm(po[:, 0:64], PT[:, k, :], v, start=(k == 0), stop=(k == n - 1))
                        k += 1
                ins.then_inc(sem("o"), 1)

            def after(i):
                pe.wait_ge(sem("or"), 1 + 4 * (i + 1))
                pe.wait_ge(sem("out"), 1 + i)
                for t in range(2):
                    ins = nc.tensor.transpose(pf[:, t, :], o[:, i % 2, t, :], c["ident"])
                ins.then_inc(sem("fin"), 1)
            units(pe, (scores, turn, apply), after)

        @block.vector
        def _(dve):
            V = nc.vector
            dve.wait_ge(sem("c"), 1 + 32)

            def queries(i, pair, par, u):
                dve.wait_ge(sem("s"), 1 + u - par)
                for g in range(3):
                    q = p[:, 2 * g:2 * g + 2, 128 * i:128 * i + 128][:, bass.ds(pair, 1), :]
                    V.tensor_tensor(qm[:, par, g:g + 1, :], q,
                                    bcast(bcast(c["halves8"][:, par], 1, 1), 2, 128), ALU.mult).then_inc(sem("q"), 1)

            def bias(i, pair, par, u):
                ws = widths(i)
                n = sum(ws)
                dve.wait_ge(sem("s"), 1 + u + 1)
                dve.wait_ge(sem("tr"), 1 + (u - 1 if (i or par) else pair * 2))
                at = 0
                for g, w in enumerate(ws):
                    end = sum(near[:g + 1])
                    h = slope[:, 4 * g:4 * g + 4].rearrange("p (a b) -> p a b", b=2)[:, bass.ds(pair, 1), par]
                    V.scalar_tensor_tensor(S[:, par, 128 * at:128 * (at + w)],
                                           dist[:, end - w:end, :].rearrange("p a b -> p (a b)"), h,
                                           score[:, g, 0:128 * w], ALU.mult, ALU.add).then_inc(sem("bias"), 1)
                    at += w
                dve.wait_ge(sem("bias"), 1 + 3 * (u + 1))
                dve.wait_ge(sem("exp"), 1 + u - par)
                V.tensor_reduce(mx[:, par:par + 1], S[:, par, 0:128 * n], AX.X, ALU.max, negate=True).then_inc(sem("mx"), 1)

            def finish(i, pair, par, u):
                dve.wait_ge(sem("exp"), 1 + u + 1)
                V.reciprocal(ri[:, par:par + 1], rs[:, par:par + 1]).then_inc(sem("ri"), 1)
                dve.wait_ge(sem("ri"), 1 + u + 1)
                dve.wait_ge(sem("o"), 1 + u + 1)
                dve.wait_ge(sem("fin"), 1 + max(i - 1, 0))
                V.tensor_scalar(o[:, i % 2, bass.ds(pair, 1), 64 * par:64 * par + 64], po[:, 0:64], ri[:, par:par + 1],
                                None, ALU.mult).then_inc(sem("or"), 1)
            units(dve, (queries, bias, finish))

        @block.scalar
        def _(act):
            A = nc.scalar.activation
            for g in range(3 * NB):
                act.wait_ge(sem("vtr"), 1 + g + 1)
                k, t = divmod(2 * g, 6)
                A(vt[:, k, 128 * t:128 * t + 256], pt[:, 4 * (g % 2):4 * (g % 2) + 2, :].rearrange("p a b -> p (a b)"),
                  ACT.Copy).then_inc(sem("vt"), 1)

            def exps(i, pair, par, u):
                n = sum(widths(i))
                x = S[:, par, 0:128 * n]
                act.wait_ge(sem("mx"), 1 + u + 1)
                act.wait_ge(sem("ri"), 1 + u - par)
                A(x, x, ACT.Exp, bias=mx[:, par:par + 1], accum_out=rs[:, par:par + 1]).then_inc(sem("exp"), 1)

            def copy(i, pair, par, u):
                n = sum(widths(i))
                act.wait_ge(sem("tr"), 1 + u + 1)
                act.wait_ge(sem("o"), 1 + u)
                A(PT[:, 0:n, :], pt[:, 0:n, :], ACT.Copy).then_inc(sem("pt"), 1)

            def after(i):
                act.wait_ge(sem("fin"), 1 + i + 1)
                A(out[:, 0:2, 128 * i:128 * i + 128], pf[:, 0:2, :], ACT.Copy).then_inc(sem("out"), 1)
            units(act, (exps, copy), after)


def stick_breaking(nc, name, p, out, c):
    NB = LAT // 128
    with ExitStack() as st:
        s = Stage(nc, st, name)
        sem = s.sem
        vt = s.sb("vt", [128, NB, 256])
        z, e, l = s.sb("z", [128, 2, LAT]), s.sb("e", [128, 2, LAT]), s.sb("l", [128, 2, LAT])
        sp, at = s.sb("sp", [128, NB, LAT]), s.sb("at", [128, NB, LAT])
        pz = [s.ps(f"pz{i}", [128, LAT]) for i in range(2)]
        pr = [s.ps(f"pr{i}", [128, LAT]) for i in range(2)]
        po = [s.ps(f"po{i}", [128, LAT]) for i in range(2)]
        pt = s.ps("pt", [128, 4, 128])
        for n in ("vtr", "vt", "z", "zs", "abs", "exp", "ln", "sp0", "sp", "sum", "log", "min", "ex", "at", "o", "or"):
            sem(n)
        block = st.enter_context(nc.Block())
        units = [(4 * h + n, h, NB - 1 - n) for h in range(4) for n in range(NB)]
        rows = lambda h: slice(64 * (h % 2), 64 * (h % 2) + 64)

        @block.tensor
        def _(pe):
            mm = nc.tensor.matmul
            for k in range(NB):
                if k >= 2:
                    pe.wait_ge(sem("vt"), k - 1)
                for t in range(2):
                    ins = nc.tensor.transpose(pt[:, 2 * (k % 2) + t, :], p[:, 22 + t, 128 * k:128 * k + 128], c["ident"])
                ins.then_inc(sem("vtr"), 1)
                pe.wait_ge(sem("vt"), k + 1)

            def scores(u, h, j):
                if u >= 2:
                    pe.wait_ge(sem("zs"), u - 1)
                t0 = 128 * j
                mm(pz[u % 2][:, t0:LAT], p[rows(h), 20 + h // 2, t0:t0 + 128], p[rows(h), 18 + h // 2, t0:LAT],
                   start=True, stop=True).then_inc(sem("z"), 1)

            def sums(u, h, j):
                pe.wait_ge(sem("sp"), u + 1)
                if u >= 2:
                    pe.wait_ge(sem("log"), u - 1)
                t0 = 128 * j
                ins = mm(pr[u % 2][:, t0:LAT], c["from128"], sp[:, j, t0:LAT], start=True, stop=(j == NB - 1))
                for j2 in range(j + 1, NB):
                    ins = mm(pr[u % 2][:, 128 * j2:LAT], c["ones"], sp[:, j2, 128 * j2:LAT], start=False,
                             stop=(j2 == NB - 1))
                ins.then_inc(sem("sum"), 1)

            def apply(h):
                pe.wait_ge(sem("at"), 4 * h + 4)
                if h >= 2:
                    pe.wait_ge(sem("or"), h - 1)
                for j in range(NB):
                    ins = mm(po[h % 2][rows(h), 128 * j:LAT], vt[:, j, 64 * h:64 * h + 64], at[:, j, 128 * j:LAT],
                             start=(j == 0), stop=(j == NB - 1))
                ins.then_inc(sem("o"), 1)
            scores(*units[0])
            for n, (u, h, j) in enumerate(units):
                if n + 1 < len(units):
                    scores(*units[n + 1])
                sums(u, h, j)
                if j == 0:
                    apply(h)

        @block.scalar
        def _(act):
            A = nc.scalar.activation
            for k in range(NB):
                act.wait_ge(sem("vtr"), k + 1)
                A(vt[:, k, :], pt[:, 2 * (k % 2):2 * (k % 2) + 2, :].rearrange("p a b -> p (a b)"), ACT.Copy)\
                    .then_inc(sem("vt"), 1)

            def first(u, h, j):
                b, t = u % 2, slice(128 * j, LAT)
                act.wait_ge(sem("z"), u + 1)
                if u >= 2:
                    act.wait_ge(sem("log"), u - 1)
                    act.wait_ge(sem("sp0"), u - 1)
                A(z[:, b, t], pz[b][:, t], ACT.Copy, scale=0.125).then_inc(sem("zs"), 1)
                act.wait_ge(sem("zs"), u + 1)
                A(e[:, b, t], z[:, b, t], ACT.Abs).then_inc(sem("abs"), 1)
                act.wait_ge(sem("abs"), u + 1)
                A(e[:, b, t], e[:, b, t], ACT.Exp, scale=-1.0).then_inc(sem("exp"), 1)
                act.wait_ge(sem("exp"), u + 1)
                A(l[:, b, t], e[:, b, t], ACT.Ln, bias=1.0).then_inc(sem("ln"), 1)

            def second(u, h, j):
                t = slice(128 * j, LAT)
                act.wait_ge(sem("min"), u + 1)
                A(at[:, j, t], at[:, j, t], ACT.Exp).then_inc(sem("ex"), 1)
                if j == 0:
                    act.wait_ge(sem("o"), h + 1)
                    A(out[rows(h), 2 + h // 2, :], po[h % 2][rows(h), :], ACT.Copy).then_inc(sem("or"), 1)
            first(*units[0])
            for n, x in enumerate(units):
                if n + 1 < len(units):
                    first(*units[n + 1])
                second(*x)

        @block.vector
        def _(dve):
            V = nc.vector

            def first(u, h, j):
                b, t = u % 2, slice(128 * j, LAT)
                dve.wait_ge(sem("ln"), u + 1)
                if u >= 1:
                    dve.wait_ge(sem("sum"), u if j < NB - 1 else 4 * h)
                V.scalar_tensor_tensor(sp[:, j, t], z[:, b, t], 0.0, l[:, b, t], ALU.max, ALU.add).then_inc(sem("sp0"), 1)
                dve.wait_ge(sem("sp0"), u + 1)
                own = sp[:, j, 128 * j:128 * j + 128]
                V.tensor_tensor(own, own, c["before128"], ALU.mult).then_inc(sem("sp"), 1)

            def second(u, h, j):
                b, t = u % 2, slice(128 * j, LAT)
                dve.wait_ge(sem("sum"), u + 1)
                if h >= 1:
                    dve.wait_ge(sem("o"), h)
                V.tensor_tensor(at[:, j, t], z[:, b, t], pr[b][:, t], ALU.subtract).then_inc(sem("log"), 1)
                dve.wait_ge(sem("log"), u + 1)
                V.tensor_scalar_min(at[:, j, t], at[:, j, t], 0.0).then_inc(sem("min"), 1)
                dve.wait_ge(sem("ex"), u + 1)
                own = at[:, j, 128 * j:128 * j + 128]
                V.tensor_tensor(own, own, c["before128"], ALU.mult).then_inc(sem("at"), 1)
            for x in units:
                first(*x)
                second(*x)


def copy_in(nc, name, pairs):
    with ExitStack() as st:
        s = Stage(nc, st, name)
        sem = s.sem
        sem("in")
        block = st.enter_context(nc.Block())

        @block.sync
        def _(sp):
            for dst, src in pairs:
                sp.dma_start(dst, src).then_inc(sem("in"), 16)
            sp.wait_ge(sem("in"), 16 * len(pairs))


def ada_gain(nc, name, gain, scale, gm):
    with ExitStack() as st:
        s = Stage(nc, st, name)
        done = s.sem("done")
        block = st.enter_context(nc.Block())

        @block.vector
        def _(dve):
            nc.vector.scalar_tensor_tensor(gm[:], scale, 1.0, bcast(gain, 2, 2), ALU.add, ALU.mult).then_inc(done, 1)
            dve.wait_ge(done, 1)


def program(nc, a, out, at):
    x_dram = nc.dram_tensor("x_between", [128, DT, T], F32, kind="Internal").ap()
    with ExitStack() as top:
        g = Stage(nc, top, "top")
        cols = g.sb("cols", list(a["cols"].shape))
        base = g.sb("base", [128, 2, 128])
        halves = g.sb("halves", [128, 2, 2])
        every_mod = g.sb("mods", [128, 12 * DT, 2])
        mods = every_mod[:, 0:6 * DT, :]
        sil = g.sb("sil", [128, DT, 2])
        gm = g.sb("gm", [128, DT, 2])
        h = g.sb("h", [128, DT, T])
        copy_in(nc, "in", [(cols[:], a["cols"]), (base[:], a["base"]), (halves[:], a["halves"])])
        consts = {"ident": base[:, 0, :], "ones": base[:, 1, :], "halves": halves[:, 0, :], "halves8": halves[:, 1, :]}
        col = lambda n, m=0: cols[:, at[n] + m:at[n] + m + 1]
        span = lambda n, m: cols[:, at[n]:at[n] + m]
        dyn = lambda n, lo, m: cols[:, at[n] + lo:at[n] + lo + DT * 3][:, bass.ds(m, 1)]

        def masks(st, name, names, extra=()):
            m = st.enter_context(nc.sbuf_tensor("m_" + name, [128, len(names), 128], F32))
            copy_in(nc, name + "_in", [(m[:], a[name])] + list(extra))
            return {n: m[:, i, :] for i, n in enumerate(names)}, m

        def ada(name, x, dst, norm, first, parts=EVERY):
            ada_gain(nc, name + "_g", span(norm, DT), mods[:, first + DT:first + 2 * DT, :], gm)
            which = 2 - len(parts)
            view = lambda y: (lambda t, t0, tn: y[:, t, t0:t0 + tn])
            rms(nc, name, view(x), view(dst), [list(range(DT))], parts, consts["ones"], D, col("eps6"),
                lambda t, p: gm[:, t, p + which:p + which + 1],
                shift=lambda t, p: mods[:, first + t, p + which:p + which + 1])

        def mlp(layer, x, h, parts, pieces):
            m = 4 * DT // pieces
            for q in range(pieces):
                with nc.sbuf_tensor(f"hidden{layer}_{q}", [128, m, sum(tn for _, tn in parts)], F32) as hid:
                    n = f"up{layer}_{q}"
                    product(nc, n, a[f"mlp_w1_{layer}"], h, DT, m, parts, RELU2, hid, tile0=m * q,
                            side=rider(n) if n in riders else None)
                    product(nc, f"down{layer}_{q}", a[f"mlp_w2_{layer}"], hid, m, DT, parts, ADD, x, k0=m * q,
                            gate=mods[:, 5 * DT:6 * DT, :])

        with ExitStack() as st:
            s = Stage(nc, st, "silu")
            done = s.sem("done")
            with nc.Block() as block:
                @block.scalar
                def _(act):
                    nc.scalar.activation(sil[:], cols[:, at["c"]:at["c"] + 2 * DT].rearrange("p (b a) -> p a b", b=2),
                                         ACT.Silu).then_inc(done, 1)
                    act.wait_ge(done, 1)
        FIRST = 20
        riders = {"in0": 2, "out0": 2, "up0_0": 1}
        starts = dict(zip(riders, (FIRST, FIRST + 2 * 26, FIRST + 2 * 26 + 2 * DT)))
        assert starts["up0_0"] + DT == 12 * DT
        rider = lambda n: Side(a["mod_w"], sil, every_mod, span("mod_b", 12 * DT), starts[n], riders[n])
        small_product(nc, "mod", a["mod_w"], sil, FIRST, every_mod, span("mod_b", 12 * DT))
        with nc.sbuf_tensor("x_0a", [128, DT, T], F32) as x:
            copy_in(nc, "x0", [(x[:], a["x"])])
            ada("n10", x, h, "norm1_0", 0)
        with ExitStack() as st:
            p = st.enter_context(nc.sbuf_tensor("p0", [128, 26, T], F32))
            product(nc, "in0", a["w_in0"], h, DT, 26, EVERY, COPY, p, side=rider("in0"))
            m, raw = masks(st, "masks0", MASKS0)
            c = {**consts, **m, "levels": raw[:, MASKS0.index("level0"):MASKS0.index("level0") + 6, :]}
            rope(nc, p, a["rope"], c)
            diff_attention(nc, p, h, a["lam"], c)
            tiles = lambda lo: (lambda t, t0, tn: h[:, lo + t, t0:t0 + tn])
            rms(nc, "sub", tiles(0), tiles(0), [[t] for t in range(4)], ((0, 512), (512, 256)), consts["ones"],
                128 * (1 - LAM_INIT) ** 2, col("eps5"), lambda t, p_: col("subln"))
            sig, kk = p[:, 0:8, :], p[:, 8:12, :]
            with ExitStack() as st2:
                b = st2.enter_context(nc.sbuf_tensor("b", [128, 4, T], F32))
                with nc.sbuf_tensor("cmask", [128, T], F32) as cm:
                    chunk_mask(nc, "cm0", cm, RC)
                    c["chunk_mask"] = cm[:, :]
                    rwkv_prepare(nc, p, sig, kk, b, col, a["lora"], c)
                rwkv_scan(nc, p, sig, kk, b, h[:, 4:8, :], c)
            rwkv_finish(nc, p, h[:, 4:8, :], col, a["g2"], c, col("epsg"))
        with nc.sbuf_tensor("x_0b", [128, DT, T], F32) as x:
            copy_in(nc, "x1", [(x[:], a["x"])])
            product(nc, "out0", a["w_out0"], h, DT, DT, EVERY, ADD, x, gate=mods[:, 2 * DT:3 * DT, :],
                    side=rider("out0"))
            ada("n20", x, h, "norm2_0", 3 * DT)
            mlp(0, x, h, EVERY, 4)
            mods = every_mod[:, 6 * DT:12 * DT, :]
            ada("n11", x, h, "norm1_1", 0)
            copy_in(nc, "x2", [(x_dram, x[:])])
        with ExitStack() as st:
            m, raw = masks(st, "masks1", MASKS1)
            k0 = MASKS1.index("pair0")
            c = {**consts, **m, "pair_level": raw[:, k0:k0 + 8, :]}
            p = st.enter_context(nc.sbuf_tensor("p1", [128, 25, T], F32))
            sp = st.enter_context(nc.sbuf_tensor("sp", [128, 4, T], F32))
            product(nc, "in1", a["w_in1"], h, DT, 25, EVERY, COPY, p)
            with nc.sbuf_tensor("dtla", [16, 2, T], F32) as dtla:
                ssd_prepare(nc, p, dtla, col, c)
                ssd_scan(nc, p, dtla, h[:, 0:4, :], c)
            ssd_finish(nc, p, h[:, 0:4, :], col)
            with nc.sbuf_tensor("cmask1", [128, T], F32) as cm:
                chunk_mask(nc, "cm1", cm, CHUNK)
                c["chunk_mask128"] = cm[:, :]
                gla_prepare(nc, p, sp, col, a["gk_up"], c)
            gla_scan(nc, p, sp, h[:, 4:8, :], c)
            ht = lambda t, t0, tn: h[:, t, t0:t0 + tn]
            rms(nc, "ssdn", ht, ht, [[0, 1], [2, 3]], LATENTS, consts["ones"], 256, col("eps6"),
                lambda t, p_: col("ssm_norm", t))
            rms(nc, "glan", ht, ht, [[4], [5], [6], [7]], LATENTS, consts["ones"], 128, col("eps6"),
                lambda t, p_: col("gla_norm"), silu_src=lambda t, t0, tn: p[:, 16 + t, t0:t0 + tn])
        with nc.sbuf_tensor("xl", [128, DT, LAT], F32) as x:
            copy_in(nc, "x3", [(x[:], x_dram[:, :, CTX:T])])
            ONE = ((0, LAT),)
            hl = h[:, :, CTX:T]
            product(nc, "out1", a["w_out1"], hl, DT, DT, ONE, ADD, x, gate=mods[:, 2 * DT:3 * DT, :])
            ada("n21", x, hl, "norm2_1", 3 * DT, ONE)
            mlp(1, x, hl, ONE, 2)
            view = lambda y: (lambda t, t0, tn: y[:, t, t0:t0 + tn])
            all_tiles = [list(range(DT))]
            rms(nc, "fin1", view(x), view(x), all_tiles, ONE, consts["ones"], D, col("eps6"),
                lambda t, p_: col("final_norm", t))

            for l in range(2):
                hs = h[:, :, 0:LAT]
                rms(nc, f"b1{l}", view(x), view(hs), all_tiles, ONE, consts["ones"], D, col("eps6"),
                    lambda t, p_: col(f"b_norm1_{l}", t))
                with ExitStack() as st:
                    m, _ = masks(st, "masks2", MASKS2) if l == 0 else masks_again(nc, st, a)
                    c = {**consts, **m}
                    gates = st.enter_context(nc.sbuf_tensor(f"gates{l}", [128, 2 * DT, LAT], F32))
                    o = st.enter_context(nc.sbuf_tensor(f"o{l}", [128, 4, LAT], F32))
                    product(nc, f"bg{l}", a[f"b_w_in{l}"][24:40], hs, DT, 16, ONE, GATE, gates,
                            bias=span(f"b_gate_{l}", 16))
                    with nc.sbuf_tensor(f"pb{l}", [128, 24, LAT], F32) as p:
                        product(nc, f"bi{l}", a[f"b_w_in{l}"][0:24], hs, DT, 24, ONE, COPY, p)
                        dilated_attention(nc, f"di{l}", p, o, a["slope"], a["dist"], c)
                        stick_breaking(nc, f"sb{l}", p, o, c)
                    product(nc, f"bm{l}", a[f"b_w_br{l}"], o, 4, DT, ((0, LAT), (0, LAT)), MERGE, hs, unit=4,
                            gate=gates)
                product(nc, f"bo{l}", a[f"b_w_o{l}"], hs, DT, DT, ONE, ADD, x)
                rms(nc, f"b2{l}", view(x), view(hs), all_tiles, ONE, consts["ones"], D, col("eps6"),
                    lambda t, p_: col(f"b_norm2_{l}", t))
                FT = 22
                with nc.sbuf_tensor(f"glu{l}", [128, FT, LAT], F32) as hid:
                    product(nc, f"bu{l}", a[f"b_w_up{l}"], hs, DT, 2 * FT, ONE, GLU, hid,
                            bias=span(f"b_conv_b{l}", FT),
                            taps=lambda k, m: cols[:, at[f"b_conv_w{l}"] + FT * k:at[f"b_conv_w{l}"] + FT * (k + 1)]
                            [:, bass.ds(m, 1)])
                    for k0 in (0, FT // 2):
                        product(nc, f"bd{l}_{k0}", a[f"b_w_down{l}"], hid[:, k0:k0 + FT // 2, :], FT // 2, DT, ONE,
                                ADD, x, unit=FT // 2, k0=k0)
            rms(nc, "fin2", view(x), view(x), all_tiles, ONE, consts["ones"], D, col("eps6"),
                lambda t, p_: col("b_norm_f", t))
            copy_in(nc, "store", [(out, x[:])])


def masks_again(nc, st, a):
    m = st.enter_context(nc.sbuf_tensor("masks2b", [128, len(MASKS2), 128], F32))
    copy_in(nc, "masks2b_in", [(m[:], a["masks2"])])
    return {n: m[:, i, :] for i, n in enumerate(MASKS2)}, m


def chunk_mask(nc, name, m, chunk):
    with ExitStack() as st:
        s = Stage(nc, st, name)
        done = s.sem("done")
        block = st.enter_context(nc.Block())

        @block.vector
        def _(dve):
            nc.vector.memset(m[:, :], 1.0).then_inc(done, 1)
            dve.wait_ge(done, 1)
            nc.vector.memset(m[:, 0:T:chunk], 0.0).then_inc(done, 1)
            dve.wait_ge(done, 2)


MASKS0 = ["head_ones", "lower", "upper", "upper_inc"] + [f"level{l}" for l in range(6)] + ["fold0", "fold1", "fold2", "rot"]
MASKS1 = ["upper_inc128", "lower128"] + [f"pair{l}" for l in range(8)]
MASKS2 = ["from128", "before128"]



def constants():
    m = {**square_masks(), **chunk_masks()}
    j, i = np.arange(128)[:, None], np.arange(128)[None, :]
    m["from128"], m["before128"] = j >= i, j < i
    lo = i % 32 < 16
    m["rot"] = np.where(lo & (j == i + 16), -1.0, 0.0) + np.where(~lo & (j == i - 16), 1.0, 0.0)
    pack = lambda names: np.stack([np.asarray(m[n], np.float32) for n in names], axis=1)
    out = {"base": pack(["ident", "ones"]), "masks0": pack(MASKS0), "masks1": pack(MASKS1), "masks2": pack(MASKS2)}
    half = (np.arange(128)[:, None] // 64 == np.arange(2)).astype(np.float32)
    out["halves"] = np.stack([half, half * np.float32(0.125)], axis=1)
    ch, t = np.arange(128), np.arange(LAT)
    inv = (np.float32(10000.0) ** (-np.arange(16, dtype=np.float32) / np.float32(16))).astype(np.float32)
    pos = np.where((ch % 64 // 32 == 0)[:, None], (t // 64)[None, :], (t % 64)[None, :]).astype(np.float32)
    ang = pos * inv[ch % 16][:, None]
    out["rope"] = np.stack([np.cos(ang), np.sin(ang)], axis=1).astype(np.float32)
    dist = []
    for (window, dilation), near in zip(GROUPS, (2, 4, 4)):
        for o in range(near - 1, -1, -1):
            d = o * 128 + j - i
            ok = (d >= 0) & (d <= window) & (d % dilation == 0)
            dist.append(np.where(ok, d, 1e30))
    out["dist"] = np.stack(dist, axis=1).astype(np.float32)
    slopes = (2.0 ** (-8.0 * np.arange(1, 13) / 12)).astype(np.float32)
    out["slope"] = np.broadcast_to(-slopes, (128, 12)).copy()
    return out


def layouts(v):
    f = np.float32
    tile_w = lambda w: np.ascontiguousarray(
        w.reshape(w.shape[0] // 128, 128, w.shape[1] // 128, 128).transpose(2, 1, 0, 3)).reshape(
            w.shape[1] // 128, 128, w.shape[0])
    chan = lambda x: np.ascontiguousarray(x.T.reshape(DT, 128, -1).transpose(1, 0, 2))
    d = constants()
    d["x"] = chan(np.concatenate([v["ctx"][0], v["x"][0]], axis=0))
    for l in range(2):
        d[f"w_out{l}"] = tile_w(v[f"l{l}_w_out"])
        d[f"mlp_w1_{l}"] = tile_w(v[f"l{l}_mlp_w1"])
        d[f"mlp_w2_{l}"] = tile_w(v[f"l{l}_mlp_w2"])
        d[f"b_w_in{l}"] = tile_w(v["w_in_2"][l])
        d[f"b_w_br{l}"] = tile_w(v["w_br_2"][l])
        d[f"b_w_o{l}"] = tile_w(v["w_o_2"][l])
        up = v["w_up_2"][l]
        d[f"b_w_up{l}"] = tile_w(up.reshape(D, 2, -1, 128).transpose(0, 2, 1, 3).reshape(D, -1))
        d[f"b_w_down{l}"] = tile_w(v["w_down_2"][l])
    d["mod_w"] = np.concatenate([tile_w(v[f"l{l}_mod_w"]) for l in range(2)], axis=0)
    d["w_in0"] = tile_w(v["l0_w_in"])
    w = v["l1_w_in"]
    last = np.zeros((D, 128), f)
    last[:, 0:16] = w[:, 1536:1552]
    last[:, 32:48] = w[:, 3088:3104]
    d["w_in1"] = tile_w(np.concatenate([w[:, 0:1536], w[:, 1552:3088], last], axis=1))
    d["lam"] = np.stack([v["l0_lam_q1"], v["l0_lam_q2"], v["l0_lam_k1"], v["l0_lam_k2"]], axis=1)
    lora = np.zeros((2, 128, 512), f)
    lora[0, 0:64], lora[0, 64:128], lora[1, 0:64] = v["l0_w2_f"], v["l0_a2"], v["l0_w2_b"]
    d["lora"], d["g2"] = lora, v["l0_g2"]
    d["gk_up"] = np.concatenate([v["l1_gk_up_f"], v["l1_gk_up_b"]], axis=1)
    one = lambda *x: np.concatenate(x + (np.zeros(128 - sum(y.size for y in x), f),))
    cols = {"c": np.concatenate([v["c_ctx"], v["c"][0]]), "final_norm": v["final_norm"], "b_norm_f": v["norm_f_2"],
            "subln": v["l0_subln"], "ssm_norm": v["l1_ssm_norm"], "gla_norm": v["l1_gla_norm"],
            "conv_w": v["l1_conv_w"].reshape(-1), "conv_b": v["l1_conv_b"],
            "dt_bias": one(v["l1_dt_bias_f"], v["l1_dt_bias_b"]), "a_log": one(v["l1_a_log_f"], v["l1_a_log_b"]),
            "gk_b": np.concatenate([v["l1_gk_b_f"], v["l1_gk_b_b"]]), "d_skip": np.repeat(v["l1_d_skip"], 64),
            "eps6": np.full(128, 1e-6, f), "eps5": np.full(128, 1e-5 / (1 - LAM_INIT) ** 2, f), "epsg": np.full(128, 64e-5, f)}
    for n in ("mu", "k_k", "k_a", "r_k", "w0_f", "w0_b", "a0", "lnx_w", "lnx_b"):
        cols[n] = v["l0_" + n]
    for l in range(2):
        for n in (1, 2):
            cols[f"norm{n}_{l}"] = v[f"l{l}_norm{n}"]
            cols[f"b_norm{n}_{l}"] = v[f"norm{n}_2"][l]
        cols[f"b_gate_{l}"] = v["b_gate_2"][l]
        cols[f"b_conv_w{l}"] = v["conv_w_2"][l].reshape(-1)
        cols[f"b_conv_b{l}"] = v["conv_b_2"][l]
    cols["mod_b"] = np.concatenate([v["l0_mod_b"], v["l1_mod_b"]])
    at, n = {}, 0
    for name, x in cols.items():
        at[name] = n
        n += x.size // 128
    d["cols"] = np.concatenate([x.reshape(-1, 128).T for x in cols.values()], axis=1)
    return {n: np.ascontiguousarray(x) for n, x in d.items()}, at


def kernel(**inputs):
    import concourse.bacc as bacc
    from concourse.bass_utils import run_bass_kernel_spmd

    arrays, at = layouts({n: np.asarray(x) for n, x in inputs.items()})
    nc = bacc.Bacc("TRN2", target_bir_lowering=False, num_devices=1)
    a = {n: nc.dram_tensor("in_" + n, x.shape, mybir.dt.from_np(x.dtype), kind="ExternalInput").ap()
         for n, x in arrays.items()}
    out = nc.dram_tensor("out", (128, DT, LAT), F32, kind="ExternalOutput").ap()
    program(nc, a, out, at)
    r = run_bass_kernel_spmd(nc, [{"in_" + n: x for n, x in arrays.items()}], core_ids=[0])
    got = r.results[0]["out"]
    return np.ascontiguousarray(got.transpose(2, 1, 0).reshape(1, LAT, D))
```
